# Optimizing a Trainium2 kernel written in Bass

```python
import jax
import jax.numpy as jnp
from jax import lax
import numpy as np

D_MODEL = 1024
BATCH = 1
SEQ = 256
DEPTH = 2

CHUNK = 64
Q_BLOCK = 128
N_A_LAYERS = DEPTH // 2
N_B_LAYERS = DEPTH - N_A_LAYERS
CONV_WIDTH = 31
N_HEADS = 8
QK_NOPE_DIM = 128
QK_ROPE_DIM = 64
QK_DIM = QK_NOPE_DIM + QK_ROPE_DIM
V_HEAD_DIM = 128
KV_LORA_RANK = D_MODEL // 4
Q_LORA_RANK = 3 * KV_LORA_RANK // 2
ROPE_THETA = 10000.0
SOFTMAX_SCALE = QK_DIM ** -0.5
N_GROUPS = 4
EXPERTS_PER_GROUP = 8
N_EXPERTS = N_GROUPS * EXPERTS_PER_GROUP
TOP_K_IN_GROUP = 2
D_EXPERT = D_MODEL // 2
EPS = 1e-6
MASK_VALUE = -1e30

kernel_name = "conv_mla_yoco_hier_moe_block"

def rms_norm(x, g):
    xf = x.astype(jnp.float32)
    y = xf * lax.rsqrt(jnp.mean(xf * xf, axis=-1, keepdims=True) + EPS)
    return (y * g.astype(jnp.float32)).astype(x.dtype)

def layer_norm(x, g, b):
    xf = x.astype(jnp.float32)
    mu = jnp.mean(xf, axis=-1, keepdims=True)
    var = jnp.mean(jnp.square(xf - mu), axis=-1, keepdims=True)
    y = (xf - mu) * lax.rsqrt(var + EPS)
    return (y * g.astype(jnp.float32) + b.astype(jnp.float32)).astype(x.dtype)

def rope_tables(positions):
    inv_freq = ROPE_THETA ** (-jnp.arange(0, QK_ROPE_DIM, 2, dtype=jnp.float32) / QK_ROPE_DIM)
    ang = positions.astype(jnp.float32)[..., None] * inv_freq
    return jnp.cos(ang)[:, :, None, :], jnp.sin(ang)[:, :, None, :]

def rope_tail(x, cos, sin):
    x_nope = x[..., :QK_NOPE_DIM]
    xr = x[..., QK_NOPE_DIM:].astype(jnp.float32)
    x1, x2 = jnp.split(xr, 2, axis=-1)
    rot = jnp.concatenate([x1 * cos - x2 * sin, x1 * sin + x2 * cos], axis=-1)
    return jnp.concatenate([x_nope, rot.astype(x.dtype)], axis=-1)

def conformer_conv_module(h, norm_g, pw1_w, pw1_b, dw_w, dw_b, ln_g, ln_b, pw2_w, pw2_b):
    hn = rms_norm(h, norm_g)
    a, gate = jnp.split(hn @ pw1_w + pw1_b, 2, axis=-1)
    u = a * jax.nn.sigmoid(gate)
    u = lax.conv_general_dilated(
        u, dw_w[:, None, :].astype(u.dtype), window_strides=(1,),
        padding=[(CONV_WIDTH - 1, 0)],
        dimension_numbers=('NWC', 'WIO', 'NWC'),
        feature_group_count=D_MODEL) + dw_b
    u = jax.nn.silu(layer_norm(u, ln_g, ln_b))
    return u @ pw2_w + pw2_b

def shared_mla_kv(h, kv_norm_g, w_dkv, kv_latent_g, w_kr, w_ukv, k_norm_g, cos, sin):
    B, S, _ = h.shape
    hn = rms_norm(h, kv_norm_g)
    c_kv = rms_norm(hn @ w_dkv, kv_latent_g)
    kv = (c_kv @ w_ukv).reshape(B, S, N_HEADS, QK_NOPE_DIM + V_HEAD_DIM)
    k_nope, v = kv[..., :QK_NOPE_DIM], kv[..., QK_NOPE_DIM:]
    k_rope = hn @ w_kr
    k = jnp.concatenate(
        [k_nope, jnp.broadcast_to(k_rope[:, :, None, :], (B, S, N_HEADS, QK_ROPE_DIM))], axis=-1)
    k = rope_tail(rms_norm(k, k_norm_g), cos, sin)
    return k, v

def chunk_causal_attention(q, k, v):
    B, S, H, Dqk = q.shape
    n_blk = S // Q_BLOCK
    qb = q.reshape(B, n_blk, Q_BLOCK, H, Dqk).transpose(1, 0, 3, 2, 4)
    key_chunk = jnp.arange(S) // CHUNK

    def one_block(args):
        q_blk, blk = args
        q_chunk = (blk * Q_BLOCK + jnp.arange(Q_BLOCK)) // CHUNK
        allowed = key_chunk[None, :] <= q_chunk[:, None]
        s = jnp.einsum('bhqd,bkhd->bhqk', q_blk, k).astype(jnp.float32) * SOFTMAX_SCALE
        s = jnp.where(allowed, s, MASK_VALUE)
        p = jax.nn.softmax(s, axis=-1).astype(v.dtype)
        return jnp.einsum('bhqk,bkhd->bqhd', p, v)

    out = lax.map(one_block, (qb, jnp.arange(n_blk)))
    return out.transpose(1, 0, 2, 3, 4).reshape(B, S, H, v.shape[-1])

def mla_attention_layer(h, k, v, norm_g, w_dq, q_latent_g, w_uq, q_norm_g, w_o, cos, sin):
    B, S, _ = h.shape
    hn = rms_norm(h, norm_g)
    c_q = rms_norm(hn @ w_dq, q_latent_g)
    q = (c_q @ w_uq).reshape(B, S, N_HEADS, QK_DIM)
    q = rope_tail(rms_norm(q, q_norm_g), cos, sin)
    o = chunk_causal_attention(q, k, v)
    return o.reshape(B, S, N_HEADS * V_HEAD_DIM) @ w_o

def hierarchical_moe(h, norm_g, w_group, b_group, w_router, b_router, w_gate_up, w_down):
    B, S, D = h.shape
    xt = rms_norm(h, norm_g).reshape(B * S, D)
    g_prob = jax.nn.softmax((xt @ w_group + b_group).astype(jnp.float32), axis=-1)
    g_idx = jnp.argmax(g_prob, axis=-1)
    g_w = jnp.take_along_axis(g_prob, g_idx[:, None], axis=-1)
    e_logits = (xt @ w_router + b_router).astype(jnp.float32).reshape(-1, N_GROUPS, EXPERTS_PER_GROUP)
    e_logits = jnp.take_along_axis(e_logits, g_idx[:, None, None], axis=1)[:, 0]
    e_prob = jax.nn.softmax(e_logits, axis=-1)
    top_p, top_i = lax.top_k(e_prob, TOP_K_IN_GROUP)
    top_p = top_p / jnp.sum(top_p, axis=-1, keepdims=True)
    expert_id = g_idx[:, None] * EXPERTS_PER_GROUP + top_i
    gates = jnp.sum(jax.nn.one_hot(expert_id, N_EXPERTS, dtype=jnp.float32)
                    * (g_w * top_p)[..., None], axis=1).astype(xt.dtype)

    def expert_step(acc, ex):
        w_gu, w_d, g = ex
        a, b = jnp.split(xt @ w_gu, 2, axis=-1)
        return acc + ((jax.nn.silu(a) * b) @ w_d) * g[:, None], None

    y, _ = lax.scan(expert_step, jnp.zeros_like(xt), (w_gate_up, w_down, gates.T))
    return y.reshape(B, S, D)

def setup_inputs(seed: int = 0) -> dict:
    key = jax.random.key(seed)
    ks = iter(jax.random.split(key, 40))

    def nrm(shape, scale):
        return jax.random.normal(next(ks), shape, jnp.float32) * scale

    def gain(shape):
        return 1.0 + nrm(shape, 0.05)

    D, NA, NB, L = D_MODEL, N_A_LAYERS, N_B_LAYERS, DEPTH
    x = nrm((BATCH, SEQ, D), 1.0)
    offsets = jax.random.randint(next(ks), (BATCH, 1), 0, 64) * CHUNK
    positions = (jnp.arange(SEQ, dtype=jnp.int32)[None, :] + offsets).astype(jnp.int32)
    return {
        "x": x,
        "positions": positions,
        "a_norm_g": gain((NA, D)),
        "a_pw1_w": nrm((NA, D, 2 * D), D ** -0.5),
        "a_pw1_b": nrm((NA, 2 * D), 0.01),
        "a_dw_w": nrm((NA, CONV_WIDTH, D), CONV_WIDTH ** -0.5),
        "a_dw_b": nrm((NA, D), 0.01),
        "a_ln_g": gain((NA, D)),
        "a_ln_b": nrm((NA, D), 0.01),
        "a_pw2_w": nrm((NA, D, D), D ** -0.5),
        "a_pw2_b": nrm((NA, D), 0.01),
        "kv_norm_g": gain((D,)),
        "w_dkv": nrm((D, KV_LORA_RANK), D ** -0.5),
        "kv_latent_g": gain((KV_LORA_RANK,)),
        "w_kr": nrm((D, QK_ROPE_DIM), D ** -0.5),
        "w_ukv": nrm((KV_LORA_RANK, N_HEADS * (QK_NOPE_DIM + V_HEAD_DIM)), KV_LORA_RANK ** -0.5),
        "k_norm_g": gain((QK_DIM,)),
        "b_norm_g": gain((NB, D)),
        "w_dq": nrm((NB, D, Q_LORA_RANK), D ** -0.5),
        "q_latent_g": gain((NB, Q_LORA_RANK)),
        "w_uq": nrm((NB, Q_LORA_RANK, N_HEADS * QK_DIM), Q_LORA_RANK ** -0.5),
        "q_norm_g": gain((NB, QK_DIM)),
        "w_o": nrm((NB, N_HEADS * V_HEAD_DIM, D), (N_HEADS * V_HEAD_DIM) ** -0.5),
        "ffn_norm_g": gain((L, D)),
        "w_group": nrm((L, D, N_GROUPS), D ** -0.5),
        "b_group": nrm((L, N_GROUPS), 0.01),
        "w_router": nrm((L, D, N_EXPERTS), D ** -0.5),
        "b_router": nrm((L, N_EXPERTS), 0.01),
        "w_gate_up": nrm((L, N_EXPERTS, D, 2 * D_EXPERT), D ** -0.5),
        "w_down": nrm((L, N_EXPERTS, D_EXPERT, D), D_EXPERT ** -0.5),
    }

def reference(x, positions, a_norm_g, a_pw1_w, a_pw1_b, a_dw_w, a_dw_b, a_ln_g, a_ln_b, a_pw2_w, a_pw2_b,
              kv_norm_g, w_dkv, kv_latent_g, w_kr, w_ukv, k_norm_g,
              b_norm_g, w_dq, q_latent_g, w_uq, q_norm_g, w_o,
              ffn_norm_g, w_group, b_group, w_router, b_router, w_gate_up, w_down):
    cos, sin = rope_tables(positions)
    h = x
    k_shared = None
    v_shared = None
    for layer in range(DEPTH):
        if layer < N_A_LAYERS:
            i = layer
            h = h + conformer_conv_module(h, a_norm_g[i], a_pw1_w[i], a_pw1_b[i], a_dw_w[i], a_dw_b[i],
                                          a_ln_g[i], a_ln_b[i], a_pw2_w[i], a_pw2_b[i])
        else:
            i = layer - N_A_LAYERS
            if i == 0:
                k_shared, v_shared = shared_mla_kv(h, kv_norm_g, w_dkv, kv_latent_g, w_kr, w_ukv,
                                                   k_norm_g, cos, sin)
            h = h + mla_attention_layer(h, k_shared, v_shared, b_norm_g[i], w_dq[i], q_latent_g[i],
                                        w_uq[i], q_norm_g[i], w_o[i], cos, sin)
        h = h + hierarchical_moe(h, ffn_norm_g[layer], w_group[layer], b_group[layer], w_router[layer],
                                 b_router[layer], w_gate_up[layer], w_down[layer])
    return h


_drawn_inputs = setup_inputs


def setup_inputs(seed=0):
    import zlib

    import numpy as np

    out = dict(_drawn_inputs(seed))
    spreads = {}
    factors = {'a_pw1_b': 4.057,
     'a_ln_b': 4.956,
     'a_pw2_b': 2.751,
     'kv_latent_g': 2.836,
     'k_norm_g': 4.324,
     'b_norm_g': 3.982,
     'q_latent_g': 3.818,
     'q_norm_g': 3.104,
     'b_group': 3.074,
     'b_router': 3.521}
    for name, (base, spread) in spreads.items():
        noise = np.random.default_rng([zlib.crc32(name.encode()), seed]).standard_normal(out[name].shape)
        drawn = base * np.exp(spread * noise) if base else spread * noise
        out[name] = jnp.asarray(drawn.astype(out[name].dtype))
    for name, factor in factors.items():
        out[name] = (out[name] * factor).astype(out[name].dtype)
    return out
```

```python
from contextlib import ExitStack

import numpy as np

import concourse.bass as bass
from concourse import mybir

ALU = mybir.AluOpType
ACT = mybir.ActivationFunctionType
F32 = mybir.dt.float32
I32 = mybir.dt.int32
AX_X = mybir.AxisListType.X

P = 128
EPS = 1e-6
NEG = 1e30
CAP = 64
PAIR = 2 * CAP
ROPE_THETA = 10000.0
CHUNK = 64
GROUPS = 4


def trunk_kernel(nc: bass.Bass, a, out):
    _, S, D = a["x"].shape
    L, NE, _, FF2 = a["w_gate_up"].shape
    F = FF2 // 2
    TT = S // P
    KD = D // P
    KF = F // P
    CW = a["a_dw_w"].shape[1]
    PAD = CW - 1
    RKV = a["w_dkv"].shape[1]
    RQ = a["w_dq"].shape[2]
    ROPE = a["w_kr"].shape[1]
    HR = ROPE // 2
    QK = a["k_norm_g"].shape[0]
    NOPE = QK - ROPE
    H = a["w_uq"].shape[2] // QK
    DV = a["w_o"].shape[1] // H
    EG = NE // GROUPS
    NR = GROUPS + NE
    PASSES = -(-S // CAP)
    PAIRS = NE // 2
    HALF = 512
    assert TT == 2 and D == 2 * HALF and NOPE == P and DV == P and PAIR == P and KF * P == F and NE == 32

    with ExitStack() as ctx:
        def sb(name, shape, dt=F32):
            return ctx.enter_context(nc.sbuf_tensor(name, shape, dt))

        def sem(name):
            return ctx.enter_context(nc.semaphore(name))

        bank = [ctx.enter_context(nc.psum_tensor(f"bank{i}", [P, HALF], F32)) for i in range(8)]

        UNIT = 4 * D
        ring = sb("ring", [P, 6 * UNIT])
        w_gate_up_sb = [ring[:, s * 3 * UNIT:(s * 3 + 2) * UNIT].rearrange("p (k c) -> p k c", k=KD) for s in range(2)]
        w_down_sb = [ring[:, (s * 3 + 2) * UNIT:(s * 3 + 3) * UNIT].rearrange("p (k c) -> p k c", k=KF) for s in range(2)]
        pw1_sb = [ring[:, u * UNIT:(u + 1) * UNIT].rearrange("p (k c) -> p k c", k=KD) for u in range(4)]
        pw2_sb = ring[:, 4 * UNIT:6 * UNIT].rearrange("p (k c) -> p k c", k=KD)
        o1 = KD * (RKV + ROPE)
        o2 = o1 + KD * RQ
        o3 = o2 + (RQ // P) * H * QK
        w_dkvr_sb = ring[:, 0:o1].rearrange("p (k c) -> p k c", k=KD)
        w_dq_sb = ring[:, o1:o2].rearrange("p (k c) -> p k c", k=KD)
        w_uq_sb = ring[:, o2:o3].rearrange("p (k c) -> p k c", k=RQ // P)
        w_ukv_sb = ring[:, 3 * UNIT:4 * UNIT].rearrange("p (k c) -> p k c", k=RKV // P)
        w_o_sb = ring[:, 4 * UNIT:6 * UNIT].rearrange("p (k c) -> p k c", k=H)
        assert o3 <= 3 * UNIT

        h = sb("h", [P, TT, D])
        xn = sb("xn", [P, TT, D])
        xT = sb("xT", [P, KD, S])
        xT2 = sb("xT2", [P, KD, S])

        arena = sb("arena", [P, 16640])

        def view(offset, *shape):
            n = int(np.prod(shape))
            v = arena[:, offset:offset + n]
            if len(shape) == 1:
                return v
            if len(shape) == 2:
                return v.rearrange("p (a b) -> p a b", b=shape[1])
            return v.rearrange("p (a b c) -> p a b c", b=shape[1], c=shape[2])

        u_sb = view(0, KD, PAD + S)
        cv = view(2560, KD, S)
        sg = view(4608, 2, S)
        std_t = view(5120, S)
        rstd_t = view(5376, S)
        dw_rows = view(6144, D)
        pw2_b_row = view(7168, D)
        q_tok = view(0, TT, H * QK)
        q_h = q_tok.rearrange("p t (h c) -> p t h c", h=H)
        k_tok = view(3072, TT, H, NOPE)
        krh = view(5120, TT, H, ROPE)
        qrr = view(6144, TT, H, ROPE)
        v_tok = view(7168, TT, H, DV)
        kTn = view(9216, H, S)
        qTn = view(11264, H, S)
        kTr = view(13312, H, S)
        ckvT = view(15360, RKV // P, S)
        cqT = view(15872, RQ // P, S)
        qTr = xT2
        sc0 = view(0, H, P)
        sc1 = view(1024, H, S)
        pT0 = view(3072, H, P)
        pT1 = view(4096, H, TT, P)
        oT = xT
        cn = xn[:, 0, :]
        ckv_n = xn[:, 0, 0:TT * RKV].rearrange("p (t c) -> p t c", t=TT)
        cq_n = xn[:, 1, 0:TT * RQ].rearrange("p (t c) -> p t c", t=TT)
        kr_raw = xn[:, 0, 512:512 + TT * ROPE].rearrange("p (t c) -> p t c", t=TT)
        kr_rot = xn[:, 0, 640:640 + TT * ROPE].rearrange("p (t c) -> p t c", t=TT)
        sq_tmp = xT2[:, 0:6, :].rearrange("p a b -> p (a b)")
        rot_tmp = [view(13312 + i * 512, TT, H, HR) for i in range(4)]
        rot_tmq = [xT2[:, 2 * i:2 * i + 2, :].rearrange("p a b -> p (a b)").rearrange("p (t h c) -> p t h c", t=TT, h=H)
                   for i in range(4)]
        xe = [view(0 + s * 512, KD, CAP) for s in range(2)]
        hT = [view(1024 + s * 256, KF, CAP) for s in range(2)]
        sil = [view(1536 + s * 256, KF, CAP) for s in range(2)]
        yT = view(2048, KD, PAIR)
        y = view(3072, D)
        pick = [view(4096 + s * 128, TT, CAP) for s in range(2)]
        pw = view(4352, TT, PAIR)
        pwT = view(4608, S)

        ident = sb("ident", [P, P])
        upto = sb("upto", [P, P])
        ones = sb("ones", [P, P])
        mean_w = sb("mean_w", [P, P])
        eps_c = sb("eps_c", [P, 1])
        rows = sb("rows", [P, P])
        cols = sb("cols", [P, P])
        dwT = sb("dwT", [P, KD, CW])
        iota_i = sb("iota_i", [P, CAP], I32)
        iota = sb("iota", [P, CAP])
        iota_m = sb("iota_m", [P, CAP])
        wr = sb("wr", [P, L, KD, NR])
        br = sb("br", [P, L, NR])
        qk_gr = sb("qk_gr", [P, 2, ROPE])
        mask = sb("mask", [P, S])
        inv_freq = sb("inv_freq", [P, HR])
        pos_i = sb("pos_i", [P, TT], I32)
        pos_f = sb("pos_f", [P, TT])
        ang = sb("ang", [P, TT, HR])
        ang_k = sb("ang_k", [P, TT, HR])
        cos = sb("cos", [P, TT, HR])
        sin = sb("sin", [P, TT, HR])
        ss = sb("ss", [P, 4])
        rms = sb("rms", [P, 4])
        rr = sb("rr", [P, 4])
        lg = sb("lg", [P, TT, NR])
        gmx = sb("gmx", [P, TT])
        gex = sb("gex", [P, TT, GROUPS])
        gsm = sb("gsm", [P, TT])
        gw = sb("gw", [P, TT])
        geq = sb("geq", [P, TT, GROUPS])
        gix = sb("gix", [P, TT])
        em = sb("em", [P, TT, NE])
        eeq = sb("eeq", [P, TT, NE])
        oh1 = sb("oh1", [P, TT, NE])
        oh2 = sb("oh2", [P, TT, NE])
        mx1 = sb("mx1", [P, TT])
        mx2 = sb("mx2", [P, TT])
        eix = sb("eix", [P, TT])
        w1 = sb("w1", [P, TT])
        w2 = sb("w2", [P, TT])
        picked = sb("picked", [P, TT, NE])
        NC_ = 2 + PASSES * NE + 2
        slot = sb("slot", [P, TT, NC_])
        gate = sb("gate", [P, TT, NC_])
        cmx = sb("cmx", [P, 4])
        npairs_i = sb("npairs_i", [P, 1], I32)
        ss_kr = sb("ss_kr", [P, TT])
        ss_h = sb("ss_h", [P, 2, TT * H])
        r_h = sb("r_h", [P, 2, TT * H])
        smax = sb("smax", [P, TT, H])
        ssum = sb("ssum", [P, TT, H])
        sinv = sb("sinv", [P, TT, H])

        row_at, spots = 0, {}
        row_loads = []
        for name, ap, n in (
            ("a_norm_g", a["a_norm_g"][0], KD), ("pw1_b", a["a_pw1_b"][0], 2 * KD), ("dw_b", a["a_dw_b"][0], KD),
            ("ln_g", a["a_ln_g"][0], KD), ("ln_b", a["a_ln_b"][0], KD), ("kv_norm_g", a["kv_norm_g"], KD),
            ("b_norm_g", a["b_norm_g"][0], KD), ("ffn_norm_g0", a["ffn_norm_g"][0], KD), ("ffn_norm_g1", a["ffn_norm_g"][1], KD),
            ("kv_latent_g", a["kv_latent_g"], RKV // P), ("q_latent_g", a["q_latent_g"][0], RQ // P),
            ("k_gn", a["k_norm_g"][0:NOPE], 1), ("q_gn", a["q_norm_g"][0][0:NOPE], 1),
        ):
            spots[name] = row_at
            row_loads.append((row_at, n, ap.rearrange("(k p) -> k p", p=P)))
            row_at += n
        N_ROWS = row_at

        def col(name, k=0, n=1):
            return cols[:, spots[name] + k:spots[name] + k + n]

        def over(ap, n):
            return ap.unsqueeze(2).to_broadcast([P, ap.shape[1], n])

        def sc_junk(i, n):
            return arena[:, 9216 + i * HALF:9216 + i * HALF + n]

        def head_block(n):
            kind, t, hg = n // 4, (n % 4) // 2, n % 2
            dst = (kTn, kTr, qTn, qTr)[kind]
            rot = kind % 2 == 1
            return (dst[0:ROPE if rot else P, 4 * hg:4 * hg + 4, t * P:(t + 1) * P], rot,
                    col("k_gn") if kind == 0 else col("q_gn"))

        def prob_bank(n):
            return (6, 7, 0, 1, 2, 3)[n]

        def prob_block(n):
            if n < 2:
                return pT0[:, 4 * n:4 * n + 4, :]
            return pT1[:, 2 * (n - 2):2 * (n - 2) + 2, :, :].rearrange("p h k q -> p (h k) q")

        x_in, w_pw1 = sem("x_in"), [sem(f"w_pw1_{i}") for i in range(4)]
        w_pw2 = sem("w_pw2")
        rows_in, small_in, small2_in = sem("rows_in"), sem("small_in"), sem("small2_in")
        zeroed, const_ready, const_f = sem("zeroed"), sem("const_ready"), sem("const_f")
        cols_tr, cols_ready = sem("cols_tr"), sem("cols_ready")
        dve_step, act_step = sem("dve_step"), sem("act_step")
        ssq, rms_ready = [sem(f"ssq{i}") for i in range(4)], [sem(f"rms_ready{i}") for i in range(4)]
        xn_ready, tr_done = [sem(f"xn_ready{i}") for i in range(4)], [sem(f"tr_done{i}") for i in range(4)]
        xT_ready = [sem(f"xT_ready{i}") for i in range(4)]
        h_ready = [sem(f"h_ready{i}") for i in range(5)]
        xT2_ready = sem("xT2_ready")
        pw1_done, sg_ready, u_ready, u_zero = sem("pw1_done"), sem("sg_ready"), sem("u_ready"), sem("u_zero")
        conv_done, mean_done, diff_ready = sem("conv_done"), sem("mean_done"), sem("diff_ready")
        sq_ready, var_done, lstd_ready, dn_ready = sem("sq_ready"), sem("var_done"), sem("lstd_ready"), sem("dn_ready")
        c_ready, pw2_done, hb_ready = sem("c_ready"), sem("pw2_done"), sem("hb_ready")
        E = []
        for l in range(L):
            E.append({n: sem(f"{n}_{l}") for n in (
                "logits_done", "gexp_in", "gexp_ready", "eexp_in", "eexp_ready", "mask_ready", "pos_done", "npairs_ready",
                "w_gu_a", "w_gu_b", "w_dn_a", "w_dn_b", "picka_ready", "pickb_ready", "pw_ready",
                "ua_done", "ub_done", "da_done", "db_done", "g_done", "t_done", "pt_done", "s_done",
                "silu_done", "y_ready", "yT_ready", "hT_ready", "xe_ready", "s_added")})
        w_c, w_uq, w_ukv, w_o = sem("w_c"), sem("w_uq"), sem("w_ukv"), sem("w_o")
        ang_ready, trig = sem("ang_ready"), sem("trig")
        c_done, csq, crms_ready, cn_ready = sem("c_done"), sem("csq"), sem("crms_ready"), sem("cn_ready")
        ctr_done, cT_ready = sem("ctr_done"), sem("cT_ready")
        kvmm_done, kv_evac, qmm_done, q_evac = sem("kvmm_done"), sem("kv_evac"), sem("qmm_done"), sem("q_evac")
        kss_ready, krms_ready, k_ready = sem("kss_ready"), sem("krms_ready"), sem("k_ready")
        qss_ready, qrms_ready, q_ready = sem("qss_ready"), sem("qrms_ready"), sem("q_ready")
        hd_tr, hd_dve, hd_act = sem("hd_tr"), sem("hd_dve"), sem("hd_act")
        sc_done, smax_ready, exp_done, p_ready = sem("sc_done"), sem("smax_ready"), sem("exp_done"), sem("p_ready")
        ptr_done, pT_dve, pT_act = sem("ptr_done"), sem("pT_dve"), sem("pT_act")
        o_done, o_dve, o_act, wo_done = sem("o_done"), sem("o_dve"), sem("o_act"), sem("wo_done")
        out_done = sem("out_done")

        block = ctx.enter_context(nc.Block())

        @block.sync
        def _(sp):
            sp.dma_start(h[:, :, :], a["x"][0].rearrange("(t p) d -> p t d", p=P)).then_inc(x_in, 16)
            pw1 = a["a_pw1_w"][0].rearrange("(k p) c -> p k c", p=P)
            for i, c0 in enumerate((0, D, HALF, D + HALF)):
                sp.dma_start(pw1_sb[i], pw1[:, :, c0:c0 + HALF]).then_inc(w_pw1[i], 16)
            sp.dma_start(pw2_sb, a["a_pw2_w"][0].rearrange("(k p) c -> p k c", p=P)).then_inc(w_pw2, 16)

            def experts(l, first):
                e = E[l]
                gu = a["w_gate_up"][l].rearrange("e (k p) c -> e p k c", p=P)
                dn = a["w_down"][l].rearrange("e (k p) c -> e p k c", p=P)
                first(e, gu, dn)
                sp.wait_ge(e["npairs_ready"], 1)
                n_pairs = sp.value_load(npairs_i[0:1, 0:1], min_val=PAIRS, max_val=PAIRS * PASSES)
                with sp.Fori(1, n_pairs) as it:
                    ex = (it % PAIRS) * 2
                    sp.wait_ge(e["ua_done"], it)
                    sp.dma_start(w_gate_up_sb[0], gu[bass.ds(ex, 1)].rearrange("e p k c -> (e p) k c")).then_inc(e["w_gu_a"], 16)
                    sp.wait_ge(e["da_done"], it)
                    sp.dma_start(w_down_sb[0], dn[bass.ds(ex, 1)].rearrange("e p k c -> (e p) k c")).then_inc(e["w_dn_a"], 16)
                    sp.wait_ge(e["ub_done"], it)
                    sp.dma_start(w_gate_up_sb[1], gu[bass.ds(ex + 1, 1)].rearrange("e p k c -> (e p) k c")).then_inc(e["w_gu_b"], 16)
                    sp.wait_ge(e["db_done"], it)
                    sp.dma_start(w_down_sb[1], dn[bass.ds(ex + 1, 1)].rearrange("e p k c -> (e p) k c")).then_inc(e["w_dn_b"], 16)
                return n_pairs

            def first_after_conv(e, gu, dn):
                sp.wait_ge(pw1_done, 4)
                sp.dma_start(w_gate_up_sb[0], gu[0]).then_inc(e["w_gu_a"], 16)
                sp.wait_ge(pw1_done, 8)
                sp.dma_start(w_down_sb[0], dn[0]).then_inc(e["w_dn_a"], 16)
                sp.wait_ge(pw2_done, 4)
                sp.dma_start(w_gate_up_sb[1], gu[1]).then_inc(e["w_gu_b"], 16)
                sp.dma_start(w_down_sb[1], dn[1]).then_inc(e["w_dn_b"], 16)

            n0 = experts(0, first_after_conv)
            sp.wait_ge(E[0]["ua_done"], n0)
            sp.wait_ge(E[0]["da_done"], n0)
            sp.dma_start(w_dkvr_sb[:, :, 0:RKV], a["w_dkv"].rearrange("(k p) c -> p k c", p=P)).then_inc(w_c, 16)
            sp.dma_start(w_dkvr_sb[:, :, RKV:RKV + ROPE], a["w_kr"].rearrange("(k p) c -> p k c", p=P)).then_inc(w_c, 16)
            sp.dma_start(w_dq_sb, a["w_dq"][0].rearrange("(k p) c -> p k c", p=P)).then_inc(w_c, 16)
            sp.dma_start(w_uq_sb, a["w_uq"][0].rearrange("(k p) c -> p k c", p=P)).then_inc(w_uq, 16)
            sp.wait_ge(E[0]["ub_done"], n0)
            sp.wait_ge(E[0]["db_done"], n0)
            sp.dma_start(w_ukv_sb, a["w_ukv"].rearrange("(k p) c -> p k c", p=P)).then_inc(w_ukv, 16)
            sp.dma_start(w_o_sb, a["w_o"][0].rearrange("(k p) c -> p k c", p=P)).then_inc(w_o, 16)

            def first_after_attention(e, gu, dn):
                sp.wait_ge(qmm_done, 6)
                sp.dma_start(w_gate_up_sb[0], gu[0]).then_inc(e["w_gu_a"], 16)
                sp.dma_start(w_down_sb[0], dn[0]).then_inc(e["w_dn_a"], 16)
                sp.wait_ge(kvmm_done, 8)
                sp.wait_ge(wo_done, 4)
                sp.dma_start(w_gate_up_sb[1], gu[1]).then_inc(e["w_gu_b"], 16)
                sp.dma_start(w_down_sb[1], dn[1]).then_inc(e["w_dn_b"], 16)

            experts(1, first_after_attention)
            out_t = out[0].rearrange("(t p) d -> p t d", p=P)
            for j in range(4):
                tt, hf = j // 2, j % 2
                sp.wait_ge(h_ready[4], j + 1)
                sp.dma_start(out_t[:, tt, hf * HALF:(hf + 1) * HALF], h[:, tt, hf * HALF:(hf + 1) * HALF]).then_inc(out_done, 16)
            sp.wait_ge(out_done, 64)

        @block.gpsimd
        def _(pool):
            nc.gpsimd.memset(ident[:, :], 0.0).then_inc(zeroed, 1)
            nc.gpsimd.memset(upto[:, :], 1.0).then_inc(zeroed, 1)
            nc.gpsimd.memset(mask[:, :], 0.0).then_inc(zeroed, 1)
            pool.wait_ge(zeroed, 3)
            nc.gpsimd.affine_select(out=ident[:, :], in_=ident[:, :], compare_op=ALU.not_equal, fill=1.0, base=0,
                                    pattern=[[-1, P]], channel_multiplier=1).then_inc(const_ready, 1)
            nc.gpsimd.affine_select(out=upto[:, :], in_=upto[:, :], compare_op=ALU.is_ge, fill=0.0, base=0,
                                    pattern=[[1, P]], channel_multiplier=-1).then_inc(const_ready, 1)
            nc.gpsimd.memset(mask[0:CHUNK, S - CHUNK:S], -NEG).then_inc(const_ready, 1)
            nc.gpsimd.memset(ones[:, :], 1.0).then_inc(const_ready, 1)
            nc.gpsimd.memset(mean_w[:, :], 1.0 / D).then_inc(const_ready, 1)
            nc.gpsimd.memset(eps_c[:, :], EPS).then_inc(const_ready, 1)
            nc.gpsimd.memset(slot[:, :, :], -1.0).then_inc(const_ready, 1)
            nc.gpsimd.memset(gate[:, :, :], 0.0).then_inc(const_ready, 1)
            nc.gpsimd.iota(iota_i[:, :], pattern=[[1, CAP]], base=0, channel_multiplier=0).then_inc(const_ready, 1)
            nc.gpsimd.memset(u_sb[:, :, 0:PAD], 0.0).then_inc(u_zero, 1)
            pool.wait_ge(small_in, 16)
            pool.wait_ge(xn_ready[0], 2)
            for t in range(TT):
                nc.gpsimd.tensor_tensor(h[:, t, :], h[:, t, :], pw2_b_row, ALU.add).then_inc(hb_ready, 1)

        @block.scalar
        def _(act):
            act_n = [0]

            def link(ins):
                act_n[0] += 1
                ins.then_inc(act_step, 1)
                act.wait_ge(act_step, act_n[0])

            for r, n, ap in row_loads:
                act.dma_start(rows[r:r + n, :], ap).then_inc(rows_in, 16)
            act.dma_start(dw_rows[0:CW, :], a["a_dw_w"][0]).then_inc(rows_in, 16)
            act.dma_start(pw2_b_row, a["a_pw2_b"].to_broadcast([P, D])).then_inc(small_in, 16)
            for l in range(L):
                act.dma_start(wr[:, l, :, 0:GROUPS], a["w_group"][l].rearrange("(k p) g -> p k g", p=P)).then_inc(small2_in, 16)
                act.dma_start(wr[:, l, :, GROUPS:NR], a["w_router"][l].rearrange("(k p) g -> p k g", p=P)).then_inc(small2_in, 16)
                act.dma_start(br[:, l, 0:GROUPS], a["b_group"][l:l + 1].to_broadcast([P, GROUPS])).then_inc(small2_in, 16)
                act.dma_start(br[:, l, GROUPS:NR], a["b_router"][l:l + 1].to_broadcast([P, NE])).then_inc(small2_in, 16)
            act.dma_start(qk_gr[:, 0, :], a["k_norm_g"][NOPE:QK].unsqueeze(0).to_broadcast([P, ROPE])).then_inc(small2_in, 16)
            act.dma_start(qk_gr[:, 1, :], a["q_norm_g"][0:1, NOPE:QK].to_broadcast([P, ROPE])).then_inc(small2_in, 16)
            act.dma_start(inv_freq[:, :], a["inv_freq"].to_broadcast([P, HR])).then_inc(small2_in, 16)
            act.dma_start(pos_i[:, :], a["positions"][0].rearrange("(t p) -> p t", p=P), allow_slow_non_contiguous=True).then_inc(small2_in, 16)

            def norm(i):
                for t in range(TT):
                    if i == 0:
                        act.wait_ge(x_in, 16)
                        act.wait_ge(const_ready, 9)
                    else:
                        act.wait_ge(h_ready[i], 2 * t + 2)
                    nc.scalar.activation(xT2[:, 4 * t:4 * t + 4, :].rearrange("p a b -> p (a b)"), h[:, t, :], ACT.Square,
                                         accum_out=ss[:, t:t + 1]).then_inc(ssq[i], 1)
                act.wait_ge(ssq[i], 2)
                nc.scalar.activation(rms[:, 0:2], ss[:, 0:2], ACT.Sqrt, scale=1.0 / D, bias=eps_c[:, :]).then_inc(rms_ready[i], 1)

            norm(0)
            act.wait_ge(cols_ready, 1)
            for m in range(KD):
                act.wait_ge(pw1_done, m + 1)
                if m >= 2:
                    act.wait_ge(u_ready, m - 1)
                nc.scalar.activation(sg[:, m % 2, :], bank[4 + m % 4][:, S:2 * S], ACT.Sigmoid,
                                     bias=col("pw1_b", KD + m)).then_inc(sg_ready, 1)
            for m in range(KD):
                act.wait_ge(diff_ready, m + 1)
                nc.scalar.activation(xT[:, m, :], cv[:, m, :], ACT.Square).then_inc(sq_ready, 1)
            act.wait_ge(var_done, 1)
            nc.scalar.activation(std_t, bank[1][:, 0:S], ACT.Sqrt, bias=eps_c[:, :]).then_inc(lstd_ready, 1)
            for m in range(KD):
                act.wait_ge(dn_ready, m + 1)
                nc.scalar.activation(cv[:, m, :], cv[:, m, :], ACT.Silu, scale=col("ln_g", m), bias=col("ln_b", m)).then_inc(c_ready, 1)

            def experts(l):
                e = E[l]
                norm(1 + 2 * l)
                act.wait_ge(e["gexp_in"], 1)
                nc.scalar.activation(gex[:, :, :], gex[:, :, :], ACT.Exp).then_inc(e["gexp_ready"], 1)
                act.wait_ge(e["eexp_in"], 1)
                nc.scalar.activation(w2[:, :], w2[:, :], ACT.Exp).then_inc(e["eexp_ready"], 1)
                act.wait_ge(e["npairs_ready"], 1)
                n_pairs = act.value_load(npairs_i[0:1, 0:1], min_val=PAIRS, max_val=PAIRS * PASSES)

                def slots_back(it):
                    act.wait_ge(e["t_done"], it + 1)
                    nc.scalar.copy(y[:, 0:HALF], bank[3][:, :])
                    nc.scalar.copy(y[:, HALF:D], bank[4][:, :])
                    act.wait_ge(e["pt_done"], it + 1)
                    nc.scalar.copy(pwT, bank[5][:, 0:S]).then_inc(e["y_ready"], 1)

                def silu(it, s):
                    act.wait_ge(e["ua_done" if s == 0 else "ub_done"], it + 1)
                    nc.scalar.activation(sil[s], bank[1][:, 0:KF * CAP].rearrange("p (k c) -> p k c", k=KF),
                                         ACT.Silu).then_inc(e["silu_done"], 1)

                def outputs(it, s):
                    act.wait_ge(e["da_done" if s == 0 else "db_done"], it + 1)
                    nc.scalar.copy(yT[:, :, s * CAP:(s + 1) * CAP],
                                   bank[2][:, :].rearrange("p (k c) -> p k c", k=KD)).then_inc(e["yT_ready"], 1)

                with act.Fori(0, n_pairs) as it:
                    silu(it, 0)
                    slots_back(it)
                    outputs(it, 0)
                    silu(it, 1)
                    outputs(it, 1)
                slots_back(n_pairs)

            experts(0)

            norm(2)
            act.wait_ge(ang_ready, 1)
            nc.scalar.activation(sin[:, :, :], ang[:, :, :], ACT.Sin).then_inc(trig, 1)
            nc.scalar.activation(cos[:, :, :], ang[:, :, :], ACT.Sin, scale=0.5).then_inc(trig, 1)
            for b in range(4):
                act.wait_ge(xT_ready[2], b + 1)
                t, kh = b // 2, b % 2
                for j in range(4):
                    k = 4 * kh + j
                    ins = nc.scalar.activation(xT2[:, k, t * P:(t + 1) * P], bank[b][:, j * P:(j + 1) * P], ACT.Copy,
                                               scale=col("b_norm_g", k))
                ins.then_inc(xT2_ready, 1)
            for t in range(TT):
                act.wait_ge(c_done, t + 1)
                nc.scalar.activation(sc_junk(t, RKV), bank[4 + t][:, 0:RKV], ACT.Square, accum_out=ss[:, t:t + 1]).then_inc(csq, 1)
                nc.scalar.activation(sc_junk(2 + t, ROPE), bank[4 + t][:, RKV:RKV + ROPE], ACT.Square, accum_out=ss_kr[:, t:t + 1]).then_inc(csq, 1)
            for t in range(TT):
                act.wait_ge(c_done, 3 + t)
                nc.scalar.activation(sc_junk(4 + t, RQ), bank[6 + t][:, 0:RQ], ACT.Square, accum_out=ss[:, 2 + t:3 + t]).then_inc(csq, 1)
            act.wait_ge(csq, 6)
            nc.scalar.activation(rms[:, 0:2], ss[:, 0:2], ACT.Sqrt, scale=1.0 / RKV, bias=eps_c[:, :]).then_inc(crms_ready, 1)
            nc.scalar.activation(rms[:, 2:4], ss[:, 2:4], ACT.Sqrt, scale=1.0 / RQ, bias=eps_c[:, :]).then_inc(crms_ready, 1)
            for i in range(2 * 4):
                t, ch = i // 4, i % 4
                act.wait_ge(kvmm_done, i + 1)
                src = bank[4 + i % 4][:, :].rearrange("p (h w d) -> p h w d", h=2, w=2)
                nc.scalar.copy(k_tok[:, t, 2 * ch:2 * ch + 2, :], src[:, :, 0, :])
                nc.scalar.copy(v_tok[:, t, 2 * ch:2 * ch + 2, :], src[:, :, 1, :]).then_inc(kv_evac, 1)
            for i, (ready, got) in enumerate(((kss_ready, krms_ready), (qss_ready, qrms_ready))):
                act.wait_ge(ready, 1)
                nc.scalar.activation(r_h[:, i, :], ss_h[:, i, :], ACT.Sqrt, scale=1.0 / QK, bias=eps_c[:, :]).then_inc(got, 1)
            for n in range(1, 16, 2):
                act.wait_ge(hd_tr, n + 1)
                dst, rot, g = head_block(n)
                if rot:
                    nc.scalar.copy(dst, bank[n % 8][0:ROPE, :].rearrange("p (h q) -> p h q", h=4)).then_inc(hd_act, 1)
                else:
                    nc.scalar.activation(dst, bank[n % 8][:, :].rearrange("p (h q) -> p h q", h=4), ACT.Copy,
                                         scale=g).then_inc(hd_act, 1)
            for t in range(TT):
                act.wait_ge(smax_ready, t + 1)
                for hh in range(H):
                    s = (sc0 if t == 0 else sc1)[:, hh, :]
                    nc.scalar.activation(s, s, ACT.Exp, bias=smax[:, t, hh:hh + 1],
                                         accum_out=ssum[:, t, hh:hh + 1]).then_inc(exp_done, 1)
            for n in range(1, 6, 2):
                act.wait_ge(ptr_done, n + 1)
                nc.scalar.copy(prob_block(n), bank[prob_bank(n)][:, :].rearrange("p (a q) -> p a q", a=4)).then_inc(pT_act, 1)
            for n in range(1, 4, 2):
                act.wait_ge(o_done, n + 1)
                t, hg = n // 2, n % 2
                nc.scalar.copy(oT[:, 4 * hg:4 * hg + 4, t * P:(t + 1) * P],
                               bank[4 + n][:, :].rearrange("p (h q) -> p h q", h=4)).then_inc(o_act, 1)

            experts(1)

        @block.tensor
        def _(pe):
            pe.wait_ge(const_ready, 9)
            pe.wait_ge(rows_in, 16 * (len(row_loads) + 1))
            nc.tensor.transpose(bank[7][:, 0:N_ROWS], rows[0:N_ROWS, :], ident[0:N_ROWS, 0:N_ROWS])
            for m in range(KD):
                ins = nc.tensor.transpose(bank[7][:, P + m * CW:P + (m + 1) * CW], dw_rows[0:CW, m * P:(m + 1) * P],
                                          ident[0:CW, 0:CW])
            ins.then_inc(cols_tr, 1)

            def norm(i):
                for b in range(4):
                    t, kh = b // 2, b % 2
                    pe.wait_ge(xn_ready[i], t + 1)
                    for j in range(4):
                        k = 4 * kh + j
                        ins = nc.tensor.transpose(bank[b][:, j * P:(j + 1) * P], xn[:, t, k * P:(k + 1) * P], ident[:, :])
                    ins.then_inc(tr_done[i], 1)

            norm(0)
            pe.wait_ge(cols_ready, 1)
            pe.wait_ge(xT_ready[0], 4)
            for m in range(KD):
                if m % 4 == 0:
                    pe.wait_ge(w_pw1[2 * (m // 4)], 16)
                    pe.wait_ge(w_pw1[2 * (m // 4) + 1], 16)
                if m >= 4:
                    pe.wait_ge(u_ready, m - 3)
                for part in range(2):
                    for k in range(KD):
                        ins = nc.tensor.matmul(bank[4 + m % 4][:, part * S:(part + 1) * S],
                                               pw1_sb[2 * (m // 4) + part][:, k, (m % 4) * P:(m % 4 + 1) * P],
                                               xT[:, k, :], start=(k == 0), stop=(k == KD - 1))
                ins.then_inc(pw1_done, 1)
            for m in range(KD):
                pe.wait_ge(conv_done, m + 1)
                ins = nc.tensor.matmul(bank[0][:, 0:S], mean_w[:, :], cv[:, m, :], start=(m == 0), stop=(m == KD - 1))
            ins.then_inc(mean_done, 1)
            for m in range(KD):
                pe.wait_ge(sq_ready, m + 1)
                ins = nc.tensor.matmul(bank[1][:, 0:S], mean_w[:, :], xT[:, m, :], start=(m == 0), stop=(m == KD - 1))
            ins.then_inc(var_done, 1)
            pe.wait_ge(w_pw2, 16)
            pe.wait_ge(u_ready, KD)
            for k in range(KD):
                pe.wait_ge(c_ready, k + 1)
                for j in range(4):
                    t, hf = j // 2, j % 2
                    ins = nc.tensor.matmul(bank[4 + j][:, :], cv[:, k, t * P:(t + 1) * P],
                                           pw2_sb[:, k, hf * HALF:(hf + 1) * HALF], start=(k == 0), stop=(k == KD - 1))
                    if k == KD - 1:
                        ins.then_inc(pw2_done, 1)

            def experts(l):
                e = E[l]
                norm(1 + 2 * l)
                if l == 0:
                    pe.wait_ge(small2_in, 16 * (4 * L + 4))
                pe.wait_ge(xT_ready[1 + 2 * l], 4)
                for t in range(TT):
                    for k in range(KD):
                        ins = nc.tensor.matmul(bank[4][:, t * CAP:t * CAP + NR], xT[:, k, t * P:(t + 1) * P], wr[:, l, k, :],
                                               start=(k == 0), stop=(k == KD - 1))
                ins.then_inc(e["logits_done"], 1)
                pe.wait_ge(e["mask_ready"], 1)
                nc.tensor.matmul(bank[5][:, 0:NE], upto[:, :], picked[:, 0, :], start=True, stop=True)
                nc.tensor.matmul(bank[5][:, NE:2 * NE], ones[:, :], picked[:, 0, :], start=True, stop=False)
                nc.tensor.matmul(bank[5][:, NE:2 * NE], upto[:, :], picked[:, 1, :], start=False, stop=True)
                nc.tensor.matmul(bank[5][:, 2 * NE:3 * NE], ones[:, :], picked[:, 0, :], start=True, stop=False)
                nc.tensor.matmul(bank[5][:, 2 * NE:3 * NE], ones[:, :], picked[:, 1, :], start=False, stop=True).then_inc(e["pos_done"], 1)

                def gather(s):
                    for k in range(KD):
                        for t in range(TT):
                            ins = nc.tensor.matmul(bank[0][:, k * CAP:(k + 1) * CAP], xn[:, t, k * P:(k + 1) * P],
                                                   pick[s][:, t, :], start=(t == 0), stop=(t == TT - 1))
                    ins.then_inc(e["g_done"], 1)

                def gate_up(s):
                    for m in range(2 * KF):
                        for k in range(KD):
                            ins = nc.tensor.matmul(bank[1][:, m * CAP:(m + 1) * CAP], w_gate_up_sb[s][:, k, m * P:(m + 1) * P],
                                                   xe[s][:, k, :], start=(k == 0), stop=(k == KD - 1))
                    ins.then_inc(e["ua_done" if s == 0 else "ub_done"], 1)

                def down(s):
                    for m in range(KD):
                        for k in range(KF):
                            ins = nc.tensor.matmul(bank[2][:, m * CAP:(m + 1) * CAP], w_down_sb[s][:, k, m * P:(m + 1) * P],
                                                   hT[s][:, k, :], start=(k == 0), stop=(k == KF - 1))
                    ins.then_inc(e["da_done" if s == 0 else "db_done"], 1)

                def slots_back(it):
                    pe.wait_ge(e["yT_ready"], 2 * it + 2)
                    for k in range(KD):
                        ins = nc.tensor.transpose(bank[3 + k // 4][:, (k % 4) * P:(k % 4 + 1) * P], yT[:, k, :], ident[:, :])
                    ins.then_inc(e["t_done"], 1)
                    pe.wait_ge(e["pw_ready"], it + 1)
                    for t in range(TT):
                        ins = nc.tensor.transpose(bank[5][:, t * P:(t + 1) * P], pw[:, t, :], ident[:, :])
                    ins.then_inc(e["pt_done"], 1)

                def scatter(it, added, base):
                    pe.wait_ge(e["y_ready"], it + 1)
                    for j in range(4):
                        t, hf = j // 2, j % 2
                        if j >= 2:
                            pe.wait_ge(added, base + j - 1)
                        nc.tensor.matmul(bank[6 + j % 2][:, :], pwT[:, t * P:(t + 1) * P], y[:, hf * HALF:(hf + 1) * HALF],
                                         start=True, stop=True).then_inc(e["s_done"], 1)

                pe.wait_ge(e["picka_ready"], 1)
                gather(0)
                pe.wait_ge(e["npairs_ready"], 1)
                n_pairs = pe.value_load(npairs_i[0:1, 0:1], min_val=PAIRS, max_val=PAIRS * PASSES)
                with pe.Fori(0, n_pairs) as it:
                    pe.wait_ge(e["xe_ready"], 2 * it + 1)
                    pe.wait_ge(e["w_gu_a"], 16 * it + 16)
                    gate_up(0)
                    slots_back(it)
                    pe.wait_ge(e["pickb_ready"], it + 1)
                    gather(1)
                    scatter(it, e["s_added"], 4 * it)
                    pe.wait_ge(e["hT_ready"], 2 * it + 1)
                    pe.wait_ge(e["w_dn_a"], 16 * it + 16)
                    down(0)
                    pe.wait_ge(e["xe_ready"], 2 * it + 2)
                    pe.wait_ge(e["w_gu_b"], 16 * it + 16)
                    gate_up(1)
                    pe.wait_ge(e["picka_ready"], it + 2)
                    gather(0)
                    pe.wait_ge(e["hT_ready"], 2 * it + 2)
                    pe.wait_ge(e["w_dn_b"], 16 * it + 16)
                    pe.wait_ge(e["yT_ready"], 2 * it + 3)
                    down(1)
                slots_back(n_pairs)
                scatter(n_pairs, h_ready[2 + 2 * l], 0)

            experts(0)

            norm(2)
            pe.wait_ge(w_c, 48)
            pe.wait_ge(xT_ready[2], 4)
            for t in range(TT):
                for k in range(KD):
                    ins = nc.tensor.matmul(bank[4 + t][:, 0:RKV + ROPE], xT[:, k, t * P:(t + 1) * P], w_dkvr_sb[:, k, :],
                                           start=(k == 0), stop=(k == KD - 1))
                ins.then_inc(c_done, 1)
            pe.wait_ge(xT2_ready, 4)
            for t in range(TT):
                for k in range(KD):
                    ins = nc.tensor.matmul(bank[6 + t][:, 0:RQ], xT2[:, k, t * P:(t + 1) * P], w_dq_sb[:, k, :],
                                           start=(k == 0), stop=(k == KD - 1))
                ins.then_inc(c_done, 1)
            pe.wait_ge(cn_ready, 4)
            for src, n, b0 in ((ckv_n, RKV // P, 0), (cq_n, RQ // P, 1)):
                for k in range(n):
                    for t in range(TT):
                        ins = nc.tensor.transpose(bank[b0 + k // 2][:, (2 * (k % 2) + t) * P:(2 * (k % 2) + t + 1) * P],
                                                  src[:, t, k * P:(k + 1) * P], ident[:, :])
                    if k % 2 == 1 or k == n - 1:
                        ins.then_inc(ctr_done, 1)
            pe.wait_ge(w_ukv, 16)
            pe.wait_ge(cT_ready, 3)
            for i in range(8):
                t, ch = i // 4, i % 4
                if i >= 4:
                    pe.wait_ge(kv_evac, i - 3)
                for k in range(RKV // P):
                    ins = nc.tensor.matmul(bank[4 + i % 4][:, :], ckvT[:, k, t * P:(t + 1) * P],
                                           w_ukv_sb[:, k, ch * HALF:(ch + 1) * HALF], start=(k == 0), stop=(k == RKV // P - 1))
                ins.then_inc(kvmm_done, 1)
            pe.wait_ge(w_uq, 16)
            for i in range(6):
                t, ch = i // 3, i % 3
                if i >= 4:
                    pe.wait_ge(q_evac, i - 3)
                for k in range(RQ // P):
                    ins = nc.tensor.matmul(bank[i % 4][:, :], cqT[:, k, t * P:(t + 1) * P],
                                           w_uq_sb[:, k, ch * HALF:(ch + 1) * HALF], start=(k == 0), stop=(k == RQ // P - 1))
                ins.then_inc(qmm_done, 1)
            pe.wait_ge(q_evac, 6)
            for n in range(16):
                kind, t, hg = n // 4, (n % 4) // 2, n % 2
                if n == 0:
                    pe.wait_ge(k_ready, 1)
                if n == 8:
                    pe.wait_ge(q_ready, 1)
                if n >= 8:
                    pe.wait_ge(hd_dve if n % 2 == 0 else hd_act, (n - 8) // 2 + 1)
                for j in range(4):
                    hh = 4 * hg + j
                    src = (k_tok[:, t, hh, :], krh[:, t, hh, :], q_h[:, t, hh, 0:NOPE], qrr[:, t, hh, :])[kind]
                    ins = nc.tensor.transpose(bank[n % 8][0:src.shape[1], j * P:(j + 1) * P], src, ident[:, :])
                ins.then_inc(hd_tr, 1)
            pe.wait_ge(hd_dve, 8)
            pe.wait_ge(hd_act, 8)
            for t in range(TT):
                nk = (t + 1) * P
                for hh in range(H):
                    b = hh // 4 if t == 0 else 2 + hh // 2
                    c = (hh % 4) * P if t == 0 else (hh % 2) * S
                    nc.tensor.matmul(bank[b][:, c:c + nk], qTn[:, hh, t * P:(t + 1) * P], kTn[:, hh, 0:nk], start=True, stop=False)
                    ins = nc.tensor.matmul(bank[b][:, c:c + nk], qTr[0:ROPE, hh, t * P:(t + 1) * P], kTr[0:ROPE, hh, 0:nk],
                                           start=False, stop=True)
                    if hh % (4 if t == 0 else 2) == (3 if t == 0 else 1):
                        ins.then_inc(sc_done, 1)
            for n in range(6):
                if n == 0:
                    pe.wait_ge(p_ready, 1)
                if n == 2:
                    pe.wait_ge(p_ready, 2)
                for j in range(4):
                    src = sc0[:, 4 * n + j, :] if n < 2 else sc1[:, 2 * (n - 2) + j // 2, (j % 2) * P:(j % 2 + 1) * P]
                    ins = nc.tensor.transpose(bank[prob_bank(n)][:, j * P:(j + 1) * P], src, ident[:, :])
                ins.then_inc(ptr_done, 1)
            pe.wait_ge(pT_dve, 3)
            pe.wait_ge(pT_act, 3)
            for t in range(TT):
                for hh in range(H):
                    for kt in range(t + 1):
                        ins = nc.tensor.matmul(bank[4 + 2 * t + hh // 4][:, (hh % 4) * P:(hh % 4 + 1) * P], v_tok[:, kt, hh, :],
                                               pT0[:, hh, :] if t == 0 else pT1[:, hh, kt, :],
                                               start=(kt == 0), stop=(kt == t))
                    if hh % 4 == 3:
                        ins.then_inc(o_done, 1)
            pe.wait_ge(w_o, 16)
            pe.wait_ge(o_dve, 2)
            pe.wait_ge(o_act, 2)
            for j in range(4):
                t, hf = j // 2, j % 2
                for hh in range(H):
                    ins = nc.tensor.matmul(bank[j][:, :], oT[:, hh, t * P:(t + 1) * P], w_o_sb[:, hh, hf * HALF:(hf + 1) * HALF],
                                           start=(hh == 0), stop=(hh == H - 1))
                ins.then_inc(wo_done, 1)

            experts(1)

        @block.vector
        def _(dve):
            dve_n = [0]
            V = nc.vector

            def link(ins):
                dve_n[0] += 1
                ins.then_inc(dve_step, 1)
                dve.wait_ge(dve_step, dve_n[0])

            dve.wait_ge(const_ready, 9)
            link(V.tensor_copy(iota[:, :], iota_i[:, :]))
            V.tensor_scalar(iota_m[:, :], iota[:, :], -float(CAP), None, ALU.add).then_inc(const_f, 1)
            dve.wait_ge(cols_tr, 1)
            V.tensor_copy(cols[:, 0:N_ROWS], bank[7][:, 0:N_ROWS])
            V.tensor_copy(dwT[:, :, :], bank[7][:, P:P + KD * CW].rearrange("p (m w) -> p m w", m=KD)).then_inc(cols_ready, 1)
            dve.wait_ge(cols_ready, 1)

            def norm(i, gain):
                dve.wait_ge(rms_ready[i], 1)
                link(V.reciprocal(rr[:, 0:2], rms[:, 0:2]))
                for t in range(TT):
                    V.tensor_scalar(xn[:, t, :], h[:, t, :], rr[:, t:t + 1], None, ALU.mult).then_inc(xn_ready[i], 1)
                for b in range(4):
                    t, kh = b // 2, b % 2
                    dve.wait_ge(tr_done[i], b + 1)
                    V.tensor_tensor(xT[:, 4 * kh:4 * kh + 4, t * P:(t + 1) * P], bank[b][:, :].rearrange("p (k q) -> p k q", k=4),
                                    over(col(gain, 4 * kh, 4), P), ALU.mult).then_inc(xT_ready[i], 1)

            norm(0, "a_norm_g")
            dve.wait_ge(u_zero, 1)
            for m in range(KD):
                dve.wait_ge(sg_ready, m + 1)
                V.scalar_tensor_tensor(out=u_sb[:, m, PAD:PAD + S], in0=bank[4 + m % 4][:, 0:S], scalar=col("pw1_b", m),
                                       in1=sg[:, m % 2, :], op0=ALU.add, op1=ALU.mult).then_inc(u_ready, 1)
                dve.wait_ge(u_ready, m + 1)
                link(V.tensor_scalar(cv[:, m, :], u_sb[:, m, 0:S], dwT[:, m, 0:1], col("dw_b", m), ALU.mult, ALU.add))
                for w in range(1, CW):
                    ins = V.scalar_tensor_tensor(out=cv[:, m, :], in0=u_sb[:, m, w:w + S], scalar=dwT[:, m, w:w + 1],
                                                 in1=cv[:, m, :], op0=ALU.mult, op1=ALU.add)
                    if w < CW - 1:
                        link(ins)
                ins.then_inc(conv_done, 1)
            dve.wait_ge(mean_done, 1)
            dve.wait_ge(conv_done, KD)
            for m in range(KD):
                V.tensor_tensor(cv[:, m, :], cv[:, m, :], bank[0][:, 0:S], ALU.subtract).then_inc(diff_ready, 1)
            dve.wait_ge(lstd_ready, 1)
            link(V.reciprocal(rstd_t, std_t))
            for m in range(KD):
                V.tensor_tensor(cv[:, m, :], cv[:, m, :], rstd_t, ALU.mult).then_inc(dn_ready, 1)
            dve.wait_ge(hb_ready, 2)
            for j in range(4):
                t, hf = j // 2, j % 2
                dve.wait_ge(pw2_done, j + 1)
                V.tensor_tensor(h[:, t, hf * HALF:(hf + 1) * HALF], bank[4 + j][:, :], h[:, t, hf * HALF:(hf + 1) * HALF],
                                ALU.add).then_inc(h_ready[1], 1)

            def experts(l):
                e = E[l]
                norm(1 + 2 * l, f"ffn_norm_g{l}")
                G = GROUPS
                dve.wait_ge(e["logits_done"], 1)
                link(V.tensor_tensor(lg[:, :, :], bank[4][:, 0:TT * CAP].rearrange("p (t c) -> p t c", t=TT)[:, :, 0:NR],
                                     br[:, l, :].unsqueeze(1).to_broadcast([P, TT, NR]), ALU.add))
                link(V.tensor_reduce(gmx[:, :], lg[:, :, 0:G], AX_X, ALU.max))
                V.tensor_tensor(gex[:, :, :], lg[:, :, 0:G], over(gmx[:, :], G), ALU.subtract).then_inc(e["gexp_in"], 1)
                link(V.tensor_tensor(geq[:, :, :], lg[:, :, 0:G], over(gmx[:, :], G), ALU.is_equal))
                link(V.tensor_tensor(geq[:, :, :], geq[:, :, :], iota_m[:, 0:G].unsqueeze(1).to_broadcast([P, TT, G]), ALU.mult))
                link(V.tensor_reduce(gix[:, :], geq[:, :, :], AX_X, ALU.min))
                link(V.tensor_tensor(geq[:, :, :], iota_m[:, 0:G].unsqueeze(1).to_broadcast([P, TT, G]), over(gix[:, :], G), ALU.is_equal))
                link(V.tensor_scalar(geq[:, :, :], geq[:, :, :], NEG, -NEG, ALU.mult, ALU.add))
                link(V.tensor_tensor(em[:, :, :].rearrange("p t (g x) -> p t g x", g=G),
                                     lg[:, :, G:NR].rearrange("p t (g x) -> p t g x", g=G),
                                     geq[:, :, :].unsqueeze(3).to_broadcast([P, TT, G, EG]), ALU.add))
                im = iota_m[:, 0:NE].unsqueeze(1).to_broadcast([P, TT, NE])
                for mx, oh in ((mx1, oh1), (mx2, oh2)):
                    link(V.tensor_reduce(mx[:, :], em[:, :, :], AX_X, ALU.max))
                    link(V.tensor_tensor(eeq[:, :, :], em[:, :, :], over(mx[:, :], NE), ALU.is_equal))
                    link(V.tensor_tensor(eeq[:, :, :], eeq[:, :, :], im, ALU.mult))
                    link(V.tensor_reduce(eix[:, :], eeq[:, :, :], AX_X, ALU.min))
                    link(V.tensor_tensor(oh[:, :, :], im, over(eix[:, :], NE), ALU.is_equal))
                    if mx is mx1:
                        link(V.scalar_tensor_tensor(out=em[:, :, :], in0=oh[:, :, :], scalar=-2 * NEG, in1=em[:, :, :],
                                                    op0=ALU.mult, op1=ALU.add))
                V.tensor_tensor(picked[:, :, :], oh1[:, :, :], oh2[:, :, :], ALU.add).then_inc(e["mask_ready"], 1)
                V.tensor_tensor(w2[:, :], mx2[:, :], mx1[:, :], ALU.subtract).then_inc(e["eexp_in"], 1)
                dve.wait_ge(e["gexp_ready"], 1)
                link(V.tensor_reduce(gsm[:, :], gex[:, :, :], AX_X, ALU.add))
                link(V.reciprocal(gw[:, :], gsm[:, :]))
                dve.wait_ge(e["eexp_ready"], 1)
                link(V.tensor_scalar(w1[:, :], w2[:, :], 1.0, None, ALU.add))
                link(V.reciprocal(w1[:, :], w1[:, :]))
                link(V.tensor_tensor(w1[:, :], w1[:, :], gw[:, :], ALU.mult))
                link(V.tensor_tensor(w2[:, :], w1[:, :], w2[:, :], ALU.mult))
                link(V.tensor_tensor(oh1[:, :, :], oh1[:, :, :], over(w1[:, :], NE), ALU.mult))
                link(V.tensor_tensor(oh2[:, :, :], oh2[:, :, :], over(w2[:, :], NE), ALU.mult))
                link(V.tensor_tensor(oh1[:, :, :], oh1[:, :, :], oh2[:, :, :], ALU.add))
                for q in range(PASSES):
                    V.tensor_copy(gate[:, :, 2 + q * NE:2 + (q + 1) * NE], oh1[:, :, :])
                dve.wait_ge(e["pos_done"], 1)
                link(V.tensor_tensor(eeq[:, :, :], bank[5][:, 0:TT * NE].rearrange("p (t x) -> p t x", t=TT), picked[:, :, :], ALU.mult))
                for q in range(PASSES):
                    ins = V.tensor_scalar(slot[:, :, 2 + q * NE:2 + (q + 1) * NE], eeq[:, :, :], -1.0 - q * CAP, None, ALU.add)
                link(ins)
                link(V.tensor_reduce(cmx[:, 0:1], bank[5][:, 2 * NE:3 * NE], AX_X, ALU.max))
                for q in range(1, PASSES):
                    link(V.tensor_scalar(cmx[:, q:q + 1], cmx[:, 0:1], q * CAP + 0.5, float(PAIRS), ALU.is_ge, ALU.mult))
                link(V.tensor_reduce(cmx[:, 0:1], cmx[:, 1:PASSES], AX_X, ALU.add))
                V.tensor_scalar(npairs_i[:, :], cmx[:, 0:1], float(PAIRS), None, ALU.add).then_inc(e["npairs_ready"], 1)

                def one_hot(s, column, done):
                    for t in range(TT):
                        ins = V.tensor_scalar(pick[s][:, t, :], iota[:, :], slot[:, t, bass.ds(column, 1)], None, ALU.is_equal)
                    ins.then_inc(done, 1)

                def gated(it):
                    for s in range(2):
                        for t in range(TT):
                            ins = V.tensor_scalar(pw[:, t, s * CAP:(s + 1) * CAP], iota[:, :], slot[:, t, bass.ds(2 * it + s, 1)],
                                                  gate[:, t, bass.ds(2 * it + s, 1)], ALU.is_equal, ALU.mult)
                    ins.then_inc(e["pw_ready"], 1)

                def tokens_in(n, s):
                    dve.wait_ge(e["g_done"], n)
                    V.tensor_tensor(xe[s], bank[0][:, :].rearrange("p (k c) -> p k c", k=KD),
                                    over(col(f"ffn_norm_g{l}", 0, KD), CAP), ALU.mult).then_inc(e["xe_ready"], 1)

                def hidden(it, s):
                    dve.wait_ge(e["silu_done"], 2 * it + 1 + s)
                    V.tensor_tensor(hT[s], sil[s], bank[1][:, KF * CAP:2 * KF * CAP].rearrange("p (k c) -> p k c", k=KF),
                                    ALU.mult).then_inc(e["hT_ready"], 1)

                def add_scattered(it, added):
                    for j in range(4):
                        t, hf = j // 2, j % 2
                        dve.wait_ge(e["s_done"], 4 * it + 1 + j)
                        V.tensor_tensor(h[:, t, hf * HALF:(hf + 1) * HALF], bank[6 + j % 2][:, :],
                                        h[:, t, hf * HALF:(hf + 1) * HALF], ALU.add).then_inc(added, 1)

                dve.wait_ge(dve_step, dve_n[0])
                V.memset(yT, 0.0).then_inc(e["yT_ready"], 2)
                one_hot(0, 2, e["picka_ready"])
                dve.wait_ge(e["npairs_ready"], 1)
                n_pairs = dve.value_load(npairs_i[0:1, 0:1], min_val=PAIRS, max_val=PAIRS * PASSES)
                tokens_in(1, 0)
                with dve.Fori(0, n_pairs) as it:
                    gated(it)
                    one_hot(1, 2 * it + 3, e["pickb_ready"])
                    hidden(it, 0)
                    tokens_in(2 * it + 2, 1)
                    add_scattered(it, e["s_added"])
                    one_hot(0, 2 * it + 4, e["picka_ready"])
                    hidden(it, 1)
                    tokens_in(2 * it + 3, 0)
                gated(n_pairs)
                add_scattered(n_pairs, h_ready[2 + 2 * l])

            experts(0)

            MAGIC = 1.5 * 2.0 ** 23
            TWO_PI = 2.0 * np.pi
            p1 = float(np.float32(np.floor(TWO_PI * 2 ** 8) / 2 ** 8))
            p2 = float(np.floor((TWO_PI - p1) * 2 ** 20) / 2 ** 20)
            p3 = float(np.float32(TWO_PI - p1 - p2))
            dve.wait_ge(small2_in, 16 * (4 * L + 4))
            link(V.tensor_copy(pos_f[:, :], pos_i[:, :]))
            for t in range(TT):
                ins = V.tensor_scalar(ang[:, t, :], inv_freq[:, :], pos_f[:, t:t + 1], None, ALU.mult)
            link(ins)
            link(V.tensor_scalar(ang_k[:, :, :], ang[:, :, :], 1.0 / TWO_PI, None, ALU.mult))
            link(V.tensor_scalar(ang_k[:, :, :], ang_k[:, :, :], MAGIC, None, ALU.add))
            link(V.tensor_scalar(ang_k[:, :, :], ang_k[:, :, :], -MAGIC, None, ALU.add))
            for part in (p1, p2):
                link(V.scalar_tensor_tensor(out=ang[:, :, :], in0=ang_k[:, :, :], scalar=-part, in1=ang[:, :, :],
                                            op0=ALU.mult, op1=ALU.add))
            link(V.scalar_tensor_tensor(out=ang[:, :, :], in0=ang_k[:, :, :], scalar=-p3, in1=ang[:, :, :],
                                        op0=ALU.mult, op1=ALU.add))
            PI_IN = float(np.nextafter(np.float32(np.pi), np.float32(0)))
            V.tensor_scalar(ang[:, :, :], ang[:, :, :], PI_IN, -PI_IN, ALU.min, ALU.max).then_inc(ang_ready, 1)

            norm(2, "kv_norm_g")
            dve.wait_ge(trig, 2)
            link(V.tensor_tensor(cos[:, :, :], cos[:, :, :], cos[:, :, :], ALU.mult))
            link(V.tensor_scalar(cos[:, :, :], cos[:, :, :], -2.0, 1.0, ALU.mult, ALU.add))
            dve.wait_ge(crms_ready, 2)
            link(V.reciprocal(rr[:, :], rms[:, :]))
            for t in range(TT):
                V.tensor_scalar(ckv_n[:, t, :], bank[4 + t][:, 0:RKV], rr[:, t:t + 1], None, ALU.mult).then_inc(cn_ready, 1)
                V.tensor_copy(kr_raw[:, t, :], bank[4 + t][:, RKV:RKV + ROPE])
                V.tensor_scalar(cq_n[:, t, :], bank[6 + t][:, 0:RQ], rr[:, 2 + t:3 + t], None, ALU.mult).then_inc(cn_ready, 1)
            for n, (dst, b, g, w) in enumerate(((ckvT, 0, "kv_latent_g", 2), (cqT[:, 0:2, :], 1, "q_latent_g", 2),
                                                (cqT[:, 2:3, :], 2, "q_latent_g", 1))):
                dve.wait_ge(ctr_done, n + 1)
                V.tensor_tensor(dst, bank[b][:, 0:w * S].rearrange("p (k q) -> p k q", k=w),
                                over(col(g, 2 if n == 2 else 0, w), S), ALU.mult).then_inc(cT_ready, 1)

            def rotate(dst, src, shape, tmp):
                def like(x):
                    return x if len(shape) == 3 else x.unsqueeze(2).to_broadcast([P, TT, H, HR])
                lo, hi = (slice(0, HR), slice(HR, ROPE))
                pick_ = (lambda x, s: x[:, :, s]) if len(shape) == 3 else (lambda x, s: x[:, :, :, s])
                c, s_ = like(cos[:, :, :]), like(sin[:, :, :])
                x1, x2 = pick_(src, lo), pick_(src, hi)
                V.tensor_tensor(tmp[0], x1, c, ALU.mult)
                V.tensor_tensor(tmp[1], x2, s_, ALU.mult)
                V.tensor_tensor(tmp[2], x1, s_, ALU.mult)
                link(V.tensor_tensor(tmp[3], x2, c, ALU.mult))
                V.tensor_tensor(pick_(dst, lo), tmp[0], tmp[1], ALU.subtract)
                link(V.tensor_tensor(pick_(dst, hi), tmp[2], tmp[3], ALU.add))

            link(V.tensor_tensor(kr_raw, kr_raw, qk_gr[:, 0, :].unsqueeze(1).to_broadcast([P, TT, ROPE]), ALU.mult))
            rotate(kr_rot, kr_raw, (P, TT, HR), [t[:, :, 0, :] for t in rot_tmp])
            dve.wait_ge(kv_evac, 8)
            for t in range(TT):
                sq = sq_tmp[:, 0:H * NOPE].rearrange("p (h c) -> p h c", h=H)
                link(V.tensor_tensor(sq, k_tok[:, t, :, :], k_tok[:, t, :, :], ALU.mult))
                link(V.tensor_reduce(ss_h[:, 0, t * H:(t + 1) * H], sq, AX_X, ALU.add))
            for t in range(TT):
                V.tensor_scalar(ss_h[:, 0, t * H:(t + 1) * H], ss_h[:, 0, t * H:(t + 1) * H], ss_kr[:, t:t + 1], None,
                                ALU.add)
            link(V.memset(ang_k[:, 0, 0:1], 0.0))
            V.memset(ang_k[:, 0, 0:1], 0.0).then_inc(kss_ready, 1)
            dve.wait_ge(krms_ready, 1)
            link(V.reciprocal(r_h[:, 0, :], r_h[:, 0, :]))
            rk = r_h[:, 0, :]
            V.tensor_tensor(k_tok.rearrange("p t h c -> p (t h) c"), k_tok.rearrange("p t h c -> p (t h) c"), over(rk, NOPE), ALU.mult)
            V.tensor_tensor(krh, kr_rot.unsqueeze(2).to_broadcast([P, TT, H, ROPE]),
                            rk.rearrange("p (t h) -> p t h", t=TT).unsqueeze(3).to_broadcast([P, TT, H, ROPE]),
                            ALU.mult).then_inc(k_ready, 1)
            for i in range(6):
                t, ch = i // 3, i % 3
                dve.wait_ge(qmm_done, i + 1)
                V.tensor_copy(q_tok[:, t, ch * HALF:(ch + 1) * HALF], bank[i % 4][:, :]).then_inc(q_evac, 1)
            dve.wait_ge(q_evac, 6)
            for t in range(TT):
                sq = sq_tmp[:, 0:H * QK].rearrange("p (h c) -> p h c", h=H)
                link(V.tensor_tensor(sq, q_h[:, t, :, :], q_h[:, t, :, :], ALU.mult))
                ins = V.tensor_reduce(ss_h[:, 1, t * H:(t + 1) * H], sq, AX_X, ALU.add)
                if t == 0:
                    link(ins)
            ins.then_inc(qss_ready, 1)
            dve.wait_ge(qrms_ready, 1)
            link(V.reciprocal(r_h[:, 1, :], r_h[:, 1, :]))
            q_all = q_tok.rearrange("p t (h c) -> p (t h) c", h=H)
            link(V.tensor_tensor(q_all, q_all, over(r_h[:, 1, :], QK), ALU.mult))
            q_r = q_h[:, :, :, NOPE:QK]
            link(V.tensor_tensor(q_r, q_r, qk_gr[:, 1, :].unsqueeze(1).unsqueeze(1).to_broadcast([P, TT, H, ROPE]), ALU.mult))
            rotate(qrr, q_r, (P, TT, H, HR), rot_tmq)
            V.memset(ang_k[:, 0, 0:1], 0.0).then_inc(q_ready, 1)
            for n in range(0, 16, 2):
                dve.wait_ge(hd_tr, n + 1)
                dst, rot, g = head_block(n)
                if rot:
                    V.tensor_copy(dst, bank[n % 8][0:ROPE, :].rearrange("p (h q) -> p h q", h=4)).then_inc(hd_dve, 1)
                else:
                    V.tensor_scalar(dst, bank[n % 8][:, :].rearrange("p (h q) -> p h q", h=4), g, None, ALU.mult).then_inc(hd_dve, 1)
            scale = float(QK) ** -0.5
            for n in range(6):
                dve.wait_ge(sc_done, n + 1)
                if n < 2:
                    dst, w, mk = sc0[:, 4 * n:4 * n + 4, :], 4, mask[:, S - P:S]
                else:
                    dst, w, mk = sc1[:, 2 * (n - 2):2 * (n - 2) + 2, :], 2, mask[:, 0:S]
                nk = HALF // w
                ins = V.scalar_tensor_tensor(out=dst, in0=bank[n][:, :].rearrange("p (h k) -> p h k", h=w), scalar=scale,
                                             in1=mk.unsqueeze(1).to_broadcast([P, w, nk]), op0=ALU.mult, op1=ALU.add)
                if n in (1, 5):
                    t = n // 5
                    link(ins)
                    link(V.tensor_reduce(smax[:, t, :], sc0 if t == 0 else sc1, AX_X, ALU.max))
                    V.tensor_scalar(smax[:, t, :], smax[:, t, :], -1.0, None, ALU.mult).then_inc(smax_ready, 1)
            for t in range(TT):
                dve.wait_ge(exp_done, (t + 1) * H)
                link(V.reciprocal(sinv[:, t, :], ssum[:, t, :]))
                s = sc0 if t == 0 else sc1
                V.tensor_tensor(s, s, over(sinv[:, t, :], (t + 1) * P), ALU.mult).then_inc(p_ready, 1)
            for n in range(0, 6, 2):
                dve.wait_ge(ptr_done, n + 1)
                V.tensor_copy(prob_block(n), bank[prob_bank(n)][:, :].rearrange("p (a q) -> p a q", a=4)).then_inc(pT_dve, 1)
            for n in range(0, 4, 2):
                dve.wait_ge(o_done, n + 1)
                t, hg = n // 2, n % 2
                V.tensor_copy(oT[:, 4 * hg:4 * hg + 4, t * P:(t + 1) * P],
                              bank[4 + n][:, :].rearrange("p (h q) -> p h q", h=4)).then_inc(o_dve, 1)
            for j in range(4):
                t, hf = j // 2, j % 2
                dve.wait_ge(wo_done, j + 1)
                V.tensor_tensor(h[:, t, hf * HALF:(hf + 1) * HALF], bank[j][:, :], h[:, t, hf * HALF:(hf + 1) * HALF],
                                ALU.add).then_inc(h_ready[3], 1)

            experts(1)


_INS = ["x", "positions", "a_norm_g", "a_pw1_w", "a_pw1_b", "a_dw_w", "a_dw_b", "a_ln_g", "a_ln_b", "a_pw2_w", "a_pw2_b",
        "kv_norm_g", "w_dkv", "kv_latent_g", "w_kr", "w_ukv", "k_norm_g", "b_norm_g", "w_dq", "q_latent_g", "w_uq",
        "q_norm_g", "w_o", "ffn_norm_g", "w_group", "b_group", "w_router", "b_router", "w_gate_up", "w_down"]


def kernel(**inputs):
    import numpy as _np
    import concourse.bacc as _bacc
    from concourse import mybir as _mybir
    from concourse.bass_utils import run_bass_kernel_spmd as _run

    nc = _bacc.Bacc("TRN2", target_bir_lowering=False, num_devices=1)
    arrays, args = {}, {}

    def declare(name, a):
        arrays[f"in_{name}_dram"] = a
        args[name] = nc.dram_tensor(f"in_{name}_dram", a.shape, _mybir.dt.from_np(a.dtype), kind="ExternalInput").ap()

    for name in _INS:
        declare(name, _np.ascontiguousarray(inputs[name]))
    rope = args["w_kr"].shape[1]
    inv = _np.float32(ROPE_THETA) ** (-_np.arange(0, rope, 2, dtype=_np.float32) / _np.float32(rope))
    declare("inv_freq", inv.astype(_np.float32).reshape(1, rope // 2))
    shape = inputs["x"].shape
    out = nc.dram_tensor("out_0_dram", shape, F32, kind="ExternalOutput").ap()
    trunk_kernel(nc, args, out)
    r = _run(nc, [arrays], core_ids=[0])
    return r.results[0]["out_0_dram"]
```

```python
from contextlib import ExitStack

import numpy as np

import concourse.bass as bass
from concourse import mybir

ALU = mybir.AluOpType
ACT = mybir.ActivationFunctionType
F32 = mybir.dt.float32
F32R = mybir.dt.float32r
I32 = mybir.dt.int32
AX_X = mybir.AxisListType.X

P = 128
EPS = 1e-6
NEG = 1e30
CAP = 64
PAIR = 2 * CAP
ROPE_THETA = 10000.0
CHUNK = 64
GROUPS = 4
SPLIT = 4


def trunk_kernel(nc: bass.Bass, a, out):
    _, S, D = a["x"].shape
    L, NE, _, FF2 = a["w_gate_up"].shape
    F = FF2 // 2
    TT = S // P
    KD = D // P
    KF = F // P
    CW = a["a_dw_w"].shape[1]
    PAD = CW - 1
    RKV = a["w_dkv"].shape[1]
    RQ = a["w_dq"].shape[2]
    ROPE = a["w_kr"].shape[1]
    HR = ROPE // 2
    QK = a["k_norm_g"].shape[0]
    NOPE = QK - ROPE
    H = a["w_uq"].shape[2] // QK
    DV = a["w_o"].shape[1] // H
    EG = NE // GROUPS
    NR = GROUPS + NE
    PASSES = -(-S // CAP)
    PAIRS = NE // 2
    HALF = 512
    assert TT == 2 and D == 2 * HALF and NOPE == P and DV == P and PAIR == P and KF * P == F and NE == 32

    with ExitStack() as ctx:
        def sb(name, shape, dt=F32):
            return ctx.enter_context(nc.sbuf_tensor(name, shape, dt))

        def sem(name):
            return ctx.enter_context(nc.semaphore(name))

        bank = [ctx.enter_context(nc.psum_tensor(f"bank{i}", [P, HALF], F32)) for i in range(8)]

        UNIT = 4 * D
        ring = sb("ring", [P, 6 * UNIT])
        raw = ring[:, :].rearrange("p (c n) -> p c n", n=D)
        unit_sb = [ring[:, u * UNIT:(u + 1) * UNIT].rearrange("p (k c) -> p k c", k=4) for u in range(6)]
        pw1_sb = [ring[:, u * UNIT:(u + 1) * UNIT].rearrange("p (k c) -> p k c", k=KD) for u in range(4)]
        pw2_sb = ring[:, 4 * UNIT:6 * UNIT].rearrange("p (k c) -> p k c", k=KD)
        o1 = KD * (RKV + ROPE)
        o2 = o1 + KD * RQ
        o3 = o2 + (RQ // P) * H * QK
        w_dkvr_sb = ring[:, 0:o1].rearrange("p (k c) -> p k c", k=KD)
        w_dq_sb = ring[:, o1:o2].rearrange("p (k c) -> p k c", k=KD)
        w_uq_sb = ring[:, o2:o3].rearrange("p (k c) -> p k c", k=RQ // P)
        w_ukv_sb = ring[:, 3 * UNIT:4 * UNIT].rearrange("p (k c) -> p k c", k=RKV // P)
        w_o_sb = ring[:, 4 * UNIT:6 * UNIT].rearrange("p (k c) -> p k c", k=H)
        assert o3 <= 3 * UNIT

        h = sb("h", [P, TT, D])
        xn = sb("xn", [P, TT, D])
        xT = sb("xT", [P, KD, S])
        NC_ = PASSES * NE + 2

        ident = sb("ident", [P, P])
        upto = sb("upto", [P, P])
        ones = sb("ones", [P, P])
        both = sb("both", [P, CAP])
        mean_w = sb("mean_w", [P, P])
        eps_c = sb("eps_c", [P, 1])
        rows = sb("rows", [P, P])
        cols = sb("cols", [P, P])
        dwT = sb("dwT", [P, KD, CW])
        iota_i = sb("iota_i", [P, CAP], I32)
        iota = sb("iota", [P, CAP])
        iota_m = sb("iota_m", [P, CAP])
        wr = sb("wr", [P, L, KD, NR])
        br = sb("br", [P, L, NR])
        qk_gr = sb("qk_gr", [P, 2, ROPE])
        mask = sb("mask", [P, S])
        inv_freq = sb("inv_freq", [P, HR])
        pos_i = sb("pos_i", [P, TT], I32)
        pos_f = sb("pos_f", [P, TT])
        ang = sb("ang", [P, TT, HR])
        ang_k = sb("ang_k", [P, TT, HR])
        cos = sb("cos", [P, TT, HR])
        sin = sb("sin", [P, TT, HR])
        ss = sb("ss", [P, 4])
        rms = sb("rms", [P, 4])
        rr = sb("rr", [P, 4])
        lg = sb("lg", [P, TT, NR])
        gmx = sb("gmx", [P, TT])
        gex = sb("gex", [P, TT, GROUPS])
        gsm = sb("gsm", [P, TT])
        gw = sb("gw", [P, TT])
        geq = sb("geq", [P, TT, GROUPS])
        gix = sb("gix", [P, TT])
        em = sb("em", [P, TT, NE])
        eeq = sb("eeq", [P, TT, NE])
        oh1 = sb("oh1", [P, TT, NE])
        oh2 = sb("oh2", [P, TT, NE])
        mx1 = sb("mx1", [P, TT])
        mx2 = sb("mx2", [P, TT])
        eix = sb("eix", [P, TT])
        w1 = sb("w1", [P, TT])
        w2 = sb("w2", [P, TT])
        picked = sb("picked", [P, TT, NE])
        slot = sb("slot", [P, TT, NC_])
        gate = sb("gate", [P, TT, NC_])
        cmx = sb("cmx", [P, 4])
        npairs_i = sb("npairs_i", [P, 1], I32)
        ss_kr = sb("ss_kr", [P, TT])
        ss_h = sb("ss_h", [P, 2, TT * H])
        r_h = sb("r_h", [P, 2, TT * H])
        smax = sb("smax", [P, TT, H])
        ssum = sb("ssum", [P, TT, H])
        sinv = sb("sinv", [P, TT, H])


        with ExitStack() as dense:
            def dense_sb(name, shape, dt=F32):
                return dense.enter_context(nc.sbuf_tensor(name, shape, dt))

            xT2 = dense_sb("xT2", [P, KD, S])
            arena = dense_sb("arena", [P, 16640])
        with ExitStack() as sparse:
            def moe_sb(name, shape, dt=F32):
                return sparse.enter_context(nc.sbuf_tensor(name, shape, dt))

            x_hi, x_lo = moe_sb("x_hi", [P, TT, D], F32R), moe_sb("x_lo", [P, TT, D], F32R)
            w_hi, w_lo = moe_sb("w_hi", [P, SPLIT, D], F32R), moe_sb("w_lo", [P, SPLIT, D], F32R)
            xs = moe_sb("xs", [P, 2, KD, PAIR], F32R)
            hs = moe_sb("hs", [P, 2, KF, PAIR], F32R)
            pick = moe_sb("pick", [P, TT, PAIR], F32R)
            hid = moe_sb("hid", [P, 2, KF, CAP])
            sil = moe_sb("sil", [P, KF, CAP])
            pw = moe_sb("pw", [P, 2, TT, PAIR])
            pwT = moe_sb("pwT", [P, 2, S])
            gain = moe_sb("gain", [P, D])
        xg = xn[:, 0, :]
        u_rows = xn[:, 1, :]
        y_rows = xT[:, :, :].rearrange("p k c -> p (k c)").rearrange("p (s d) -> p s d", s=2)

        def view(offset, *shape):
            n = int(np.prod(shape))
            v = arena[:, offset:offset + n]
            if len(shape) == 1:
                return v
            if len(shape) == 2:
                return v.rearrange("p (a b) -> p a b", b=shape[1])
            return v.rearrange("p (a b c) -> p a b c", b=shape[1], c=shape[2])

        u_sb = view(0, KD, PAD + S)
        cv = view(2560, KD, S)
        sg = view(4608, 2, S)
        std_t = view(5120, S)
        rstd_t = view(5376, S)
        dw_rows = view(6144, D)
        pw2_b_row = view(7168, D)
        q_tok = view(0, TT, H * QK)
        q_h = q_tok.rearrange("p t (h c) -> p t h c", h=H)
        k_tok = view(3072, TT, H, NOPE)
        krh = view(5120, TT, H, ROPE)
        qrr = view(6144, TT, H, ROPE)
        v_tok = view(7168, TT, H, DV)
        kTn = view(9216, H, S)
        qTn = view(11264, H, S)
        kTr = view(13312, H, S)
        ckvT = view(15360, RKV // P, S)
        cqT = view(15872, RQ // P, S)
        qTr = xT2
        sc0 = view(0, H, P)
        sc1 = view(1024, H, S)
        pT0 = view(3072, H, P)
        pT1 = view(4096, H, TT, P)
        oT = xT
        cn = xn[:, 0, :]
        ckv_n = xn[:, 0, 0:TT * RKV].rearrange("p (t c) -> p t c", t=TT)
        cq_n = xn[:, 1, 0:TT * RQ].rearrange("p (t c) -> p t c", t=TT)
        kr_raw = xn[:, 0, 512:512 + TT * ROPE].rearrange("p (t c) -> p t c", t=TT)
        kr_rot = xn[:, 0, 640:640 + TT * ROPE].rearrange("p (t c) -> p t c", t=TT)
        sq_tmp = xT2[:, 0:6, :].rearrange("p a b -> p (a b)")
        rot_tmp = [view(13312 + i * 512, TT, H, HR) for i in range(4)]
        rot_tmq = [xT2[:, 2 * i:2 * i + 2, :].rearrange("p a b -> p (a b)").rearrange("p (t h c) -> p t h c", t=TT, h=H)
                   for i in range(4)]

        row_at, spots = 0, {}
        row_loads = []
        for name, ap, n in (
            ("a_norm_g", a["a_norm_g"][0], KD), ("pw1_b", a["a_pw1_b"][0], 2 * KD), ("dw_b", a["a_dw_b"][0], KD),
            ("ln_g", a["a_ln_g"][0], KD), ("ln_b", a["a_ln_b"][0], KD), ("kv_norm_g", a["kv_norm_g"], KD),
            ("b_norm_g", a["b_norm_g"][0], KD), ("ffn_norm_g0", a["ffn_norm_g"][0], KD), ("ffn_norm_g1", a["ffn_norm_g"][1], KD),
            ("kv_latent_g", a["kv_latent_g"], RKV // P), ("q_latent_g", a["q_latent_g"][0], RQ // P),
            ("k_gn", a["k_norm_g"][0:NOPE], 1), ("q_gn", a["q_norm_g"][0][0:NOPE], 1),
        ):
            spots[name] = row_at
            row_loads.append((row_at, n, ap.rearrange("(k p) -> k p", p=P)))
            row_at += n
        N_ROWS = row_at

        def col(name, k=0, n=1):
            return cols[:, spots[name] + k:spots[name] + k + n]

        def over(ap, n):
            return ap.unsqueeze(2).to_broadcast([P, ap.shape[1], n])

        def sc_junk(i, n):
            return arena[:, 9216 + i * HALF:9216 + i * HALF + n]

        def head_block(n):
            kind, t, hg = n // 4, (n % 4) // 2, n % 2
            dst = (kTn, kTr, qTn, qTr)[kind]
            rot = kind % 2 == 1
            return (dst[0:ROPE if rot else P, 4 * hg:4 * hg + 4, t * P:(t + 1) * P], rot,
                    col("k_gn") if kind == 0 else col("q_gn"))

        def prob_bank(n):
            return (6, 7, 0, 1, 2, 3)[n]

        def prob_block(n):
            if n < 2:
                return pT0[:, 4 * n:4 * n + 4, :]
            return pT1[:, 2 * (n - 2):2 * (n - 2) + 2, :, :].rearrange("p h k q -> p (h k) q")

        x_in, w_pw1 = sem("x_in"), [sem(f"w_pw1_{i}") for i in range(4)]
        w_pw2 = sem("w_pw2")
        rows_in, small_in, small2_in = sem("rows_in"), sem("small_in"), sem("small2_in")
        zeroed, const_ready, const_f = sem("zeroed"), sem("const_ready"), sem("const_f")
        cols_tr, cols_ready = sem("cols_tr"), sem("cols_ready")
        dve_step, act_step = sem("dve_step"), sem("act_step")
        ssq, rms_ready, xn_ready, tr_done, xT_ready = sem("ssq"), sem("rms_ready"), sem("xn_ready"), sem("tr_done"), sem("xT_ready")
        h_ready = [sem(f"h_ready{i}") for i in range(5)]
        xT2_ready = sem("xT2_ready")
        pw1_done, sg_ready, u_ready, u_zero = sem("pw1_done"), sem("sg_ready"), sem("u_ready"), sem("u_zero")
        conv_done, mean_done, diff_ready = sem("conv_done"), sem("mean_done"), sem("diff_ready")
        sq_ready, var_done, lstd_ready, dn_ready = sem("sq_ready"), sem("var_done"), sem("lstd_ready"), sem("dn_ready")
        c_ready, pw2_done, hb_ready = sem("c_ready"), sem("pw2_done"), sem("hb_ready")
        E = []
        for l in range(L):
            E.append({n: sem(f"{n}_{l}") for n in (
                "gain_in", "xh_ready", "xsplit_ready", "logits_done", "gexp_in", "gexp_ready", "eexp_in", "eexp_ready", "mask_ready",
                "pos_done", "npairs_ready", "unit_in0", "unit_in1", "unit_in2", "unit_in3", "unit_in4", "unit_in5",
                "chunk_free", "hi_ready", "lo_ready", "pick_ready", "pw_ready", "g_done", "xg_ready", "xtr_done", "xhi_ready",
                "xs_ready", "u_ready", "sum_done", "silu_done", "h_prod", "h_hi", "hs_ready", "y_ready",
                "pwtr_done", "pwT_ready", "s_done", "s_added")})
        w_c, w_uq, w_ukv, w_o = sem("w_c"), sem("w_uq"), sem("w_ukv"), sem("w_o")
        ang_ready, trig = sem("ang_ready"), sem("trig")
        c_done, csq, crms_ready, cn_ready = sem("c_done"), sem("csq"), sem("crms_ready"), sem("cn_ready")
        ctr_done, cT_ready = sem("ctr_done"), sem("cT_ready")
        kvmm_done, kv_evac, qmm_done, q_evac = sem("kvmm_done"), sem("kv_evac"), sem("qmm_done"), sem("q_evac")
        kss_ready, krms_ready, k_ready = sem("kss_ready"), sem("krms_ready"), sem("k_ready")
        qss_ready, qrms_ready, q_ready = sem("qss_ready"), sem("qrms_ready"), sem("q_ready")
        hd_tr, hd_dve, hd_act = sem("hd_tr"), sem("hd_dve"), sem("hd_act")
        sc_done, smax_ready, exp_done, p_ready = sem("sc_done"), sem("smax_ready"), sem("exp_done"), sem("p_ready")
        ptr_done, pT_dve, pT_act = sem("ptr_done"), sem("pT_dve"), sem("pT_act")
        o_done, o_dve, o_act, wo_done = sem("o_done"), sem("o_dve"), sem("o_act"), sem("wo_done")
        out_done = sem("out_done")

        block = ctx.enter_context(nc.Block())

        @block.sync
        def _(sp):
            sp.dma_start(h[:, :, :], a["x"][0].rearrange("(t p) d -> p t d", p=P)).then_inc(x_in, 16)
            pw1 = a["a_pw1_w"][0].rearrange("(k p) c -> p k c", p=P)
            for i, c0 in enumerate((0, D, HALF, D + HALF)):
                sp.dma_start(pw1_sb[i], pw1[:, :, c0:c0 + HALF]).then_inc(w_pw1[i], 16)
            sp.dma_start(pw2_sb, a["a_pw2_w"][0].rearrange("(k p) c -> p k c", p=P)).then_inc(w_pw2, 16)

            def unit_dma(l, u, ex):
                src = a["w_gate_up"][l] if u % 3 < 2 else a["w_down"][l]
                r0 = HALF if u % 3 == 1 else 0
                src = src[bass.ds(ex, 1), r0:r0 + HALF, :].rearrange("e (k p) c -> (e p) k c", p=P)
                sp.dma_start(unit_sb[u], src).then_inc(E[l][f"unit_in{u}"], 16)

            def experts(l, first):
                e = E[l]
                for u in range(6):
                    first(u)
                    unit_dma(l, u, u // 3)
                sp.wait_ge(e["npairs_ready"], 1)
                n_pairs = sp.value_load(npairs_i[0:1, 0:1], min_val=PAIRS, max_val=PAIRS * PASSES)
                with sp.Fori(1, n_pairs) as it:
                    ex = (it % PAIRS) * 2
                    for u in range(6):
                        sp.wait_ge(e["lo_ready"], 24 * it - (24 - 4 * (u + 1)))
                        unit_dma(l, u, ex + u // 3)
                return n_pairs

            def first_after_conv(u):
                if u == 0:
                    sp.wait_ge(pw1_done, 4)
                if u == 2:
                    sp.wait_ge(pw1_done, 8)
                if u == 4:
                    sp.wait_ge(pw2_done, 4)

            n0 = experts(0, first_after_conv)
            sp.wait_ge(E[0]["lo_ready"], 24 * n0)
            sp.dma_start(w_dkvr_sb[:, :, 0:RKV], a["w_dkv"].rearrange("(k p) c -> p k c", p=P)).then_inc(w_c, 16)
            sp.dma_start(w_dkvr_sb[:, :, RKV:RKV + ROPE], a["w_kr"].rearrange("(k p) c -> p k c", p=P)).then_inc(w_c, 16)
            sp.dma_start(w_dq_sb, a["w_dq"][0].rearrange("(k p) c -> p k c", p=P)).then_inc(w_c, 16)
            sp.dma_start(w_uq_sb, a["w_uq"][0].rearrange("(k p) c -> p k c", p=P)).then_inc(w_uq, 16)
            sp.dma_start(w_ukv_sb, a["w_ukv"].rearrange("(k p) c -> p k c", p=P)).then_inc(w_ukv, 16)
            sp.dma_start(w_o_sb, a["w_o"][0].rearrange("(k p) c -> p k c", p=P)).then_inc(w_o, 16)

            def first_after_attention(u):
                if u == 0:
                    sp.wait_ge(qmm_done, 6)
                if u == 3:
                    sp.wait_ge(kvmm_done, 8)
                if u == 4:
                    sp.wait_ge(wo_done, 4)

            experts(1, first_after_attention)
            out_t = out[0].rearrange("(t p) d -> p t d", p=P)
            for j in range(4):
                tt, hf = j // 2, j % 2
                sp.wait_ge(h_ready[4], j + 1)
                sp.dma_start(out_t[:, tt, hf * HALF:(hf + 1) * HALF], h[:, tt, hf * HALF:(hf + 1) * HALF]).then_inc(out_done, 16)
            sp.wait_ge(out_done, 64)

        @block.gpsimd
        def _(pool):
            nc.gpsimd.memset(ident[:, :], 0.0).then_inc(zeroed, 1)
            nc.gpsimd.memset(upto[:, :], 1.0).then_inc(zeroed, 1)
            nc.gpsimd.memset(mask[:, :], 0.0).then_inc(zeroed, 1)
            nc.gpsimd.memset(both[:, :], 0.0).then_inc(zeroed, 1)
            pool.wait_ge(zeroed, 4)
            nc.gpsimd.affine_select(out=ident[:, :], in_=ident[:, :], compare_op=ALU.not_equal, fill=1.0, base=0,
                                    pattern=[[-1, P]], channel_multiplier=1).then_inc(const_ready, 1)
            nc.gpsimd.affine_select(out=upto[:, :], in_=upto[:, :], compare_op=ALU.is_ge, fill=0.0, base=0,
                                    pattern=[[1, P]], channel_multiplier=-1).then_inc(const_ready, 1)
            nc.gpsimd.memset(mask[0:CHUNK, S - CHUNK:S], -NEG).then_inc(const_ready, 1)
            nc.gpsimd.memset(ones[:, :], 1.0).then_inc(const_ready, 1)
            nc.gpsimd.memset(mean_w[:, :], 1.0 / D).then_inc(const_ready, 1)
            nc.gpsimd.memset(eps_c[:, :], EPS).then_inc(const_ready, 1)
            nc.gpsimd.memset(slot[:, :, :], -1.0).then_inc(const_ready, 1)
            nc.gpsimd.memset(gate[:, :, :], 0.0).then_inc(const_ready, 1)
            nc.gpsimd.iota(iota_i[:, :], pattern=[[1, CAP]], base=0, channel_multiplier=0).then_inc(const_ready, 1)
            for half in range(2):
                nc.gpsimd.affine_select(out=both[:, :], in_=both[:, :], compare_op=ALU.not_equal, fill=1.0, base=-half * CAP,
                                        pattern=[[-1, CAP]], channel_multiplier=1).then_inc(const_ready, 1)
                pool.wait_ge(const_ready, 10 + half)
            nc.gpsimd.memset(u_sb[:, :, 0:PAD], 0.0).then_inc(u_zero, 1)
            pool.wait_ge(small_in, 16)
            pool.wait_ge(xn_ready, 2)
            for t in range(TT):
                nc.gpsimd.tensor_tensor(h[:, t, :], h[:, t, :], pw2_b_row, ALU.add).then_inc(hb_ready, 1)
            for l in range(L):
                pool.wait_ge(h_ready[1 + 2 * l], 4)
                nc.gpsimd.dma_start(gain[:, :], a["ffn_norm_g"][l:l + 1].to_broadcast([P, D])).then_inc(E[l]["gain_in"], 16)

        @block.scalar
        def _(act):
            act_n = [0]

            def link(ins):
                act_n[0] += 1
                ins.then_inc(act_step, 1)
                act.wait_ge(act_step, act_n[0])

            for r, n, ap in row_loads:
                act.dma_start(rows[r:r + n, :], ap).then_inc(rows_in, 16)
            act.dma_start(dw_rows[0:CW, :], a["a_dw_w"][0]).then_inc(rows_in, 16)
            act.dma_start(pw2_b_row, a["a_pw2_b"].to_broadcast([P, D])).then_inc(small_in, 16)
            for l in range(L):
                act.dma_start(wr[:, l, :, 0:GROUPS], a["w_group"][l].rearrange("(k p) g -> p k g", p=P)).then_inc(small2_in, 16)
                act.dma_start(wr[:, l, :, GROUPS:NR], a["w_router"][l].rearrange("(k p) g -> p k g", p=P)).then_inc(small2_in, 16)
                act.dma_start(br[:, l, 0:GROUPS], a["b_group"][l:l + 1].to_broadcast([P, GROUPS])).then_inc(small2_in, 16)
                act.dma_start(br[:, l, GROUPS:NR], a["b_router"][l:l + 1].to_broadcast([P, NE])).then_inc(small2_in, 16)
            act.dma_start(qk_gr[:, 0, :], a["k_norm_g"][NOPE:QK].unsqueeze(0).to_broadcast([P, ROPE])).then_inc(small2_in, 16)
            act.dma_start(qk_gr[:, 1, :], a["q_norm_g"][0:1, NOPE:QK].to_broadcast([P, ROPE])).then_inc(small2_in, 16)
            act.dma_start(inv_freq[:, :], a["inv_freq"].to_broadcast([P, HR])).then_inc(small2_in, 16)
            act.dma_start(pos_i[:, :], a["positions"][0].rearrange("(t p) -> p t", p=P), allow_slow_non_contiguous=True).then_inc(small2_in, 16)

            def norm(i):
                for t in range(TT):
                    if i == 0:
                        act.wait_ge(x_in, 16)
                        act.wait_ge(const_ready, 11)
                    else:
                        act.wait_ge(h_ready[i], 2 * t + 2)
                    nc.scalar.activation(xn[:, t, :], h[:, t, :], ACT.Square,
                                         accum_out=ss[:, t:t + 1]).then_inc(ssq, 1)
                act.wait_ge(ssq, 2 * i + 2)
                nc.scalar.activation(rms[:, 0:2], ss[:, 0:2], ACT.Sqrt, scale=1.0 / D, bias=eps_c[:, :]).then_inc(rms_ready, 1)

            norm(0)
            act.wait_ge(cols_ready, 1)
            for m in range(KD):
                act.wait_ge(pw1_done, m + 1)
                if m >= 2:
                    act.wait_ge(u_ready, m - 1)
                nc.scalar.activation(sg[:, m % 2, :], bank[4 + m % 4][:, S:2 * S], ACT.Sigmoid,
                                     bias=col("pw1_b", KD + m)).then_inc(sg_ready, 1)
            for m in range(KD):
                act.wait_ge(diff_ready, m + 1)
                nc.scalar.activation(xT[:, m, :], cv[:, m, :], ACT.Square).then_inc(sq_ready, 1)
            act.wait_ge(var_done, 1)
            nc.scalar.activation(std_t, bank[1][:, 0:S], ACT.Sqrt, bias=eps_c[:, :]).then_inc(lstd_ready, 1)
            for m in range(KD):
                act.wait_ge(dn_ready, m + 1)
                nc.scalar.activation(cv[:, m, :], cv[:, m, :], ACT.Silu, scale=col("ln_g", m), bias=col("ln_b", m)).then_inc(c_ready, 1)

            def experts(l):
                e = E[l]
                norm(1 + 2 * l)
                for t in range(TT):
                    act.wait_ge(xn_ready, 2 * (1 + 2 * l) + t + 1)
                    nc.scalar.copy(x_hi[:, t, :], xn[:, t, :]).then_inc(e["xh_ready"], 1)
                act.wait_ge(e["gexp_in"], 1)
                nc.scalar.activation(gex[:, :, :], gex[:, :, :], ACT.Exp).then_inc(e["gexp_ready"], 1)
                act.wait_ge(e["eexp_in"], 1)
                nc.scalar.activation(w2[:, :], w2[:, :], ACT.Exp).then_inc(e["eexp_ready"], 1)
                act.wait_ge(e["npairs_ready"], 1)
                n_pairs = act.value_load(npairs_i[0:1, 0:1], min_val=PAIRS, max_val=PAIRS * PASSES)

                def high(it, first, last):
                    for c in range(first, last):
                        if c % 4 == 0:
                            act.wait_ge(e[f"unit_in{c // 4}"], 16 * it + 16)
                        act.wait_ge(e["chunk_free"], 24 * it + c + 1)
                        nc.scalar.copy(w_hi[:, c % SPLIT, :], raw[:, c, :]).then_inc(e["hi_ready"], 1)

                def out_of(banks, dst, wait, n, done):
                    act.wait_ge(e[wait], n)
                    nc.scalar.copy(dst[:, 0:HALF], bank[banks][:, :])
                    nc.scalar.copy(dst[:, HALF:D], bank[banks + 1][:, :]).then_inc(e[done], 1)

                def silu(n):
                    act.wait_ge(e["sum_done"], n)
                    nc.scalar.activation(sil[:, :, :], bank[0][:, 0:KF * CAP].rearrange("p (k c) -> p k c", k=KF),
                                         ACT.Silu).then_inc(e["silu_done"], 1)

                def tokens_high(n):
                    act.wait_ge(e["xtr_done"], n)
                    for b in range(2):
                        ins = nc.scalar.copy(xs[:, :, 4 * b:4 * b + 4, 0:CAP].rearrange("p s k c -> p k s c"),
                                             bank[4 + b][:, :].rearrange("p (k s c) -> p k s c", k=4, s=2))
                    ins.then_inc(e["xhi_ready"], 1)

                out_of(4, xg, "g_done", 1, "xg_ready")
                tokens_high(1)
                with act.Fori(0, n_pairs) as it:
                    high(it, 0, 4)
                    out_of(2, y_rows[:, 1, :], "chunk_free", SPLIT + 24 * it, "y_ready")
                    high(it, 4, 11)
                    out_of(0, u_rows, "chunk_free", SPLIT + 24 * it + 8, "u_ready")
                    high(it, 11, 12)
                    silu(2 * it + 1)
                    high(it, 12, 16)
                    out_of(2, y_rows[:, 0, :], "chunk_free", SPLIT + 24 * it + 12, "y_ready")
                    high(it, 16, 23)
                    out_of(0, u_rows, "chunk_free", SPLIT + 24 * it + 20, "u_ready")
                    high(it, 23, 24)
                    out_of(4, xg, "g_done", it + 2, "xg_ready")
                    silu(2 * it + 2)
                    act.wait_ge(e["pwtr_done"], it + 1)
                    nc.scalar.copy(pwT[:, :, :].rearrange("p s t -> p (s t)"), bank[1][:, :]).then_inc(e["pwT_ready"], 1)
                    tokens_high(it + 2)
                out_of(2, y_rows[:, 1, :], "chunk_free", SPLIT + 24 * n_pairs, "y_ready")

            experts(0)

            norm(2)
            act.wait_ge(ang_ready, 1)
            nc.scalar.activation(sin[:, :, :], ang[:, :, :], ACT.Sin).then_inc(trig, 1)
            nc.scalar.activation(cos[:, :, :], ang[:, :, :], ACT.Sin, scale=0.5).then_inc(trig, 1)
            for b in range(4):
                act.wait_ge(xT_ready, 8 + b + 1)
                t, kh = b // 2, b % 2
                for j in range(4):
                    k = 4 * kh + j
                    ins = nc.scalar.activation(xT2[:, k, t * P:(t + 1) * P], bank[b][:, j * P:(j + 1) * P], ACT.Copy,
                                               scale=col("b_norm_g", k))
                ins.then_inc(xT2_ready, 1)
            for t in range(TT):
                act.wait_ge(c_done, t + 1)
                nc.scalar.activation(sc_junk(t, RKV), bank[4 + t][:, 0:RKV], ACT.Square, accum_out=ss[:, t:t + 1]).then_inc(csq, 1)
                nc.scalar.activation(sc_junk(2 + t, ROPE), bank[4 + t][:, RKV:RKV + ROPE], ACT.Square, accum_out=ss_kr[:, t:t + 1]).then_inc(csq, 1)
            for t in range(TT):
                act.wait_ge(c_done, 3 + t)
                nc.scalar.activation(sc_junk(4 + t, RQ), bank[6 + t][:, 0:RQ], ACT.Square, accum_out=ss[:, 2 + t:3 + t]).then_inc(csq, 1)
            act.wait_ge(csq, 6)
            nc.scalar.activation(rms[:, 0:2], ss[:, 0:2], ACT.Sqrt, scale=1.0 / RKV, bias=eps_c[:, :]).then_inc(crms_ready, 1)
            nc.scalar.activation(rms[:, 2:4], ss[:, 2:4], ACT.Sqrt, scale=1.0 / RQ, bias=eps_c[:, :]).then_inc(crms_ready, 1)
            for i in range(2 * 4):
                t, ch = i // 4, i % 4
                act.wait_ge(kvmm_done, i + 1)
                src = bank[4 + i % 4][:, :].rearrange("p (h w d) -> p h w d", h=2, w=2)
                nc.scalar.copy(k_tok[:, t, 2 * ch:2 * ch + 2, :], src[:, :, 0, :])
                nc.scalar.copy(v_tok[:, t, 2 * ch:2 * ch + 2, :], src[:, :, 1, :]).then_inc(kv_evac, 1)
            for i, (ready, got) in enumerate(((kss_ready, krms_ready), (qss_ready, qrms_ready))):
                act.wait_ge(ready, 1)
                nc.scalar.activation(r_h[:, i, :], ss_h[:, i, :], ACT.Sqrt, scale=1.0 / QK, bias=eps_c[:, :]).then_inc(got, 1)
            for n in range(1, 16, 2):
                act.wait_ge(hd_tr, n + 1)
                dst, rot, g = head_block(n)
                if rot:
                    nc.scalar.copy(dst, bank[n % 8][0:ROPE, :].rearrange("p (h q) -> p h q", h=4)).then_inc(hd_act, 1)
                else:
                    nc.scalar.activation(dst, bank[n % 8][:, :].rearrange("p (h q) -> p h q", h=4), ACT.Copy,
                                         scale=g).then_inc(hd_act, 1)
            for t in range(TT):
                act.wait_ge(smax_ready, t + 1)
                for hh in range(H):
                    s = (sc0 if t == 0 else sc1)[:, hh, :]
                    nc.scalar.activation(s, s, ACT.Exp, bias=smax[:, t, hh:hh + 1],
                                         accum_out=ssum[:, t, hh:hh + 1]).then_inc(exp_done, 1)
            for n in range(1, 6, 2):
                act.wait_ge(ptr_done, n + 1)
                nc.scalar.copy(prob_block(n), bank[prob_bank(n)][:, :].rearrange("p (a q) -> p a q", a=4)).then_inc(pT_act, 1)
            for n in range(1, 4, 2):
                act.wait_ge(o_done, n + 1)
                t, hg = n // 2, n % 2
                nc.scalar.copy(oT[:, 4 * hg:4 * hg + 4, t * P:(t + 1) * P],
                               bank[4 + n][:, :].rearrange("p (h q) -> p h q", h=4)).then_inc(o_act, 1)

            experts(1)

        @block.tensor
        def _(pe):
            pe.wait_ge(const_ready, 11)
            pe.wait_ge(rows_in, 16 * (len(row_loads) + 1))
            nc.tensor.transpose(bank[7][:, 0:N_ROWS], rows[0:N_ROWS, :], ident[0:N_ROWS, 0:N_ROWS])
            for m in range(KD):
                ins = nc.tensor.transpose(bank[7][:, P + m * CW:P + (m + 1) * CW], dw_rows[0:CW, m * P:(m + 1) * P],
                                          ident[0:CW, 0:CW])
            ins.then_inc(cols_tr, 1)

            def norm(i):
                for b in range(4):
                    t, kh = b // 2, b % 2
                    pe.wait_ge(xn_ready, 2 * i + t + 1)
                    for j in range(4):
                        k = 4 * kh + j
                        ins = nc.tensor.transpose(bank[b][:, j * P:(j + 1) * P], xn[:, t, k * P:(k + 1) * P], ident[:, :])
                    ins.then_inc(tr_done, 1)

            norm(0)
            pe.wait_ge(cols_ready, 1)
            pe.wait_ge(xT_ready, 4)
            for m in range(KD):
                if m % 4 == 0:
                    pe.wait_ge(w_pw1[2 * (m // 4)], 16)
                    pe.wait_ge(w_pw1[2 * (m // 4) + 1], 16)
                if m >= 4:
                    pe.wait_ge(u_ready, m - 3)
                for part in range(2):
                    for k in range(KD):
                        ins = nc.tensor.matmul(bank[4 + m % 4][:, part * S:(part + 1) * S],
                                               pw1_sb[2 * (m // 4) + part][:, k, (m % 4) * P:(m % 4 + 1) * P],
                                               xT[:, k, :], start=(k == 0), stop=(k == KD - 1))
                ins.then_inc(pw1_done, 1)
            for m in range(KD):
                pe.wait_ge(conv_done, m + 1)
                ins = nc.tensor.matmul(bank[0][:, 0:S], mean_w[:, :], cv[:, m, :], start=(m == 0), stop=(m == KD - 1))
            ins.then_inc(mean_done, 1)
            for m in range(KD):
                pe.wait_ge(sq_ready, m + 1)
                ins = nc.tensor.matmul(bank[1][:, 0:S], mean_w[:, :], xT[:, m, :], start=(m == 0), stop=(m == KD - 1))
            ins.then_inc(var_done, 1)
            pe.wait_ge(w_pw2, 16)
            pe.wait_ge(u_ready, KD)
            for k in range(KD):
                pe.wait_ge(c_ready, k + 1)
                for j in range(4):
                    t, hf = j // 2, j % 2
                    ins = nc.tensor.matmul(bank[4 + j][:, :], cv[:, k, t * P:(t + 1) * P],
                                           pw2_sb[:, k, hf * HALF:(hf + 1) * HALF], start=(k == 0), stop=(k == KD - 1))
                    if k == KD - 1:
                        ins.then_inc(pw2_done, 1)

            def experts(l):
                e = E[l]
                norm(1 + 2 * l)
                if l == 0:
                    pe.wait_ge(small2_in, 16 * (4 * L + 4))
                pe.wait_ge(xT_ready, 4 * (2 + 2 * l))
                for t in range(TT):
                    for k in range(KD):
                        ins = nc.tensor.matmul(bank[4][:, t * CAP:t * CAP + NR], xT[:, k, t * P:(t + 1) * P], wr[:, l, k, :],
                                               start=(k == 0), stop=(k == KD - 1))
                ins.then_inc(e["logits_done"], 1)
                pe.wait_ge(e["mask_ready"], 1)
                nc.tensor.matmul(bank[5][:, 0:NE], upto[:, :], picked[:, 0, :], start=True, stop=True)
                nc.tensor.matmul(bank[5][:, NE:2 * NE], ones[:, :], picked[:, 0, :], start=True, stop=False)
                nc.tensor.matmul(bank[5][:, NE:2 * NE], upto[:, :], picked[:, 1, :], start=False, stop=True)
                nc.tensor.matmul(bank[5][:, 2 * NE:3 * NE], ones[:, :], picked[:, 0, :], start=True, stop=False)
                nc.tensor.matmul(bank[5][:, 2 * NE:3 * NE], ones[:, :], picked[:, 1, :], start=False, stop=True).then_inc(e["pos_done"], 1)

                def gather(n):
                    pe.wait_ge(e["pick_ready"], n)
                    for b in range(2):
                        for i, (t, part) in enumerate(((0, x_hi), (0, x_lo), (1, x_hi), (1, x_lo))):
                            ins = nc.tensor.matmul(bank[4 + b][:, :], pick[:, t, :], part[:, t, b * HALF:(b + 1) * HALF],
                                                   start=(i == 0), stop=(i == 3))
                    ins.then_inc(e["g_done"], 1)

                def tokens_across(n):
                    pe.wait_ge(e["xg_ready"], n)
                    for k in range(KD):
                        ins = nc.tensor.transpose(bank[4 + k // 4][:, (k % 4) * P:(k % 4 + 1) * P], xg[:, k * P:(k + 1) * P],
                                                  ident[:, :])
                    ins.then_inc(e["xtr_done"], 1)

                def rows_times(it, stationary, first, last, b0):
                    for c in range(first, last):
                        pe.wait_ge(e["lo_ready"], 24 * it + c + 1)
                        for part in (w_hi, w_lo):
                            for b in range(2):
                                ins = nc.tensor.matmul(bank[b0 + b][:, :], stationary[:, c - first, :],
                                                       part[:, c % SPLIT, b * HALF:(b + 1) * HALF],
                                                       start=(c == first and part is w_hi), stop=(c == last - 1 and part is w_lo))
                        ins.then_inc(e["chunk_free"], 1)

                def add_parts(n):
                    pe.wait_ge(e["u_ready"], n)
                    for m in range(2 * KF):
                        ins = nc.tensor.matmul(bank[0][:, m * CAP:(m + 1) * CAP], u_rows[:, m * P:(m + 1) * P], both[:, :],
                                               start=True, stop=True)
                    ins.then_inc(e["sum_done"], 1)

                def scatter(j, it, added, base):
                    t, hf = j // 2, j % 2
                    if j == 0:
                        pe.wait_ge(e["y_ready"], 2 * it + 2)
                        pe.wait_ge(e["pwT_ready"], it + 1)
                    if j >= 2:
                        pe.wait_ge(added, base + j - 1)
                    for s in range(2):
                        ins = nc.tensor.matmul(bank[6 + j % 2][:, :], pwT[:, s, t * P:(t + 1) * P],
                                               y_rows[:, s, hf * HALF:(hf + 1) * HALF], start=(s == 0), stop=(s == 1))
                    ins.then_inc(e["s_done"], 1)

                def gates_across(n):
                    pe.wait_ge(e["pw_ready"], n)
                    for s in range(2):
                        for t in range(TT):
                            ins = nc.tensor.transpose(bank[1][:, (2 * s + t) * P:(2 * s + t + 1) * P], pw[:, s, t, :], ident[:, :])
                    ins.then_inc(e["pwtr_done"], 1)

                pe.wait_ge(e["xsplit_ready"], 2)
                gather(1)
                tokens_across(1)
                pe.wait_ge(e["npairs_ready"], 1)
                n_pairs = pe.value_load(npairs_i[0:1, 0:1], min_val=PAIRS, max_val=PAIRS * PASSES)
                with pe.Fori(0, n_pairs) as it:
                    pe.wait_ge(e["xs_ready"], it + 1)
                    pe.wait_ge(e["pwT_ready"], it + 1)
                    rows_times(it, xs[:, 0, :, :], 0, 8, 0)
                    scatter(0, it, e["s_added"], 4 * it)
                    scatter(1, it, e["s_added"], 4 * it)
                    add_parts(2 * it + 1)
                    scatter(2, it, e["s_added"], 4 * it)
                    scatter(3, it, e["s_added"], 4 * it)
                    pe.wait_ge(e["hs_ready"], 2 * it + 1)
                    rows_times(it, hs[:, 0, :, :], 8, 12, 2)
                    rows_times(it, xs[:, 1, :, :], 12, 20, 0)
                    gather(it + 2)
                    add_parts(2 * it + 2)
                    gates_across(it + 1)
                    tokens_across(it + 2)
                    pe.wait_ge(e["hs_ready"], 2 * it + 2)
                    pe.wait_ge(e["y_ready"], 2 * it + 3)
                    rows_times(it, hs[:, 1, :, :], 20, 24, 2)
                for j in range(4):
                    scatter(j, n_pairs, h_ready[2 + 2 * l], 0)

            experts(0)

            norm(2)
            pe.wait_ge(w_c, 48)
            pe.wait_ge(xT_ready, 12)
            for t in range(TT):
                for k in range(KD):
                    ins = nc.tensor.matmul(bank[4 + t][:, 0:RKV + ROPE], xT[:, k, t * P:(t + 1) * P], w_dkvr_sb[:, k, :],
                                           start=(k == 0), stop=(k == KD - 1))
                ins.then_inc(c_done, 1)
            pe.wait_ge(xT2_ready, 4)
            for t in range(TT):
                for k in range(KD):
                    ins = nc.tensor.matmul(bank[6 + t][:, 0:RQ], xT2[:, k, t * P:(t + 1) * P], w_dq_sb[:, k, :],
                                           start=(k == 0), stop=(k == KD - 1))
                ins.then_inc(c_done, 1)
            pe.wait_ge(cn_ready, 4)
            for src, n, b0 in ((ckv_n, RKV // P, 0), (cq_n, RQ // P, 1)):
                for k in range(n):
                    for t in range(TT):
                        ins = nc.tensor.transpose(bank[b0 + k // 2][:, (2 * (k % 2) + t) * P:(2 * (k % 2) + t + 1) * P],
                                                  src[:, t, k * P:(k + 1) * P], ident[:, :])
                    if k % 2 == 1 or k == n - 1:
                        ins.then_inc(ctr_done, 1)
            pe.wait_ge(w_ukv, 16)
            pe.wait_ge(cT_ready, 3)
            for i in range(8):
                t, ch = i // 4, i % 4
                if i >= 4:
                    pe.wait_ge(kv_evac, i - 3)
                for k in range(RKV // P):
                    ins = nc.tensor.matmul(bank[4 + i % 4][:, :], ckvT[:, k, t * P:(t + 1) * P],
                                           w_ukv_sb[:, k, ch * HALF:(ch + 1) * HALF], start=(k == 0), stop=(k == RKV // P - 1))
                ins.then_inc(kvmm_done, 1)
            pe.wait_ge(w_uq, 16)
            for i in range(6):
                t, ch = i // 3, i % 3
                if i >= 4:
                    pe.wait_ge(q_evac, i - 3)
                for k in range(RQ // P):
                    ins = nc.tensor.matmul(bank[i % 4][:, :], cqT[:, k, t * P:(t + 1) * P],
                                           w_uq_sb[:, k, ch * HALF:(ch + 1) * HALF], start=(k == 0), stop=(k == RQ // P - 1))
                ins.then_inc(qmm_done, 1)
            pe.wait_ge(q_evac, 6)
            for n in range(16):
                kind, t, hg = n // 4, (n % 4) // 2, n % 2
                if n == 0:
                    pe.wait_ge(k_ready, 1)
                if n == 8:
                    pe.wait_ge(q_ready, 1)
                if n >= 8:
                    pe.wait_ge(hd_dve if n % 2 == 0 else hd_act, (n - 8) // 2 + 1)
                for j in range(4):
                    hh = 4 * hg + j
                    src = (k_tok[:, t, hh, :], krh[:, t, hh, :], q_h[:, t, hh, 0:NOPE], qrr[:, t, hh, :])[kind]
                    ins = nc.tensor.transpose(bank[n % 8][0:src.shape[1], j * P:(j + 1) * P], src, ident[:, :])
                ins.then_inc(hd_tr, 1)
            pe.wait_ge(hd_dve, 8)
            pe.wait_ge(hd_act, 8)
            for t in range(TT):
                nk = (t + 1) * P
                for hh in range(H):
                    b = hh // 4 if t == 0 else 2 + hh // 2
                    c = (hh % 4) * P if t == 0 else (hh % 2) * S
                    nc.tensor.matmul(bank[b][:, c:c + nk], qTn[:, hh, t * P:(t + 1) * P], kTn[:, hh, 0:nk], start=True, stop=False)
                    ins = nc.tensor.matmul(bank[b][:, c:c + nk], qTr[0:ROPE, hh, t * P:(t + 1) * P], kTr[0:ROPE, hh, 0:nk],
                                           start=False, stop=True)
                    if hh % (4 if t == 0 else 2) == (3 if t == 0 else 1):
                        ins.then_inc(sc_done, 1)
            for n in range(6):
                if n == 0:
                    pe.wait_ge(p_ready, 1)
                if n == 2:
                    pe.wait_ge(p_ready, 2)
                for j in range(4):
                    src = sc0[:, 4 * n + j, :] if n < 2 else sc1[:, 2 * (n - 2) + j // 2, (j % 2) * P:(j % 2 + 1) * P]
                    ins = nc.tensor.transpose(bank[prob_bank(n)][:, j * P:(j + 1) * P], src, ident[:, :])
                ins.then_inc(ptr_done, 1)
            pe.wait_ge(pT_dve, 3)
            pe.wait_ge(pT_act, 3)
            for t in range(TT):
                for hh in range(H):
                    for kt in range(t + 1):
                        ins = nc.tensor.matmul(bank[4 + 2 * t + hh // 4][:, (hh % 4) * P:(hh % 4 + 1) * P], v_tok[:, kt, hh, :],
                                               pT0[:, hh, :] if t == 0 else pT1[:, hh, kt, :],
                                               start=(kt == 0), stop=(kt == t))
                    if hh % 4 == 3:
                        ins.then_inc(o_done, 1)
            pe.wait_ge(w_o, 16)
            pe.wait_ge(o_dve, 2)
            pe.wait_ge(o_act, 2)
            for j in range(4):
                t, hf = j // 2, j % 2
                for hh in range(H):
                    ins = nc.tensor.matmul(bank[j][:, :], oT[:, hh, t * P:(t + 1) * P], w_o_sb[:, hh, hf * HALF:(hf + 1) * HALF],
                                           start=(hh == 0), stop=(hh == H - 1))
                ins.then_inc(wo_done, 1)

            experts(1)

        @block.vector
        def _(dve):
            dve_n = [0]
            V = nc.vector

            def link(ins):
                dve_n[0] += 1
                ins.then_inc(dve_step, 1)
                dve.wait_ge(dve_step, dve_n[0])

            dve.wait_ge(const_ready, 11)
            link(V.tensor_copy(iota[:, :], iota_i[:, :]))
            V.tensor_scalar(iota_m[:, :], iota[:, :], -float(CAP), None, ALU.add).then_inc(const_f, 1)
            dve.wait_ge(cols_tr, 1)
            V.tensor_copy(cols[:, 0:N_ROWS], bank[7][:, 0:N_ROWS])
            V.tensor_copy(dwT[:, :, :], bank[7][:, P:P + KD * CW].rearrange("p (m w) -> p m w", m=KD)).then_inc(cols_ready, 1)
            dve.wait_ge(cols_ready, 1)

            def norm(i, g):
                dve.wait_ge(rms_ready, i + 1)
                link(V.reciprocal(rr[:, 0:2], rms[:, 0:2]))
                if g is None:
                    dve.wait_ge(E[i // 2]["gain_in"], 16)
                for t in range(TT):
                    if g is None:
                        V.scalar_tensor_tensor(out=xn[:, t, :], in0=h[:, t, :], scalar=rr[:, t:t + 1], in1=gain[:, :],
                                               op0=ALU.mult, op1=ALU.mult).then_inc(xn_ready, 1)
                    else:
                        V.tensor_scalar(xn[:, t, :], h[:, t, :], rr[:, t:t + 1], None, ALU.mult).then_inc(xn_ready, 1)
                for b in range(4):
                    t, kh = b // 2, b % 2
                    dve.wait_ge(tr_done, 4 * i + b + 1)
                    dst = xT[:, 4 * kh:4 * kh + 4, t * P:(t + 1) * P]
                    src = bank[b][:, :].rearrange("p (k q) -> p k q", k=4)
                    if g is None:
                        V.tensor_copy(dst, src).then_inc(xT_ready, 1)
                    else:
                        V.tensor_tensor(dst, src, over(col(g, 4 * kh, 4), P), ALU.mult).then_inc(xT_ready, 1)

            norm(0, "a_norm_g")
            dve.wait_ge(u_zero, 1)
            for m in range(KD):
                dve.wait_ge(sg_ready, m + 1)
                V.scalar_tensor_tensor(out=u_sb[:, m, PAD:PAD + S], in0=bank[4 + m % 4][:, 0:S], scalar=col("pw1_b", m),
                                       in1=sg[:, m % 2, :], op0=ALU.add, op1=ALU.mult).then_inc(u_ready, 1)
                dve.wait_ge(u_ready, m + 1)
                link(V.tensor_scalar(cv[:, m, :], u_sb[:, m, 0:S], dwT[:, m, 0:1], col("dw_b", m), ALU.mult, ALU.add))
                for w in range(1, CW):
                    ins = V.scalar_tensor_tensor(out=cv[:, m, :], in0=u_sb[:, m, w:w + S], scalar=dwT[:, m, w:w + 1],
                                                 in1=cv[:, m, :], op0=ALU.mult, op1=ALU.add)
                    if w < CW - 1:
                        link(ins)
                ins.then_inc(conv_done, 1)
            dve.wait_ge(mean_done, 1)
            dve.wait_ge(conv_done, KD)
            for m in range(KD):
                V.tensor_tensor(cv[:, m, :], cv[:, m, :], bank[0][:, 0:S], ALU.subtract).then_inc(diff_ready, 1)
            dve.wait_ge(lstd_ready, 1)
            link(V.reciprocal(rstd_t, std_t))
            for m in range(KD):
                V.tensor_tensor(cv[:, m, :], cv[:, m, :], rstd_t, ALU.mult).then_inc(dn_ready, 1)
            dve.wait_ge(hb_ready, 2)
            for j in range(4):
                t, hf = j // 2, j % 2
                dve.wait_ge(pw2_done, j + 1)
                V.tensor_tensor(h[:, t, hf * HALF:(hf + 1) * HALF], bank[4 + j][:, :], h[:, t, hf * HALF:(hf + 1) * HALF],
                                ALU.add).then_inc(h_ready[1], 1)

            def experts(l):
                e = E[l]
                norm(1 + 2 * l, None)
                for t in range(TT):
                    dve.wait_ge(e["xh_ready"], t + 1)
                    V.tensor_tensor(x_lo[:, t, :], xn[:, t, :], x_hi[:, t, :], ALU.subtract).then_inc(e["xsplit_ready"], 1)
                G = GROUPS
                dve.wait_ge(e["logits_done"], 1)
                link(V.tensor_tensor(lg[:, :, :], bank[4][:, 0:TT * CAP].rearrange("p (t c) -> p t c", t=TT)[:, :, 0:NR],
                                     br[:, l, :].unsqueeze(1).to_broadcast([P, TT, NR]), ALU.add))
                link(V.tensor_reduce(gmx[:, :], lg[:, :, 0:G], AX_X, ALU.max))
                V.tensor_tensor(gex[:, :, :], lg[:, :, 0:G], over(gmx[:, :], G), ALU.subtract).then_inc(e["gexp_in"], 1)
                link(V.tensor_tensor(geq[:, :, :], lg[:, :, 0:G], over(gmx[:, :], G), ALU.is_equal))
                link(V.tensor_tensor(geq[:, :, :], geq[:, :, :], iota_m[:, 0:G].unsqueeze(1).to_broadcast([P, TT, G]), ALU.mult))
                link(V.tensor_reduce(gix[:, :], geq[:, :, :], AX_X, ALU.min))
                link(V.tensor_tensor(geq[:, :, :], iota_m[:, 0:G].unsqueeze(1).to_broadcast([P, TT, G]), over(gix[:, :], G), ALU.is_equal))
                link(V.tensor_scalar(geq[:, :, :], geq[:, :, :], NEG, -NEG, ALU.mult, ALU.add))
                link(V.tensor_tensor(em[:, :, :].rearrange("p t (g x) -> p t g x", g=G),
                                     lg[:, :, G:NR].rearrange("p t (g x) -> p t g x", g=G),
                                     geq[:, :, :].unsqueeze(3).to_broadcast([P, TT, G, EG]), ALU.add))
                im = iota_m[:, 0:NE].unsqueeze(1).to_broadcast([P, TT, NE])
                for mx, oh in ((mx1, oh1), (mx2, oh2)):
                    link(V.tensor_reduce(mx[:, :], em[:, :, :], AX_X, ALU.max))
                    link(V.tensor_tensor(eeq[:, :, :], em[:, :, :], over(mx[:, :], NE), ALU.is_equal))
                    link(V.tensor_tensor(eeq[:, :, :], eeq[:, :, :], im, ALU.mult))
                    link(V.tensor_reduce(eix[:, :], eeq[:, :, :], AX_X, ALU.min))
                    link(V.tensor_tensor(oh[:, :, :], im, over(eix[:, :], NE), ALU.is_equal))
                    if mx is mx1:
                        link(V.scalar_tensor_tensor(out=em[:, :, :], in0=oh[:, :, :], scalar=-2 * NEG, in1=em[:, :, :],
                                                    op0=ALU.mult, op1=ALU.add))
                V.tensor_tensor(picked[:, :, :], oh1[:, :, :], oh2[:, :, :], ALU.add).then_inc(e["mask_ready"], 1)
                V.tensor_tensor(w2[:, :], mx2[:, :], mx1[:, :], ALU.subtract).then_inc(e["eexp_in"], 1)
                dve.wait_ge(e["gexp_ready"], 1)
                link(V.tensor_reduce(gsm[:, :], gex[:, :, :], AX_X, ALU.add))
                link(V.reciprocal(gw[:, :], gsm[:, :]))
                dve.wait_ge(e["eexp_ready"], 1)
                link(V.tensor_scalar(w1[:, :], w2[:, :], 1.0, None, ALU.add))
                link(V.reciprocal(w1[:, :], w1[:, :]))
                link(V.tensor_tensor(w1[:, :], w1[:, :], gw[:, :], ALU.mult))
                link(V.tensor_tensor(w2[:, :], w1[:, :], w2[:, :], ALU.mult))
                link(V.tensor_tensor(oh1[:, :, :], oh1[:, :, :], over(w1[:, :], NE), ALU.mult))
                link(V.tensor_tensor(oh2[:, :, :], oh2[:, :, :], over(w2[:, :], NE), ALU.mult))
                link(V.tensor_tensor(oh1[:, :, :], oh1[:, :, :], oh2[:, :, :], ALU.add))
                for q in range(PASSES):
                    V.tensor_copy(gate[:, :, q * NE:(q + 1) * NE], oh1[:, :, :])
                dve.wait_ge(e["pos_done"], 1)
                link(V.tensor_tensor(eeq[:, :, :], bank[5][:, 0:TT * NE].rearrange("p (t x) -> p t x", t=TT), picked[:, :, :], ALU.mult))
                for q in range(PASSES):
                    ins = V.tensor_scalar(slot[:, :, q * NE:(q + 1) * NE], eeq[:, :, :], -1.0 - q * CAP, None, ALU.add)
                link(ins)
                link(V.tensor_reduce(cmx[:, 0:1], bank[5][:, 2 * NE:3 * NE], AX_X, ALU.max))
                for q in range(1, PASSES):
                    link(V.tensor_scalar(cmx[:, q:q + 1], cmx[:, 0:1], q * CAP + 0.5, float(PAIRS), ALU.is_ge, ALU.mult))
                link(V.tensor_reduce(cmx[:, 0:1], cmx[:, 1:PASSES], AX_X, ALU.add))
                V.tensor_scalar(npairs_i[:, :], cmx[:, 0:1], float(PAIRS), None, ALU.add).then_inc(e["npairs_ready"], 1)

                def low(it, first, last):
                    for c in range(first, last):
                        dve.wait_ge(e["hi_ready"], 24 * it + c + 1)
                        V.tensor_tensor(w_lo[:, c % SPLIT, :], raw[:, c, :], w_hi[:, c % SPLIT, :],
                                        ALU.subtract).then_inc(e["lo_ready"], 1)

                def one_hot(n):
                    for s in range(2):
                        for t in range(TT):
                            ins = V.tensor_scalar(pick[:, t, s * CAP:(s + 1) * CAP], iota[:, :],
                                                  slot[:, t, bass.ds(2 * n + s, 1)], None, ALU.is_equal)
                    ins.then_inc(e["pick_ready"], 1)

                def gated(n):
                    for s in range(2):
                        for t in range(TT):
                            ins = V.tensor_scalar(pw[:, s, t, :].rearrange("p (a c) -> p a c", a=2),
                                                  iota[:, :].unsqueeze(1).to_broadcast([P, 2, CAP]),
                                                  slot[:, t, bass.ds(2 * n + s, 1)], gate[:, t, bass.ds(2 * n + s, 1)],
                                                  ALU.is_equal, ALU.mult)
                    ins.then_inc(e["pw_ready"], 1)

                def tokens_low(n):
                    dve.wait_ge(e["xhi_ready"], n)
                    for b in range(2):
                        ins = V.tensor_tensor(xs[:, :, 4 * b:4 * b + 4, CAP:PAIR].rearrange("p s k c -> p k s c"),
                                              bank[4 + b][:, :].rearrange("p (k s c) -> p k s c", k=4, s=2),
                                              xs[:, :, 4 * b:4 * b + 4, 0:CAP].rearrange("p s k c -> p k s c"), ALU.subtract)
                    ins.then_inc(e["xs_ready"], 1)

                def hidden(n, s):
                    dve.wait_ge(e["silu_done"], n)
                    V.tensor_tensor(hid[:, s, :, :], sil[:, :, :], bank[0][:, KF * CAP:2 * KF * CAP].rearrange("p (k c) -> p k c", k=KF),
                                    ALU.mult).then_inc(e["h_prod"], 1)
                    dve.wait_ge(e["h_prod"], n)
                    V.tensor_copy(hs[:, s, :, 0:CAP], hid[:, s, :, :]).then_inc(e["h_hi"], 1)
                    dve.wait_ge(e["h_hi"], n)
                    V.tensor_tensor(hs[:, s, :, CAP:PAIR], hid[:, s, :, :], hs[:, s, :, 0:CAP], ALU.subtract).then_inc(e["hs_ready"], 1)

                def add_scattered(j, it, added):
                    t, hf = j // 2, j % 2
                    dve.wait_ge(e["s_done"], 4 * it + 1 + j)
                    V.tensor_tensor(h[:, t, hf * HALF:(hf + 1) * HALF], bank[6 + j % 2][:, :],
                                    h[:, t, hf * HALF:(hf + 1) * HALF], ALU.add).then_inc(added, 1)

                dve.wait_ge(dve_step, dve_n[0])
                one_hot(0)
                dve.wait_ge(e["logits_done"], 1)
                V.memset(y_rows[:, 0, :], 0.0).then_inc(e["y_ready"], 1)
                V.memset(pwT[:, :, :], 0.0).then_inc(e["pwT_ready"], 1)
                V.memset(bank[2][:, :], 0.0)
                V.memset(bank[3][:, :], 0.0)
                V.memset(sil[:, 0, 0:1], 0.0).then_inc(e["chunk_free"], SPLIT)
                dve.wait_ge(e["npairs_ready"], 1)
                n_pairs = dve.value_load(npairs_i[0:1, 0:1], min_val=PAIRS, max_val=PAIRS * PASSES)
                tokens_low(1)
                with dve.Fori(0, n_pairs) as it:
                    low(it, 0, 10)
                    add_scattered(0, it, e["s_added"])
                    low(it, 10, 11)
                    add_scattered(1, it, e["s_added"])
                    low(it, 11, 12)
                    hidden(2 * it + 1, 0)
                    add_scattered(2, it, e["s_added"])
                    gated(it)
                    add_scattered(3, it, e["s_added"])
                    one_hot(it + 1)
                    low(it, 12, 24)
                    hidden(2 * it + 2, 1)
                    tokens_low(it + 2)
                for j in range(4):
                    add_scattered(j, n_pairs, h_ready[2 + 2 * l])

            experts(0)

            MAGIC = 1.5 * 2.0 ** 23
            TWO_PI = 2.0 * np.pi
            p1 = float(np.float32(np.floor(TWO_PI * 2 ** 8) / 2 ** 8))
            p2 = float(np.floor((TWO_PI - p1) * 2 ** 20) / 2 ** 20)
            p3 = float(np.float32(TWO_PI - p1 - p2))
            dve.wait_ge(small2_in, 16 * (4 * L + 4))
            link(V.tensor_copy(pos_f[:, :], pos_i[:, :]))
            for t in range(TT):
                ins = V.tensor_scalar(ang[:, t, :], inv_freq[:, :], pos_f[:, t:t + 1], None, ALU.mult)
            link(ins)
            link(V.tensor_scalar(ang_k[:, :, :], ang[:, :, :], 1.0 / TWO_PI, None, ALU.mult))
            link(V.tensor_scalar(ang_k[:, :, :], ang_k[:, :, :], MAGIC, None, ALU.add))
            link(V.tensor_scalar(ang_k[:, :, :], ang_k[:, :, :], -MAGIC, None, ALU.add))
            for part in (p1, p2):
                link(V.scalar_tensor_tensor(out=ang[:, :, :], in0=ang_k[:, :, :], scalar=-part, in1=ang[:, :, :],
                                            op0=ALU.mult, op1=ALU.add))
            link(V.scalar_tensor_tensor(out=ang[:, :, :], in0=ang_k[:, :, :], scalar=-p3, in1=ang[:, :, :],
                                        op0=ALU.mult, op1=ALU.add))
            PI_IN = float(np.nextafter(np.float32(np.pi), np.float32(0)))
            V.tensor_scalar(ang[:, :, :], ang[:, :, :], PI_IN, -PI_IN, ALU.min, ALU.max).then_inc(ang_ready, 1)

            norm(2, "kv_norm_g")
            dve.wait_ge(trig, 2)
            link(V.tensor_tensor(cos[:, :, :], cos[:, :, :], cos[:, :, :], ALU.mult))
            link(V.tensor_scalar(cos[:, :, :], cos[:, :, :], -2.0, 1.0, ALU.mult, ALU.add))
            dve.wait_ge(crms_ready, 2)
            link(V.reciprocal(rr[:, :], rms[:, :]))
            for t in range(TT):
                V.tensor_scalar(ckv_n[:, t, :], bank[4 + t][:, 0:RKV], rr[:, t:t + 1], None, ALU.mult).then_inc(cn_ready, 1)
                V.tensor_copy(kr_raw[:, t, :], bank[4 + t][:, RKV:RKV + ROPE])
                V.tensor_scalar(cq_n[:, t, :], bank[6 + t][:, 0:RQ], rr[:, 2 + t:3 + t], None, ALU.mult).then_inc(cn_ready, 1)
            for n, (dst, b, g, w) in enumerate(((ckvT, 0, "kv_latent_g", 2), (cqT[:, 0:2, :], 1, "q_latent_g", 2),
                                                (cqT[:, 2:3, :], 2, "q_latent_g", 1))):
                dve.wait_ge(ctr_done, n + 1)
                V.tensor_tensor(dst, bank[b][:, 0:w * S].rearrange("p (k q) -> p k q", k=w),
                                over(col(g, 2 if n == 2 else 0, w), S), ALU.mult).then_inc(cT_ready, 1)

            def rotate(dst, src, shape, tmp):
                def like(x):
                    return x if len(shape) == 3 else x.unsqueeze(2).to_broadcast([P, TT, H, HR])
                lo, hi = (slice(0, HR), slice(HR, ROPE))
                pick_ = (lambda x, s: x[:, :, s]) if len(shape) == 3 else (lambda x, s: x[:, :, :, s])
                c, s_ = like(cos[:, :, :]), like(sin[:, :, :])
                x1, x2 = pick_(src, lo), pick_(src, hi)
                V.tensor_tensor(tmp[0], x1, c, ALU.mult)
                V.tensor_tensor(tmp[1], x2, s_, ALU.mult)
                V.tensor_tensor(tmp[2], x1, s_, ALU.mult)
                link(V.tensor_tensor(tmp[3], x2, c, ALU.mult))
                V.tensor_tensor(pick_(dst, lo), tmp[0], tmp[1], ALU.subtract)
                link(V.tensor_tensor(pick_(dst, hi), tmp[2], tmp[3], ALU.add))

            link(V.tensor_tensor(kr_raw, kr_raw, qk_gr[:, 0, :].unsqueeze(1).to_broadcast([P, TT, ROPE]), ALU.mult))
            rotate(kr_rot, kr_raw, (P, TT, HR), [t[:, :, 0, :] for t in rot_tmp])
            dve.wait_ge(kv_evac, 8)
            for t in range(TT):
                sq = sq_tmp[:, 0:H * NOPE].rearrange("p (h c) -> p h c", h=H)
                link(V.tensor_tensor(sq, k_tok[:, t, :, :], k_tok[:, t, :, :], ALU.mult))
                link(V.tensor_reduce(ss_h[:, 0, t * H:(t + 1) * H], sq, AX_X, ALU.add))
            for t in range(TT):
                V.tensor_scalar(ss_h[:, 0, t * H:(t + 1) * H], ss_h[:, 0, t * H:(t + 1) * H], ss_kr[:, t:t + 1], None,
                                ALU.add)
            link(V.memset(ang_k[:, 0, 0:1], 0.0))
            V.memset(ang_k[:, 0, 0:1], 0.0).then_inc(kss_ready, 1)
            dve.wait_ge(krms_ready, 1)
            link(V.reciprocal(r_h[:, 0, :], r_h[:, 0, :]))
            rk = r_h[:, 0, :]
            V.tensor_tensor(k_tok.rearrange("p t h c -> p (t h) c"), k_tok.rearrange("p t h c -> p (t h) c"), over(rk, NOPE), ALU.mult)
            V.tensor_tensor(krh, kr_rot.unsqueeze(2).to_broadcast([P, TT, H, ROPE]),
                            rk.rearrange("p (t h) -> p t h", t=TT).unsqueeze(3).to_broadcast([P, TT, H, ROPE]),
                            ALU.mult).then_inc(k_ready, 1)
            for i in range(6):
                t, ch = i // 3, i % 3
                dve.wait_ge(qmm_done, i + 1)
                V.tensor_copy(q_tok[:, t, ch * HALF:(ch + 1) * HALF], bank[i % 4][:, :]).then_inc(q_evac, 1)
            dve.wait_ge(q_evac, 6)
            for t in range(TT):
                sq = sq_tmp[:, 0:H * QK].rearrange("p (h c) -> p h c", h=H)
                link(V.tensor_tensor(sq, q_h[:, t, :, :], q_h[:, t, :, :], ALU.mult))
                ins = V.tensor_reduce(ss_h[:, 1, t * H:(t + 1) * H], sq, AX_X, ALU.add)
                if t == 0:
                    link(ins)
            ins.then_inc(qss_ready, 1)
            dve.wait_ge(qrms_ready, 1)
            link(V.reciprocal(r_h[:, 1, :], r_h[:, 1, :]))
            q_all = q_tok.rearrange("p t (h c) -> p (t h) c", h=H)
            link(V.tensor_tensor(q_all, q_all, over(r_h[:, 1, :], QK), ALU.mult))
            q_r = q_h[:, :, :, NOPE:QK]
            link(V.tensor_tensor(q_r, q_r, qk_gr[:, 1, :].unsqueeze(1).unsqueeze(1).to_broadcast([P, TT, H, ROPE]), ALU.mult))
            rotate(qrr, q_r, (P, TT, H, HR), rot_tmq)
            V.memset(ang_k[:, 0, 0:1], 0.0).then_inc(q_ready, 1)
            for n in range(0, 16, 2):
                dve.wait_ge(hd_tr, n + 1)
                dst, rot, g = head_block(n)
                if rot:
                    V.tensor_copy(dst, bank[n % 8][0:ROPE, :].rearrange("p (h q) -> p h q", h=4)).then_inc(hd_dve, 1)
                else:
                    V.tensor_scalar(dst, bank[n % 8][:, :].rearrange("p (h q) -> p h q", h=4), g, None, ALU.mult).then_inc(hd_dve, 1)
            scale = float(QK) ** -0.5
            for n in range(6):
                dve.wait_ge(sc_done, n + 1)
                if n < 2:
                    dst, w, mk = sc0[:, 4 * n:4 * n + 4, :], 4, mask[:, S - P:S]
                else:
                    dst, w, mk = sc1[:, 2 * (n - 2):2 * (n - 2) + 2, :], 2, mask[:, 0:S]
                nk = HALF // w
                ins = V.scalar_tensor_tensor(out=dst, in0=bank[n][:, :].rearrange("p (h k) -> p h k", h=w), scalar=scale,
                                             in1=mk.unsqueeze(1).to_broadcast([P, w, nk]), op0=ALU.mult, op1=ALU.add)
                if n in (1, 5):
                    t = n // 5
                    link(ins)
                    link(V.tensor_reduce(smax[:, t, :], sc0 if t == 0 else sc1, AX_X, ALU.max))
                    V.tensor_scalar(smax[:, t, :], smax[:, t, :], -1.0, None, ALU.mult).then_inc(smax_ready, 1)
            for t in range(TT):
                dve.wait_ge(exp_done, (t + 1) * H)
                link(V.reciprocal(sinv[:, t, :], ssum[:, t, :]))
                s = sc0 if t == 0 else sc1
                V.tensor_tensor(s, s, over(sinv[:, t, :], (t + 1) * P), ALU.mult).then_inc(p_ready, 1)
            for n in range(0, 6, 2):
                dve.wait_ge(ptr_done, n + 1)
                V.tensor_copy(prob_block(n), bank[prob_bank(n)][:, :].rearrange("p (a q) -> p a q", a=4)).then_inc(pT_dve, 1)
            for n in range(0, 4, 2):
                dve.wait_ge(o_done, n + 1)
                t, hg = n // 2, n % 2
                V.tensor_copy(oT[:, 4 * hg:4 * hg + 4, t * P:(t + 1) * P],
                              bank[4 + n][:, :].rearrange("p (h q) -> p h q", h=4)).then_inc(o_dve, 1)
            for j in range(4):
                t, hf = j // 2, j % 2
                dve.wait_ge(wo_done, j + 1)
                V.tensor_tensor(h[:, t, hf * HALF:(hf + 1) * HALF], bank[j][:, :], h[:, t, hf * HALF:(hf + 1) * HALF],
                                ALU.add).then_inc(h_ready[3], 1)

            experts(1)


_INS = ["x", "positions", "a_norm_g", "a_pw1_w", "a_pw1_b", "a_dw_w", "a_dw_b", "a_ln_g", "a_ln_b", "a_pw2_w", "a_pw2_b",
        "kv_norm_g", "w_dkv", "kv_latent_g", "w_kr", "w_ukv", "k_norm_g", "b_norm_g", "w_dq", "q_latent_g", "w_uq",
        "q_norm_g", "w_o", "ffn_norm_g", "w_group", "b_group", "w_router", "b_router", "w_gate_up", "w_down"]


def kernel(**inputs):
    import numpy as _np
    import concourse.bacc as _bacc
    from concourse import mybir as _mybir
    from concourse.bass_utils import run_bass_kernel_spmd as _run

    nc = _bacc.Bacc("TRN2", target_bir_lowering=False, num_devices=1)
    arrays, args = {}, {}

    def declare(name, a):
        arrays[f"in_{name}_dram"] = a
        args[name] = nc.dram_tensor(f"in_{name}_dram", a.shape, _mybir.dt.from_np(a.dtype), kind="ExternalInput").ap()

    for name in _INS:
        declare(name, _np.ascontiguousarray(inputs[name]))
    rope = args["w_kr"].shape[1]
    inv = _np.float32(ROPE_THETA) ** (-_np.arange(0, rope, 2, dtype=_np.float32) / _np.float32(rope))
    declare("inv_freq", inv.astype(_np.float32).reshape(1, rope // 2))
    shape = inputs["x"].shape
    out = nc.dram_tensor("out_0_dram", shape, F32, kind="ExternalOutput").ap()
    trunk_kernel(nc, args, out)
    r = _run(nc, [arrays], core_ids=[0])
    return r.results[0]["out_0_dram"]
```

```python
from contextlib import ExitStack

import numpy as np

import concourse.bass as bass
from concourse import mybir

ALU = mybir.AluOpType
ACT = mybir.ActivationFunctionType
F32 = mybir.dt.float32
F32R = mybir.dt.float32r
I32 = mybir.dt.int32
AX_X = mybir.AxisListType.X

P = 128
EPS = 1e-6
NEG = 1e30
CAP = 64
PAIR = 2 * CAP
ROPE_THETA = 10000.0
CHUNK = 64
GROUPS = 4
SPLIT = 5


def trunk_kernel(nc: bass.Bass, a, out):
    _, S, D = a["x"].shape
    L, NE, _, FF2 = a["w_gate_up"].shape
    F = FF2 // 2
    TT = S // P
    KD = D // P
    KF = F // P
    CW = a["a_dw_w"].shape[1]
    PAD = CW - 1
    RKV = a["w_dkv"].shape[1]
    RQ = a["w_dq"].shape[2]
    ROPE = a["w_kr"].shape[1]
    HR = ROPE // 2
    QK = a["k_norm_g"].shape[0]
    NOPE = QK - ROPE
    H = a["w_uq"].shape[2] // QK
    DV = a["w_o"].shape[1] // H
    EG = NE // GROUPS
    NR = GROUPS + NE
    PASSES = -(-S // CAP)
    PAIRS = NE // 2
    HALF = 512
    assert TT == 2 and D == 2 * HALF and NOPE == P and DV == P and PAIR == P and KF * P == F and NE == 32

    with ExitStack() as ctx:
        def sb(name, shape, dt=F32):
            return ctx.enter_context(nc.sbuf_tensor(name, shape, dt))

        def sem(name):
            return ctx.enter_context(nc.semaphore(name))

        bank = [ctx.enter_context(nc.psum_tensor(f"bank{i}", [P, HALF], F32)) for i in range(8)]

        UNIT = 4 * D
        ring = sb("ring", [P, 6 * UNIT])
        raw = ring[:, :].rearrange("p (c n) -> p c n", n=D)
        unit_sb = [ring[:, u * UNIT:(u + 1) * UNIT].rearrange("p (k c) -> p k c", k=4) for u in range(6)]
        pw1_sb = [ring[:, i * UNIT // 2:(i + 1) * UNIT // 2].rearrange("p (k c) -> p k c", k=KD) for i in range(KD)]
        pw2_sb = ring[:, 4 * UNIT:6 * UNIT].rearrange("p (k c) -> p k c", k=KD)
        o1 = KD * (RKV + ROPE)
        o2 = o1 + KD * RQ
        o3 = o2 + (RQ // P) * H * QK
        w_dkvr_sb = ring[:, 0:o1].rearrange("p (k c) -> p k c", k=KD)
        w_dq_sb = ring[:, o1:o2].rearrange("p (k c) -> p k c", k=KD)
        w_uq_sb = ring[:, o2:o3].rearrange("p (k c) -> p k c", k=RQ // P)
        w_ukv_sb = ring[:, 3 * UNIT:4 * UNIT].rearrange("p (k c) -> p k c", k=RKV // P)
        w_o_sb = ring[:, 4 * UNIT:6 * UNIT].rearrange("p (k c) -> p k c", k=H)
        assert o3 <= 3 * UNIT

        h = sb("h", [P, TT, D])
        xn = sb("xn", [P, TT, D])
        xT = sb("xT", [P, KD, S])
        NC_ = PASSES * NE + 2

        ident = sb("ident", [P, P])
        upto = sb("upto", [P, P])
        ones = sb("ones", [P, P])
        both = sb("both", [P, CAP])
        eps_c = sb("eps_c", [P, 1])
        warm = sb("warm", [P, 1])
        cols = sb("cols", [P, P])
        dwT = sb("dwT", [P, KD, CW])
        iota_i = sb("iota_i", [P, CAP], I32)
        iota = sb("iota", [P, CAP])
        iota_m = sb("iota_m", [P, CAP])
        wr = sb("wr", [P, L, KD, NR])
        br = sb("br", [P, L, NR])
        qk_gr = sb("qk_gr", [P, 2, ROPE])
        mask = sb("mask", [P, S])
        inv_freq = sb("inv_freq", [P, HR])
        pos_i = sb("pos_i", [P, TT], I32)
        pos_f = sb("pos_f", [P, TT])
        cos = sb("cos", [P, TT, HR])
        sin = sb("sin", [P, TT, HR])
        ss = sb("ss", [P, 4])
        rms = sb("rms", [P, 4])
        rn = sb("rn", [P, TT])
        rr = sb("rr", [P, 4])
        lg = sb("lg", [P, TT, NR])
        gmx = sb("gmx", [P, TT])
        gex = sb("gex", [P, TT, GROUPS])
        gsm = sb("gsm", [P, TT])
        gw = sb("gw", [P, TT])
        geq = sb("geq", [P, TT, GROUPS])
        gix = sb("gix", [P, TT])
        em = sb("em", [P, TT, NE])
        eeq = sb("eeq", [P, TT, NE])
        oh1 = sb("oh1", [P, TT, NE])
        oh2 = sb("oh2", [P, TT, NE])
        mx1 = sb("mx1", [P, TT])
        mx2 = sb("mx2", [P, TT])
        eix = sb("eix", [P, TT])
        w1 = sb("w1", [P, TT])
        w2 = sb("w2", [P, TT])
        picked = sb("picked", [P, TT, NE])
        slot = sb("slot", [P, TT, NC_])
        gate = sb("gate", [P, TT, NC_])
        cmx = sb("cmx", [P, 4])
        npairs_i = sb("npairs_i", [P, 1], I32)
        gate_c = sb("gate_c", [P, 1])
        ss_kr = sb("ss_kr", [P, TT])
        ss_h = sb("ss_h", [P, 2, TT * H])
        r_h = sb("r_h", [P, 2, TT * H])
        smax = sb("smax", [P, TT, H])
        ssum = sb("ssum", [P, TT, H])
        sinv = sb("sinv", [P, TT, H])


        with ExitStack() as dense:
            def dense_sb(name, shape, dt=F32):
                return dense.enter_context(nc.sbuf_tensor(name, shape, dt))

            xT2 = dense_sb("xT2", [P, KD, S])
            arena = dense_sb("arena", [P, 16640])
        with ExitStack() as sparse:
            def moe_sb(name, shape, dt=F32):
                return sparse.enter_context(nc.sbuf_tensor(name, shape, dt))

            x_hi, x_lo = moe_sb("x_hi", [P, TT, D], F32R), moe_sb("x_lo", [P, TT, D], F32R)
            w_hi, w_lo = moe_sb("w_hi", [P, SPLIT, D], F32R), moe_sb("w_lo", [P, SPLIT, D], F32R)
            xs = moe_sb("xs", [P, 2, KD, PAIR], F32R)
            pick = moe_sb("pick", [P, TT, PAIR], F32R)
            y_hi, y_lo = moe_sb("y_hi", [P, D], F32R), moe_sb("y_lo", [P, D], F32R)
            pickT = moe_sb("pickT", [P, S], F32R)
        xg = xn[:, 0, :]
        u_rows = xn[:, 1, :]
        xT_flat = xT[:, :, :].rearrange("p k c -> p (k c)")
        n_hid = 2 * KF * PAIR
        hid = xT_flat[:, 0:n_hid].rearrange("p (s k c) -> p s k c", s=2, k=KF)
        sil = xT_flat[:, n_hid:n_hid + KF * CAP].rearrange("p (k c) -> p k c", k=KF)
        pw = xT_flat[:, n_hid + KF * CAP:n_hid + KF * CAP + TT * PAIR].rearrange("p (t c) -> p t c", t=TT)

        def view(offset, *shape):
            n = int(np.prod(shape))
            v = arena[:, offset:offset + n]
            if len(shape) == 1:
                return v
            if len(shape) == 2:
                return v.rearrange("p (a b) -> p a b", b=shape[1])
            return v.rearrange("p (a b c) -> p a b c", b=shape[1], c=shape[2])

        gain = view(15360, D)
        u_sb = view(0, KD, PAD + S)
        cv = view(2560, KD, S)
        sg = view(4608, 2, S)
        N_PE = 2

        def diag(i):
            return view(8192 + i * P, P) if i < 56 else xT2[:, :, :].rearrange("p k c -> p (k c)")[:, (i - 56) * P:(i - 55) * P]

        std_t = view(5120, S)
        rstd_t = view(5376, S)
        ang, ang_k = view(5888, TT, HR), view(5888 + TT * HR, TT, HR)
        mean_w = view(5632, P)
        rows = view(5760, P)
        dw_rows = view(6144, D)
        pw2_b_row = view(7168, D)
        q_tok = view(0, TT, H * QK)
        q_h = q_tok.rearrange("p t (h c) -> p t h c", h=H)
        k_tok = view(3072, TT, H, NOPE)
        krh = view(5120, TT, H, ROPE)
        qrr = view(6144, TT, H, ROPE)
        v_tok = view(7168, TT, H, DV)
        kTn = view(9216, H, S)
        qTn = view(11264, H, S)
        kTr = view(13312, H, S)
        ckvT = view(15360, RKV // P, S)
        cqT = view(15872, RQ // P, S)
        qTr = xT2
        sc0 = view(0, H, P)
        sc1 = view(1024, H, S)
        pT0 = view(3072, H, P)
        pT1 = view(4096, H, TT, P)
        oT = xT
        ckv_n = xn[:, 0, 0:TT * RKV].rearrange("p (t c) -> p t c", t=TT)
        cq_n = xn[:, 1, 0:TT * RQ].rearrange("p (t c) -> p t c", t=TT)
        kr_raw = xn[:, 0, 512:512 + TT * ROPE].rearrange("p (t c) -> p t c", t=TT)
        kr_rot = xn[:, 0, 640:640 + TT * ROPE].rearrange("p (t c) -> p t c", t=TT)
        rot_tmp = [view(13312 + i * 512, TT, H, HR) for i in range(4)]
        rot_tmq = [xT2[:, 2 * i:2 * i + 2, :].rearrange("p a b -> p (a b)").rearrange("p (t h c) -> p t h c", t=TT, h=H)
                   for i in range(4)]

        row_at, spots = 0, {}
        row_loads = []
        for name, ap, n in (
            ("a_norm_g", a["a_norm_g"][0], KD), ("pw1_b", a["a_pw1_b"][0], 2 * KD), ("dw_b", a["a_dw_b"][0], KD),
            ("ln_g", a["a_ln_g"][0], KD), ("ln_b", a["a_ln_b"][0], KD), ("kv_norm_g", a["kv_norm_g"], KD),
            ("b_norm_g", a["b_norm_g"][0], KD), ("ffn_norm_g0", a["ffn_norm_g"][0], KD), ("ffn_norm_g1", a["ffn_norm_g"][1], KD),
            ("kv_latent_g", a["kv_latent_g"], RKV // P), ("q_latent_g", a["q_latent_g"][0], RQ // P),
            ("k_gn", a["k_norm_g"][0:NOPE], 1), ("q_gn", a["q_norm_g"][0][0:NOPE], 1),
        ):
            spots[name] = row_at
            row_loads.append((row_at, n, ap.rearrange("(k p) -> k p", p=P)))
            row_at += n
        N_ROWS = row_at

        def col(name, k=0, n=1):
            return cols[:, spots[name] + k:spots[name] + k + n]

        def over(ap, n):
            return ap.unsqueeze(2).to_broadcast([P, ap.shape[1], n])

        def sc_junk(i, n):
            return arena[:, 9216 + i * HALF:9216 + i * HALF + n]

        def raw_at(c):
            return c + 4 * (c // 8)

        def head_block(n):
            kind, t, hg = n // 4, (n % 4) // 2, n % 2
            dst = (qTn, qTr, kTn, kTr)[kind]
            rot = kind % 2 == 1
            return (dst[0:ROPE if rot else P, 4 * hg:4 * hg + 4, t * P:(t + 1) * P], rot,
                    col("q_gn") if kind == 0 else col("k_gn"))

        def prob_bank(n):
            return (6, 7, 2, 3, 4, 5)[n]

        def wo_bank(j):
            return (6, 7, 2, 3)[j]

        def prob_block(n):
            if n < 2:
                return pT0[:, 4 * n:4 * n + 4, :]
            return pT1[:, 2 * (n - 2):2 * (n - 2) + 2, :, :].rearrange("p h k q -> p (h k) q")

        x_in, w_pw1 = sem("x_in"), [sem(f"w_pw1_{i}") for i in range(KD)]
        w_pw2 = sem("w_pw2")
        pos_in = sem("pos_in")
        rows_in, small_in, small2_in = sem("rows_in"), sem("small_in"), sem("small2_in")
        zeroed, const_ready = sem("zeroed"), sem("const_ready")
        cols_tr, cols_ready = sem("cols_tr"), sem("cols_ready")
        dve_step = sem("dve_step")
        rn_ready = sem("rn_ready")
        ssq, rms_ready, xn_ready, tr_done, xT_ready = sem("ssq"), sem("rms_ready"), sem("xn_ready"), sem("tr_done"), sem("xT_ready")
        h_ready = [sem(f"h_ready{i}") for i in range(5)]
        xT2_ready = sem("xT2_ready")
        pw1_done, sg_ready, u_ready, u_zero = sem("pw1_done"), sem("sg_ready"), sem("u_ready"), sem("u_zero")
        tap_done, diag_ready, pe_conv_done = sem("tap_done"), sem("diag_ready"), sem("pe_conv_done")
        conv_done, mean_done, diff_ready = sem("conv_done"), sem("mean_done"), sem("diff_ready")
        sq_ready, var_done, lstd_ready, dn_ready = sem("sq_ready"), sem("var_done"), sem("lstd_ready"), sem("dn_ready")
        c_ready, pw2_done, hb_ready = sem("c_ready"), sem("pw2_done"), sem("hb_ready")
        gain_in, xh_ready, xsplit_ready, logits_done = sem("gain_in"), sem("xh_ready"), sem("xsplit_ready"), sem("logits_done")
        gexp_in, gexp_ready, eexp_in, eexp_ready = sem("gexp_in"), sem("gexp_ready"), sem("eexp_in"), sem("eexp_ready")
        mask_ready, pos_done, npairs_ready = sem("mask_ready"), sem("pos_done"), sem("npairs_ready")
        count_done = sem("count_done")
        E = []
        for l in range(L):
            E.append({n: sem(f"{n}_{l}") for n in (
                "unit_in0", "unit_in1", "unit_in2", "unit_in3", "unit_in4", "unit_in5",
                "chunk_free", "hi_ready", "lo_ready", "pick_ready", "pw_ready", "g_done", "xg_ready", "xtr_done", "xhi_ready",
                "xs_ready", "u_ready", "sum_done", "silu_done", "hid_ready", "down_done", "pair_done", "y_ready",
                "back_done", "pickT_ready", "y_hi_ready", "s_done", "s_added")})
        w_c, w_uq, w_ukv, w_o = sem("w_c"), sem("w_uq"), sem("w_ukv"), sem("w_o")
        ang_ready, trig = sem("ang_ready"), sem("trig")
        c_done, csq, crms_ready, cn_ready = sem("c_done"), sem("csq"), sem("crms_ready"), sem("cn_ready")
        ctr_done, cT_ready = sem("ctr_done"), sem("cT_ready")
        kvmm_done, kv_evac, qmm_done, q_evac = sem("kvmm_done"), sem("kv_evac"), sem("qmm_done"), sem("q_evac")
        kr_ready = sem("kr_ready")
        kss_ready, krms_ready, k_ready = sem("kss_ready"), sem("krms_ready"), sem("k_ready")
        qss_ready, qrms_ready, q_ready = sem("qss_ready"), sem("qrms_ready"), sem("q_ready")
        hd_tr, hd_dve, hd_act = sem("hd_tr"), sem("hd_dve"), sem("hd_act")
        sc_done, smax_ready, exp_done, p_ready = sem("sc_done"), sem("smax_ready"), sem("exp_done"), sem("p_ready")
        ptr_done, pT_dve, pT_act = sem("ptr_done"), sem("pT_dve"), sem("pT_act")
        o_done, o_dve, o_act, wo_done = sem("o_done"), sem("o_dve"), sem("o_act"), sem("wo_done")
        out_done = sem("out_done")

        block = ctx.enter_context(nc.Block())

        @block.sync
        def _(sp):
            sp.dma_start(h[:, :, :], a["x"][0].rearrange("(t p) d -> p t d", p=P)).then_inc(x_in, 16)
            sp.wait_ge(rows_in, 16 * (len(row_loads) + 1))
            pw1 = a["a_pw1_w"][0].rearrange("(k p) c -> p k c", p=P)
            for i in range(KD):
                c0 = (i % 2) * D + (i // 2) * 2 * P
                sp.dma_start(pw1_sb[i], pw1[:, :, c0:c0 + 2 * P]).then_inc(w_pw1[i], 16)
            sp.dma_start(pw2_sb, a["a_pw2_w"][0].rearrange("(k p) c -> p k c", p=P)).then_inc(w_pw2, 16)

            def unit_dma(l, u, ex):
                src = a["w_gate_up"][l] if u % 3 < 2 else a["w_down"][l]
                r0 = HALF if u % 3 == 1 else 0
                src = src[bass.ds(ex, 1), r0:r0 + HALF, :].rearrange("e (k p) c -> (e p) k c", p=P)
                sp.dma_start(unit_sb[u], src).then_inc(E[l][f"unit_in{u}"], 16)

            def experts(l, first):
                e = E[l]
                for u in range(6):
                    first(u)
                    unit_dma(l, u, u // 3)
                sp.wait_ge(npairs_ready, l + 1)
                n_pairs = sp.value_load(npairs_i[0:1, 0:1], min_val=PAIRS, max_val=PAIRS * PASSES)
                with sp.Fori(1, n_pairs) as it:
                    ex = (it % PAIRS) * 2
                    for u in range(6):
                        if u == 2:
                            sp.wait_ge(e["down_done"], it)
                        elif u == 5:
                            sp.wait_ge(e["pair_done"], it + 1)
                        else:
                            sp.wait_ge(e["lo_ready"], 16 * it - (16 - 4 * (u + 1 - u // 3)))
                        unit_dma(l, u, ex + u // 3)
                return n_pairs

            def first_after_conv(u):
                if u < 4:
                    sp.wait_ge(pw1_done, 2 * (u + 1))
                if u == 4:
                    sp.wait_ge(pw2_done, 4)

            sp.dma_start(gain, a["ffn_norm_g"][0:1].to_broadcast([P, D])).then_inc(gain_in, 16)
            n0 = experts(0, first_after_conv)
            sp.wait_ge(E[0]["down_done"], n0)
            sp.dma_start(w_dkvr_sb[:, :, 0:RKV], a["w_dkv"].rearrange("(k p) c -> p k c", p=P)).then_inc(w_c, 16)
            sp.dma_start(w_dkvr_sb[:, :, RKV:RKV + ROPE], a["w_kr"].rearrange("(k p) c -> p k c", p=P)).then_inc(w_c, 16)
            sp.dma_start(w_dq_sb, a["w_dq"][0].rearrange("(k p) c -> p k c", p=P)).then_inc(w_c, 16)
            sp.dma_start(w_uq_sb, a["w_uq"][0].rearrange("(k p) c -> p k c", p=P)).then_inc(w_uq, 16)
            sp.wait_ge(E[0]["lo_ready"], 16 * n0)
            sp.dma_start(w_ukv_sb, a["w_ukv"].rearrange("(k p) c -> p k c", p=P)).then_inc(w_ukv, 16)
            sp.wait_ge(E[0]["pair_done"], n0 + 1)
            sp.dma_start(w_o_sb, a["w_o"][0].rearrange("(k p) c -> p k c", p=P)).then_inc(w_o, 16)

            def first_after_attention(u):
                if u == 0:
                    sp.wait_ge(qmm_done, 6)
                    sp.wait_ge(kvmm_done, 8)
                    sp.dma_start(gain, a["ffn_norm_g"][1:2].to_broadcast([P, D])).then_inc(gain_in, 16)
                if u == 4:
                    sp.wait_ge(wo_done, 4)

            experts(1, first_after_attention)
            out_t = out[0].rearrange("(t p) d -> p t d", p=P)
            for j in range(4):
                tt, hf = j // 2, j % 2
                sp.wait_ge(h_ready[4], j + 1)
                sp.dma_start(out_t[:, tt, hf * HALF:(hf + 1) * HALF], h[:, tt, hf * HALF:(hf + 1) * HALF]).then_inc(out_done, 16)
            sp.wait_ge(out_done, 64)

        @block.gpsimd
        def _(pool):
            nc.gpsimd.memset(ident[:, :], 0.0).then_inc(zeroed, 1)
            nc.gpsimd.memset(upto[:, :], 1.0).then_inc(zeroed, 1)
            nc.gpsimd.memset(mask[:, :], 0.0).then_inc(zeroed, 1)
            nc.gpsimd.memset(both[:, :], 0.0).then_inc(zeroed, 1)
            pool.wait_ge(zeroed, 4)
            nc.gpsimd.affine_select(out=ident[:, :], in_=ident[:, :], compare_op=ALU.not_equal, fill=1.0, base=0,
                                    pattern=[[-1, P]], channel_multiplier=1).then_inc(const_ready, 1)
            nc.gpsimd.affine_select(out=upto[:, :], in_=upto[:, :], compare_op=ALU.is_ge, fill=0.0, base=0,
                                    pattern=[[1, P]], channel_multiplier=-1).then_inc(const_ready, 1)
            nc.gpsimd.memset(mask[0:CHUNK, S - CHUNK:S], -NEG).then_inc(const_ready, 1)
            nc.gpsimd.memset(ones[:, :], 1.0).then_inc(const_ready, 1)
            nc.gpsimd.memset(mean_w[:, :], 1.0 / D).then_inc(const_ready, 1)
            nc.gpsimd.memset(eps_c[:, :], EPS).then_inc(const_ready, 1)
            nc.gpsimd.memset(slot[:, :, :], -1.0).then_inc(const_ready, 1)
            nc.gpsimd.memset(gate[:, :, :], 0.0).then_inc(const_ready, 1)
            nc.gpsimd.iota(iota_i[:, :], pattern=[[1, CAP]], base=0, channel_multiplier=0).then_inc(const_ready, 1)
            for half in range(2):
                nc.gpsimd.affine_select(out=both[:, :], in_=both[:, :], compare_op=ALU.not_equal, fill=1.0, base=-half * CAP,
                                        pattern=[[-1, CAP]], channel_multiplier=1).then_inc(const_ready, 1)
                pool.wait_ge(const_ready, 10 + half)
            nc.gpsimd.memset(u_sb[:, :, 0:PAD], 0.0).then_inc(u_zero, 1)
            pool.wait_ge(small_in, 16)
            pool.wait_ge(xn_ready, 2)
            for t in range(TT):
                nc.gpsimd.tensor_tensor(h[:, t, :], h[:, t, :], pw2_b_row, ALU.add).then_inc(hb_ready, 1)

        @block.scalar
        def _(act):
            for r, n, ap in row_loads:
                act.dma_start(rows[r:r + n, :], ap).then_inc(rows_in, 16)
            act.dma_start(dw_rows[0:CW, :], a["a_dw_w"][0]).then_inc(rows_in, 16)
            act.dma_start(inv_freq[:, :], a["inv_freq"].to_broadcast([P, HR])).then_inc(pos_in, 16)
            act.dma_start(pos_i[:, :], a["positions"][0].rearrange("(t p) -> p t", p=P), allow_slow_non_contiguous=True).then_inc(pos_in, 16)
            def norm(i):
                for t in range(TT):
                    if i == 0:
                        act.wait_ge(x_in, 16)
                        act.wait_ge(const_ready, 11)
                    else:
                        act.wait_ge(h_ready[i], 2 * t + 2)
                    nc.scalar.activation(xn[:, t, :], h[:, t, :], ACT.Square,
                                         accum_out=ss[:, t:t + 1]).then_inc(ssq, 1)
                act.wait_ge(ssq, 2 * i + 2)
                nc.scalar.activation(rms[:, 0:2], ss[:, 0:2], ACT.Sqrt, scale=1.0 / D, bias=eps_c[:, :]).then_inc(rms_ready, 1)

            norm(0)
            act.dma_start(pw2_b_row, a["a_pw2_b"].to_broadcast([P, D])).then_inc(small_in, 16)
            for l in range(L):
                act.dma_start(wr[:, l, :, 0:GROUPS], a["w_group"][l].rearrange("(k p) g -> p k g", p=P)).then_inc(small2_in, 16)
                act.dma_start(wr[:, l, :, GROUPS:NR], a["w_router"][l].rearrange("(k p) g -> p k g", p=P)).then_inc(small2_in, 16)
                act.dma_start(br[:, l, 0:GROUPS], a["b_group"][l:l + 1].to_broadcast([P, GROUPS])).then_inc(small2_in, 16)
                act.dma_start(br[:, l, GROUPS:NR], a["b_router"][l:l + 1].to_broadcast([P, NE])).then_inc(small2_in, 16)
            act.dma_start(qk_gr[:, 0, :], a["k_norm_g"][NOPE:QK].unsqueeze(0).to_broadcast([P, ROPE])).then_inc(small2_in, 16)
            act.dma_start(qk_gr[:, 1, :], a["q_norm_g"][0:1, NOPE:QK].to_broadcast([P, ROPE])).then_inc(small2_in, 16)
            act.wait_ge(ang_ready, 1)
            nc.scalar.activation(sin[:, :, :], ang[:, :, :], ACT.Sin).then_inc(trig, 1)
            nc.scalar.activation(cos[:, :, :], ang[:, :, :], ACT.Sin, scale=0.5).then_inc(trig, 1)
            act.wait_ge(cols_ready, 1)
            diags = iter(range(N_PE * CW))
            for m in range(KD):
                act.wait_ge(pw1_done, m + 1)
                if m >= 2:
                    act.wait_ge(u_ready, m - 1)
                nc.scalar.activation(sg[:, m % 2, :], bank[4 + m % 4][:, S:2 * S], ACT.Sigmoid,
                                     bias=col("pw1_b", KD + m)).then_inc(sg_ready, 1)
                if m in (1, 3, 5):
                    for _ in range(-(-N_PE * CW // 3)):
                        if (i := next(diags, None)) is not None:
                            nc.scalar.activation(diag(i), ident[:, :], ACT.Copy,
                                                 scale=dwT[:, KD - N_PE + i // CW, i % CW:i % CW + 1]).then_inc(diag_ready, 1)
            for m in range(KD):
                act.wait_ge(diff_ready, m + 1)
                nc.scalar.activation(xT[:, m, :], cv[:, m, :], ACT.Square).then_inc(sq_ready, 1)
            act.wait_ge(var_done, 1)
            nc.scalar.activation(std_t, bank[1][:, 0:S], ACT.Sqrt, bias=eps_c[:, :]).then_inc(lstd_ready, 1)
            for m in range(KD):
                act.wait_ge(dn_ready, m + 1)
                nc.scalar.activation(cv[:, m, :], cv[:, m, :], ACT.Silu, scale=col("ln_g", m), bias=col("ln_b", m)).then_inc(c_ready, 1)

            def experts(l):
                e = E[l]
                norm(1 + 2 * l)
                def high(it, first, last):
                    for c in range(first, last):
                        if c % 4 == 0:
                            act.wait_ge(e[f"unit_in{c // 4 + c // 8}"], 16 * it + 16)
                        if c % 8 >= SPLIT:
                            act.wait_ge(e["chunk_free"], 16 * it + 8 + c - SPLIT + 1)
                        elif c % 8 < 8 - SPLIT:
                            act.wait_ge(e["chunk_free"], 16 * it + c + SPLIT + 1)
                        nc.scalar.copy(w_hi[:, c % 8 % SPLIT, :], raw[:, raw_at(c), :]).then_inc(e["hi_ready"], 1)

                def rows_out(n):
                    act.wait_ge(e["chunk_free"], n)
                    for b in range(2):
                        nc.scalar.copy(u_rows[:, b * HALF:(b + 1) * HALF], bank[b][:, :]).then_inc(e["u_ready"], 1)

                def gated_high(n):
                    act.wait_ge(e["pair_done"], n)
                    act.wait_ge(e["pickT_ready"], n)
                    for b in range(2):
                        ins = nc.scalar.activation(y_hi[:, b * HALF:(b + 1) * HALF], bank[2 + b][:, :], ACT.Copy, scale=gate_c[:, :])
                    ins.then_inc(e["y_hi_ready"], 1)

                def tokens_out(n):
                    for b in range(2):
                        act.wait_ge(e["g_done"], 2 * n - 1 + b)
                        nc.scalar.copy(xg[:, b * HALF:(b + 1) * HALF], bank[4 + b][:, :]).then_inc(e["xg_ready"], 1)

                def silu(n):
                    act.wait_ge(e["sum_done"], 2 * n - 1)
                    nc.scalar.activation(sil[:, :, :], bank[0][:, 0:KF * CAP].rearrange("p (k c) -> p k c", k=KF),
                                         ACT.Silu).then_inc(e["silu_done"], 1)

                def tokens_high(n):
                    for b in range(2):
                        act.wait_ge(e["xtr_done"], 2 * n - 1 + b)
                        nc.scalar.copy(xs[:, :, 4 * b:4 * b + 4, 0:CAP].rearrange("p s k c -> p k s c"),
                                       bank[4 + b][:, :].rearrange("p (k s c) -> p k s c", k=4, s=2)).then_inc(e["xhi_ready"], 1)

                for t in range(TT):
                    act.wait_ge(xn_ready, 2 * (1 + l) + t + 1)
                    nc.scalar.copy(x_hi[:, t, :], xn[:, t, :]).then_inc(xh_ready, 1)
                act.wait_ge(gexp_in, l + 1)
                nc.scalar.activation(gex[:, :, :], gex[:, :, :], ACT.Exp).then_inc(gexp_ready, 1)
                high(0, 0, SPLIT - 1)
                act.wait_ge(eexp_in, l + 1)
                nc.scalar.activation(w2[:, :], w2[:, :], ACT.Exp).then_inc(eexp_ready, 1)
                high(0, SPLIT - 1, SPLIT)
                tokens_out(1)
                tokens_high(1)
                nc.scalar.activation(warm[:, :], eps_c[:, :], ACT.Silu)
                act.wait_ge(npairs_ready, l + 1)
                n_pairs = act.value_load(npairs_i[0:1, 0:1], min_val=PAIRS, max_val=PAIRS * PASSES)

                def pair(it):
                    gated_high(it + 1)
                    high(it, SPLIT, 8)
                    rows_out(16 * it + 16)
                    high(it, 8, 10)
                    silu(2 * it + 1)
                    act.wait_ge(e["back_done"], it + 1)
                    act.wait_ge(e["s_done"], 4 * it + 4)
                    nc.scalar.copy(gate_c[:, :], bank[4][:, S:S + 1])
                    nc.scalar.copy(pickT[:, :], bank[4][:, 0:S]).then_inc(e["pickT_ready"], 1)
                    high(it, 10, 16)
                    rows_out(16 * it + 24)
                    tokens_out(it + 2)
                    silu(2 * it + 2)
                    tokens_high(it + 2)

                pair(0)
                with act.Fori(1, n_pairs) as it:
                    high(it, 0, SPLIT)
                    pair(it)
                gated_high(n_pairs + 1)

            experts(0)

            norm(2)
            for b in range(4):
                act.wait_ge(xT_ready, 8 + b + 1)
                t, kh = b // 2, b % 2
                for j in range(4):
                    k = 4 * kh + j
                    ins = nc.scalar.activation(xT2[:, k, t * P:(t + 1) * P], bank[b][:, j * P:(j + 1) * P], ACT.Copy,
                                               scale=col("kv_norm_g", k))
                ins.then_inc(xT2_ready, 1)
            act.wait_ge(rn_ready, 3)
            for t in range(TT):
                act.wait_ge(c_done, t + 1)
                nc.scalar.activation(sc_junk(t, RQ), bank[6 + t][:, 0:RQ], ACT.Square, scale=rn[:, t:t + 1],
                                     accum_out=ss[:, 2 + t:3 + t]).then_inc(csq, 1)
            act.wait_ge(csq, 2)
            nc.scalar.activation(rms[:, 2:4], ss[:, 2:4], ACT.Sqrt, scale=1.0 / RQ, bias=eps_c[:, :]).then_inc(crms_ready, 1)
            for t in range(TT):
                act.wait_ge(c_done, 3 + t)
                nc.scalar.activation(sc_junk(2 + t, RKV), bank[4 + t][:, 0:RKV], ACT.Square, scale=rn[:, t:t + 1],
                                     accum_out=ss[:, t:t + 1]).then_inc(csq, 1)
                nc.scalar.activation(sc_junk(4 + t, ROPE), bank[4 + t][:, RKV:RKV + ROPE], ACT.Square, scale=rn[:, t:t + 1],
                                     accum_out=ss_kr[:, t:t + 1]).then_inc(csq, 1)
            act.wait_ge(csq, 6)
            nc.scalar.activation(rms[:, 0:2], ss[:, 0:2], ACT.Sqrt, scale=1.0 / RKV, bias=eps_c[:, :]).then_inc(crms_ready, 1)
            for t in range(TT):
                act.wait_ge(q_evac, 3 * t + 3)
                for hh in range(H):
                    i = t * H + hh
                    nc.scalar.activation(arena[:, 9216 + i * QK:9216 + (i + 1) * QK], q_h[:, t, hh, :], ACT.Square,
                                         accum_out=ss_h[:, 1, i:i + 1]).then_inc(qss_ready, 1)
            act.wait_ge(qss_ready, TT * H)
            nc.scalar.activation(r_h[:, 1, :], ss_h[:, 1, :], ACT.Sqrt, scale=1.0 / QK, bias=eps_c[:, :]).then_inc(qrms_ready, 1)
            act.wait_ge(kr_ready, 1)
            for t in range(TT):
                for ch in range(4):
                    act.wait_ge(kvmm_done, 4 * t + ch + 1)
                    src = bank[4 + ch][:, :].rearrange("p (h w d) -> p h w d", h=2, w=2)
                    for w in range(2):
                        i = t * H + 2 * ch + w
                        nc.scalar.activation(arena[:, 9216 + i * NOPE:9216 + (i + 1) * NOPE], src[:, w, 0, :], ACT.Square,
                                             accum_out=ss_h[:, 0, i:i + 1]).then_inc(kss_ready, 1)
                    nc.scalar.copy(k_tok[:, t, 2 * ch:2 * ch + 2, :], src[:, :, 0, :])
                    nc.scalar.copy(v_tok[:, t, 2 * ch:2 * ch + 2, :], src[:, :, 1, :]).then_inc(kv_evac, 1)
                act.wait_ge(kss_ready, (t + 1) * H)
                nc.scalar.activation(r_h[:, 0, t * H:(t + 1) * H], ss_h[:, 0, t * H:(t + 1) * H], ACT.Sqrt, scale=1.0 / QK,
                                     bias=ss_kr[:, t:t + 1]).then_inc(krms_ready, 1)
            for n in range(1, 16, 2):
                act.wait_ge(hd_tr, n + 1)
                dst, rot, g = head_block(n)
                if rot:
                    nc.scalar.copy(dst, bank[n % 8][0:ROPE, :].rearrange("p (h q) -> p h q", h=4)).then_inc(hd_act, 1)
                else:
                    nc.scalar.activation(dst, bank[n % 8][:, :].rearrange("p (h q) -> p h q", h=4), ACT.Copy,
                                         scale=g).then_inc(hd_act, 1)
            for t in range(TT):
                act.wait_ge(smax_ready, t + 1)
                for hh in range(H):
                    sc = (sc0 if t == 0 else sc1)[:, hh, :]
                    nc.scalar.activation(sc, sc, ACT.Exp, bias=smax[:, t, hh:hh + 1],
                                         accum_out=ssum[:, t, hh:hh + 1]).then_inc(exp_done, 1)
                for n in ((1,), (3, 5))[t]:
                    act.wait_ge(ptr_done, n + 1)
                    nc.scalar.copy(prob_block(n), bank[prob_bank(n)][:, :].rearrange("p (a q) -> p a q", a=4)).then_inc(pT_act, 1)
                act.wait_ge(o_done, 2 * t + 2)
                nc.scalar.copy(oT[:, 4:8, t * P:(t + 1) * P], bank[1][:, :].rearrange("p (h q) -> p h q", h=4)).then_inc(o_act, 1)

            experts(1)

        @block.tensor
        def _(pe):
            pe.wait_ge(const_ready, 11)
            pe.wait_ge(rows_in, 16 * (len(row_loads) + 1))
            nc.tensor.transpose(bank[7][:, 0:N_ROWS], rows[0:N_ROWS, :], ident[0:N_ROWS, 0:N_ROWS])
            for m in range(KD):
                ins = nc.tensor.transpose(bank[7][:, P + m * CW:P + (m + 1) * CW], dw_rows[0:CW, m * P:(m + 1) * P],
                                          ident[0:CW, 0:CW])
            ins.then_inc(cols_tr, 1)

            def norm(i):
                for b in range(4):
                    t, kh = b // 2, b % 2
                    if i == 0:
                        pe.wait_ge(xn_ready, t + 1)
                    else:
                        pe.wait_ge(h_ready[i], b + 1)
                    for j in range(4):
                        k = 4 * kh + j
                        ins = nc.tensor.transpose(bank[b][:, j * P:(j + 1) * P], (xn if i == 0 else h)[:, t, k * P:(k + 1) * P], ident[:, :])
                    ins.then_inc(tr_done, 1)

            norm(0)
            pe.wait_ge(cols_ready, 1)
            pe.wait_ge(xT_ready, 4)
            for m in range(KD):
                if m % 2 == 0:
                    pe.wait_ge(w_pw1[m], 16)
                    pe.wait_ge(w_pw1[m + 1], 16)
                if m >= 4:
                    pe.wait_ge(u_ready, m - 3)
                for part in range(2):
                    for k in range(KD):
                        ins = nc.tensor.matmul(bank[4 + m % 4][:, part * S:(part + 1) * S],
                                               pw1_sb[2 * (m // 2) + part][:, k, (m % 2) * P:(m % 2 + 1) * P],
                                               xT[:, k, :], start=(k == 0), stop=(k == KD - 1))
                ins.then_inc(pw1_done, 1)
            for i in range(N_PE * CW):
                m, w = KD - N_PE + i // CW, i % CW
                if w == 0:
                    pe.wait_ge(u_ready, m + 1)
                pe.wait_ge(diag_ready, i + 1)
                ins = nc.tensor.matmul(bank[2 + i // CW][:, 0:S], diag(i), u_sb[:, m, w:w + S], start=(w == 0), stop=(w == CW - 1))
                if w == CW - 1:
                    ins.then_inc(pe_conv_done, 1)
            for m in range(KD):
                pe.wait_ge(conv_done, m + 1)
                ins = nc.tensor.matmul(bank[0][:, 0:S], mean_w[:, :], cv[:, m, :], start=(m == 0), stop=(m == KD - 1))
            ins.then_inc(mean_done, 1)
            for m in range(KD):
                pe.wait_ge(sq_ready, m + 1)
                ins = nc.tensor.matmul(bank[1][:, 0:S], mean_w[:, :], xT[:, m, :], start=(m == 0), stop=(m == KD - 1))
            ins.then_inc(var_done, 1)
            pe.wait_ge(w_pw2, 16)
            pe.wait_ge(u_ready, KD)
            for k in range(KD):
                pe.wait_ge(c_ready, k + 1)
                for j in range(4):
                    t, hf = j // 2, j % 2
                    ins = nc.tensor.matmul(bank[4 + j][:, :], cv[:, k, t * P:(t + 1) * P],
                                           pw2_sb[:, k, hf * HALF:(hf + 1) * HALF], start=(k == 0), stop=(k == KD - 1))
                    if k == KD - 1:
                        ins.then_inc(pw2_done, 1)

            def experts(l):
                e = E[l]
                norm(1 + 2 * l)
                if l == 0:
                    pe.wait_ge(small2_in, 16 * (4 * L + 2))
                pe.wait_ge(xT_ready, 4 * (2 + 2 * l))
                for t in range(TT):
                    for k in range(KD):
                        ins = nc.tensor.matmul(bank[4][:, t * CAP:t * CAP + NR], xT[:, k, t * P:(t + 1) * P], wr[:, l, k, :],
                                               start=(k == 0), stop=(k == KD - 1))
                ins.then_inc(logits_done, 1)
                pe.wait_ge(mask_ready, l + 1)
                nc.tensor.matmul(bank[5][:, 0:NE], upto[:, :], picked[:, 0, :], start=True, stop=True)
                nc.tensor.matmul(bank[5][:, NE:2 * NE], ones[:, :], picked[:, 0, :], start=True, stop=False)
                nc.tensor.matmul(bank[5][:, NE:2 * NE], upto[:, :], picked[:, 1, :], start=False, stop=True).then_inc(pos_done, 1)
                nc.tensor.matmul(bank[6][:, 0:NE], ones[:, :], picked[:, 0, :], start=True, stop=False)
                nc.tensor.matmul(bank[6][:, 0:NE], ones[:, :], picked[:, 1, :], start=False, stop=True).then_inc(count_done, 1)

                def gather(n):
                    pe.wait_ge(e["pick_ready"], n)
                    for b in range(2):
                        for i, (t, part) in enumerate(((0, x_hi), (0, x_lo), (1, x_hi), (1, x_lo))):
                            ins = nc.tensor.matmul(bank[4 + b][:, :], pick[:, t, :], part[:, t, b * HALF:(b + 1) * HALF],
                                                   start=(i == 0), stop=(i == 3))
                        ins.then_inc(e["g_done"], 1)

                def tokens_across(n):
                    for k in range(KD):
                        if k % 4 == 0:
                            pe.wait_ge(e["xg_ready"], 2 * n - 1 + k // 4)
                        ins = nc.tensor.transpose(bank[4 + k // 4][:, (k % 4) * P:(k % 4 + 1) * P], xg[:, k * P:(k + 1) * P],
                                                  ident[:, :])
                        if k % 4 == 3:
                            ins.then_inc(e["xtr_done"], 1)

                def gate_up(it, stationary, first, last):
                    for c in range(first, last):
                        pe.wait_ge(e["lo_ready"], 16 * it + c + 1)
                        for part in (w_hi, w_lo):
                            for b in range(2):
                                ins = nc.tensor.matmul(bank[b][:, :], stationary[:, c - first, :],
                                                       part[:, c % 8 % SPLIT, b * HALF:(b + 1) * HALF],
                                                       start=(c == first and part is w_hi), stop=(c == last - 1 and part is w_lo))
                        ins.then_inc(e["chunk_free"], 1)

                def down(s, done):
                    for k in range(KF):
                        for b in range(2):
                            ins = nc.tensor.matmul(bank[2 + b][:, :], hid[:, s, k, :], raw[:, 12 * s + 2 * KF + k, b * HALF:(b + 1) * HALF],
                                                   start=(s == 0 and k == 0), stop=(s == 1 and k == KF - 1))
                    ins.then_inc(done, 1)

                def add_parts(n):
                    for half in range(2):
                        pe.wait_ge(e["u_ready"], 2 * n - 1 + half)
                        for m in range(KF):
                            c = half * HALF + m * P
                            ins = nc.tensor.matmul(bank[half][:, m * CAP:(m + 1) * CAP], u_rows[:, c:c + P], both[:, :],
                                                   start=True, stop=True)
                        ins.then_inc(e["sum_done"], 1)

                def scatter(j, it, added, base):
                    t, hf = j // 2, j % 2
                    if j == 0:
                        pe.wait_ge(e["y_ready"], it + 1)
                    if j >= 2:
                        pe.wait_ge(added, base + j - 1)
                    for y in (y_hi, y_lo):
                        ins = nc.tensor.matmul(bank[6 + j % 2][:, :], pickT[:, t * P:(t + 1) * P],
                                               y[:, hf * HALF:(hf + 1) * HALF], start=(y is y_hi), stop=(y is y_lo))
                    ins.then_inc(e["s_done"], 1)

                def way_back(n):
                    for t in range(TT):
                        nc.tensor.transpose(bank[4][:, t * P:(t + 1) * P], pick[:, t, :].bitcast(F32), ident[:, :])
                    pe.wait_ge(e["pw_ready"], n)
                    for t in range(TT):
                        ins = nc.tensor.matmul(bank[4][:, S:S + 1], pw[:, t, :], ones[:, 0:1], start=(t == 0), stop=(t == TT - 1))
                    ins.then_inc(e["back_done"], 1)

                pe.wait_ge(xsplit_ready, 2 * l + 2)
                gather(1)
                tokens_across(1)
                pe.wait_ge(npairs_ready, l + 1)
                n_pairs = pe.value_load(npairs_i[0:1, 0:1], min_val=PAIRS, max_val=PAIRS * PASSES)
                with pe.Fori(0, n_pairs) as it:
                    pe.wait_ge(e["xs_ready"], it + 1)
                    gate_up(it, xs[:, 0, :, :], 0, 8)
                    scatter(0, it, e["s_added"], 4 * it)
                    scatter(1, it, e["s_added"], 4 * it)
                    way_back(it + 1)
                    add_parts(2 * it + 1)
                    scatter(2, it, e["s_added"], 4 * it)
                    scatter(3, it, e["s_added"], 4 * it)
                    pe.wait_ge(e["unit_in2"], 16 * it + 16)
                    pe.wait_ge(e["hid_ready"], 2 * it + 1)
                    down(0, e["down_done"])
                    gate_up(it, xs[:, 1, :, :], 8, 16)
                    pe.wait_ge(e["pickT_ready"], it + 2)
                    gather(it + 2)
                    add_parts(2 * it + 2)
                    tokens_across(it + 2)
                    pe.wait_ge(e["unit_in5"], 16 * it + 16)
                    pe.wait_ge(e["hid_ready"], 2 * it + 2)
                    down(1, e["pair_done"])
                for j in range(4):
                    scatter(j, n_pairs, h_ready[2 + 2 * l], 0)

            experts(0)

            norm(2)
            pe.wait_ge(w_c, 48)

            def latents_across(src, t_banks, n):
                for k in range(n):
                    for t in range(TT):
                        ins = nc.tensor.transpose(bank[t_banks + k // 2][:, (2 * (k % 2) + t) * P:(2 * (k % 2) + t + 1) * P],
                                                  src[:, t, k * P:(k + 1) * P], ident[:, :])
                    if k % 2 == 1 or k == n - 1:
                        ins.then_inc(ctr_done, 1)

            pe.wait_ge(xT_ready, 12)
            for t in range(TT):
                for k in range(KD):
                    ins = nc.tensor.matmul(bank[6 + t][:, 0:RQ], xT[:, k, t * P:(t + 1) * P], w_dq_sb[:, k, :],
                                           start=(k == 0), stop=(k == KD - 1))
                ins.then_inc(c_done, 1)
            pe.wait_ge(xT2_ready, 4)
            for t in range(TT):
                for k in range(KD):
                    ins = nc.tensor.matmul(bank[4 + t][:, 0:RKV + ROPE], xT2[:, k, t * P:(t + 1) * P], w_dkvr_sb[:, k, :],
                                           start=(k == 0), stop=(k == KD - 1))
                ins.then_inc(c_done, 1)
                if t == 0:
                    pe.wait_ge(cn_ready, 2)
                    latents_across(cq_n, 1, RQ // P)
            pe.wait_ge(w_uq, 16)
            pe.wait_ge(cT_ready, 2)
            for i in range(6):
                t, ch = i // 3, i % 3
                if i == 3:
                    pe.wait_ge(cn_ready, 4)
                    latents_across(ckv_n, 6, RKV // P)
                if i >= 4:
                    pe.wait_ge(q_evac, i - 3)
                for k in range(RQ // P):
                    ins = nc.tensor.matmul(bank[i % 4][:, :], cqT[:, k, t * P:(t + 1) * P],
                                           w_uq_sb[:, k, ch * HALF:(ch + 1) * HALF], start=(k == 0), stop=(k == RQ // P - 1))
                ins.then_inc(qmm_done, 1)
            pe.wait_ge(w_ukv, 16)
            pe.wait_ge(cT_ready, 3)
            for i in range(8):
                t, ch = i // 4, i % 4
                if i >= 4:
                    pe.wait_ge(kv_evac, i - 3)
                for k in range(RKV // P):
                    ins = nc.tensor.matmul(bank[4 + i % 4][:, :], ckvT[:, k, t * P:(t + 1) * P],
                                           w_ukv_sb[:, k, ch * HALF:(ch + 1) * HALF], start=(k == 0), stop=(k == RKV // P - 1))
                ins.then_inc(kvmm_done, 1)
            pe.wait_ge(q_evac, 6)
            for n in range(16):
                kind, t, hg = n // 4, (n % 4) // 2, n % 2
                if n == 0:
                    pe.wait_ge(q_ready, 1)
                if n == 4:
                    pe.wait_ge(kv_evac, 8)
                if n == 8:
                    pe.wait_ge(k_ready, 1)
                if n >= 8:
                    pe.wait_ge(hd_dve if n % 2 == 0 else hd_act, (n - 8) // 2 + 1)
                for j in range(4):
                    hh = 4 * hg + j
                    src = (q_h[:, t, hh, 0:NOPE], qrr[:, t, hh, :], k_tok[:, t, hh, :], krh[:, t, hh, :])[kind]
                    ins = nc.tensor.transpose(bank[n % 8][0:src.shape[1], j * P:(j + 1) * P], src, ident[:, :])
                ins.then_inc(hd_tr, 1)
            pe.wait_ge(hd_dve, 8)
            pe.wait_ge(hd_act, 8)
            for t in range(TT):
                nk = (t + 1) * P
                for hh in range(H):
                    b = hh // 4 if t == 0 else 2 + hh // 2
                    c = (hh % 4) * P if t == 0 else (hh % 2) * S
                    nc.tensor.matmul(bank[b][:, c:c + nk], qTn[:, hh, t * P:(t + 1) * P], kTn[:, hh, 0:nk], start=True, stop=False)
                    ins = nc.tensor.matmul(bank[b][:, c:c + nk], qTr[0:ROPE, hh, t * P:(t + 1) * P], kTr[0:ROPE, hh, 0:nk],
                                           start=False, stop=True)
                    if hh % (4 if t == 0 else 2) == (3 if t == 0 else 1):
                        ins.then_inc(sc_done, 1)
            for t in range(TT):
                pe.wait_ge(p_ready, t + 1)
                for n in ((0, 1), (2, 3, 4, 5))[t]:
                    for j in range(4):
                        src = sc0[:, 4 * n + j, :] if n < 2 else sc1[:, 2 * (n - 2) + j // 2, (j % 2) * P:(j % 2 + 1) * P]
                        ins = nc.tensor.transpose(bank[prob_bank(n)][:, j * P:(j + 1) * P], src, ident[:, :])
                    ins.then_inc(ptr_done, 1)
                pe.wait_ge(pT_dve, 1 + 2 * t)
                pe.wait_ge(pT_act, 1 + 2 * t)
                for hh in range(H):
                    for kt in range(t + 1):
                        ins = nc.tensor.matmul(bank[hh // 4][:, (hh % 4) * P:(hh % 4 + 1) * P], v_tok[:, kt, hh, :],
                                               pT0[:, hh, :] if t == 0 else pT1[:, hh, kt, :],
                                               start=(kt == 0), stop=(kt == t))
                    if hh % 4 == 3:
                        ins.then_inc(o_done, 1)
                if t == 0:
                    pe.wait_ge(w_o, 16)
                pe.wait_ge(o_dve, t + 1)
                pe.wait_ge(o_act, t + 1)
                for hf in range(2):
                    for hh in range(H):
                        ins = nc.tensor.matmul(bank[wo_bank(2 * t + hf)][:, :], oT[:, hh, t * P:(t + 1) * P],
                                               w_o_sb[:, hh, hf * HALF:(hf + 1) * HALF], start=(hh == 0), stop=(hh == H - 1))
                    ins.then_inc(wo_done, 1)

            experts(1)

        @block.vector
        def _(dve):
            dve_n = [0]
            V = nc.vector

            def link(ins):
                dve_n[0] += 1
                ins.then_inc(dve_step, 1)
                dve.wait_ge(dve_step, dve_n[0])

            dve.wait_ge(const_ready, 11)
            link(V.tensor_copy(iota[:, :], iota_i[:, :]))
            V.tensor_scalar(iota_m[:, :], iota[:, :], -float(CAP), None, ALU.add)
            dve.wait_ge(cols_tr, 1)
            V.tensor_copy(cols[:, 0:N_ROWS], bank[7][:, 0:N_ROWS])
            V.tensor_copy(dwT[:, :, :], bank[7][:, P:P + KD * CW].rearrange("p (m w) -> p m w", m=KD)).then_inc(cols_ready, 1)
            dve.wait_ge(cols_ready, 1)

            def across(i, g):
                for b in range(4):
                    t, kh = b // 2, b % 2
                    dve.wait_ge(tr_done, 4 * i + b + 1)
                    V.tensor_tensor(xT[:, 4 * kh:4 * kh + 4, t * P:(t + 1) * P], bank[b][:, :].rearrange("p (k q) -> p k q", k=4),
                                    over(col(g, 4 * kh, 4), P), ALU.mult).then_inc(xT_ready, 1)

            def inverse_rms(i):
                dve.wait_ge(rms_ready, i + 1)
                V.reciprocal(rn[:, :], rms[:, 0:2]).then_inc(rn_ready, 1)

            inverse_rms(0)
            dve.wait_ge(rn_ready, 1)
            for t in range(TT):
                V.tensor_scalar(xn[:, t, :], h[:, t, :], rn[:, t:t + 1], None, ALU.mult).then_inc(xn_ready, 1)
            across(0, "a_norm_g")
            MAGIC = 1.5 * 2.0 ** 23
            TWO_PI = 2.0 * np.pi
            p1 = float(np.float32(np.floor(TWO_PI * 2 ** 8) / 2 ** 8))
            p2 = float(np.floor((TWO_PI - p1) * 2 ** 20) / 2 ** 20)
            p3 = float(np.float32(TWO_PI - p1 - p2))
            dve.wait_ge(pos_in, 32)
            link(V.tensor_copy(pos_f[:, :], pos_i[:, :]))
            for t in range(TT):
                ins = V.tensor_scalar(ang[:, t, :], inv_freq[:, :], pos_f[:, t:t + 1], None, ALU.mult)
            link(ins)
            link(V.tensor_scalar(ang_k[:, :, :], ang[:, :, :], 1.0 / TWO_PI, None, ALU.mult))
            link(V.tensor_scalar(ang_k[:, :, :], ang_k[:, :, :], MAGIC, None, ALU.add))
            link(V.tensor_scalar(ang_k[:, :, :], ang_k[:, :, :], -MAGIC, None, ALU.add))
            for part in (p1, p2):
                link(V.scalar_tensor_tensor(out=ang[:, :, :], in0=ang_k[:, :, :], scalar=-part, in1=ang[:, :, :],
                                            op0=ALU.mult, op1=ALU.add))
            link(V.scalar_tensor_tensor(out=ang[:, :, :], in0=ang_k[:, :, :], scalar=-p3, in1=ang[:, :, :],
                                        op0=ALU.mult, op1=ALU.add))
            PI_IN = float(np.nextafter(np.float32(np.pi), np.float32(0)))
            V.tensor_scalar(ang[:, :, :], ang[:, :, :], PI_IN, -PI_IN, ALU.min, ALU.max).then_inc(ang_ready, 1)

            dve.wait_ge(u_zero, 1)
            def glu(m):
                dve.wait_ge(sg_ready, m + 1)
                V.scalar_tensor_tensor(out=u_sb[:, m, PAD:PAD + S], in0=bank[4 + m % 4][:, 0:S], scalar=col("pw1_b", m),
                                       in1=sg[:, m % 2, :], op0=ALU.add, op1=ALU.mult).then_inc(u_ready, 1)

            taps, last_tap = 0, {}
            for m0 in range(0, KD - N_PE, 2):
                if m0 < KD - N_PE - 2:
                    glu(m0)
                    glu(m0 + 1)
                dve.wait_ge(u_ready, m0 + 2)
                for w in range(CW):
                    if m0 == KD - N_PE - 4 and w == 20:
                        for m in range(m0 + 2, KD):
                            glu(m)
                    for m in (m0, m0 + 1):
                        if w == 0:
                            ins = V.tensor_scalar(cv[:, m, :], u_sb[:, m, 0:S], dwT[:, m, 0:1], col("dw_b", m), ALU.mult, ALU.add)
                        else:
                            dve.wait_ge(tap_done, last_tap[m])
                            ins = V.scalar_tensor_tensor(out=cv[:, m, :], in0=u_sb[:, m, w:w + S], scalar=dwT[:, m, w:w + 1],
                                                         in1=cv[:, m, :], op0=ALU.mult, op1=ALU.add)
                        if w < CW - 1:
                            ins.then_inc(tap_done, 1)
                            taps += 1
                            last_tap[m] = taps
                        else:
                            ins.then_inc(conv_done, 1)
            for i in range(N_PE):
                m = KD - N_PE + i
                dve.wait_ge(pe_conv_done, i + 1)
                V.tensor_scalar(cv[:, m, :], bank[2 + i][:, 0:S], col("dw_b", m), None, ALU.add).then_inc(conv_done, 1)
            dve.wait_ge(mean_done, 1)
            dve.wait_ge(conv_done, KD)
            for m in range(KD):
                V.tensor_tensor(cv[:, m, :], cv[:, m, :], bank[0][:, 0:S], ALU.subtract).then_inc(diff_ready, 1)
            dve.wait_ge(lstd_ready, 1)
            link(V.reciprocal(rstd_t, std_t))
            for m in range(KD):
                V.tensor_tensor(cv[:, m, :], cv[:, m, :], rstd_t, ALU.mult).then_inc(dn_ready, 1)
            dve.wait_ge(hb_ready, 2)
            for j in range(4):
                t, hf = j // 2, j % 2
                dve.wait_ge(pw2_done, j + 1)
                V.tensor_tensor(h[:, t, hf * HALF:(hf + 1) * HALF], bank[4 + j][:, :], h[:, t, hf * HALF:(hf + 1) * HALF],
                                ALU.add).then_inc(h_ready[1], 1)

            def experts(l):
                e = E[l]
                across(1 + 2 * l, f"ffn_norm_g{l}")
                inverse_rms(1 + 2 * l)
                dve.wait_ge(rn_ready, 2 + 2 * l)
                dve.wait_ge(gain_in, 16 * (l + 1))
                for t in range(TT):
                    V.scalar_tensor_tensor(out=xn[:, t, :], in0=h[:, t, :], scalar=rn[:, t:t + 1], in1=gain,
                                           op0=ALU.mult, op1=ALU.mult).then_inc(xn_ready, 1)
                def tokens_split(t):
                    dve.wait_ge(xh_ready, 2 * l + t + 1)
                    V.tensor_tensor(x_lo[:, t, :], xn[:, t, :], x_hi[:, t, :], ALU.subtract).then_inc(xsplit_ready, 1)

                V.memset(gate_c[:, :], 0.0)
                V.tensor_scalar(pickT[:, :], mask[:, :], 0.0, None, ALU.mult).then_inc(e["pickT_ready"], 1)
                V.memset(bank[2][:, :], 0.0)
                V.memset(bank[3][:, :], 0.0).then_inc(e["pair_done"], 1)
                V.memset(cmx[:, 0:1], 0.0).then_inc(e["chunk_free"], 8)
                tokens_split(0)
                G = GROUPS
                dve.wait_ge(logits_done, l + 1)
                for t in range(TT):
                    ins = V.scalar_tensor_tensor(out=lg[:, t, :], in0=bank[4][:, t * CAP:t * CAP + NR], scalar=rn[:, t:t + 1],
                                                 in1=br[:, l, :], op0=ALU.mult, op1=ALU.add)
                link(ins)
                link(V.tensor_reduce(gmx[:, :], lg[:, :, 0:G], AX_X, ALU.max))
                V.tensor_tensor(gex[:, :, :], lg[:, :, 0:G], over(gmx[:, :], G), ALU.subtract).then_inc(gexp_in, 1)
                link(V.tensor_tensor(geq[:, :, :], lg[:, :, 0:G], over(gmx[:, :], G), ALU.is_equal))
                link(V.tensor_tensor(geq[:, :, :], geq[:, :, :], iota_m[:, 0:G].unsqueeze(1).to_broadcast([P, TT, G]), ALU.mult))
                link(V.tensor_reduce(gix[:, :], geq[:, :, :], AX_X, ALU.min))
                link(V.tensor_tensor(geq[:, :, :], iota_m[:, 0:G].unsqueeze(1).to_broadcast([P, TT, G]), over(gix[:, :], G), ALU.is_equal))
                link(V.tensor_scalar(geq[:, :, :], geq[:, :, :], NEG, -NEG, ALU.mult, ALU.add))
                link(V.tensor_tensor(em[:, :, :].rearrange("p t (g x) -> p t g x", g=G),
                                     lg[:, :, G:NR].rearrange("p t (g x) -> p t g x", g=G),
                                     geq[:, :, :].unsqueeze(3).to_broadcast([P, TT, G, EG]), ALU.add))
                im = iota_m[:, 0:NE].unsqueeze(1).to_broadcast([P, TT, NE])
                for mx, oh in ((mx1, oh1), (mx2, oh2)):
                    link(V.tensor_reduce(mx[:, :], em[:, :, :], AX_X, ALU.max))
                    link(V.tensor_tensor(eeq[:, :, :], em[:, :, :], over(mx[:, :], NE), ALU.is_equal))
                    link(V.tensor_tensor(eeq[:, :, :], eeq[:, :, :], im, ALU.mult))
                    link(V.tensor_reduce(eix[:, :], eeq[:, :, :], AX_X, ALU.min))
                    link(V.tensor_tensor(oh[:, :, :], im, over(eix[:, :], NE), ALU.is_equal))
                    if mx is mx1:
                        link(V.scalar_tensor_tensor(out=em[:, :, :], in0=oh[:, :, :], scalar=-2 * NEG, in1=em[:, :, :],
                                                    op0=ALU.mult, op1=ALU.add))
                V.tensor_tensor(picked[:, :, :], oh1[:, :, :], oh2[:, :, :], ALU.add).then_inc(mask_ready, 1)
                V.tensor_tensor(w2[:, :], mx2[:, :], mx1[:, :], ALU.subtract).then_inc(eexp_in, 1)
                tokens_split(1)
                dve.wait_ge(pos_done, l + 1)
                link(V.tensor_tensor(eeq[:, :, :], bank[5][:, 0:TT * NE].rearrange("p (t x) -> p t x", t=TT), picked[:, :, :], ALU.mult))
                for q in range(PASSES):
                    ins = V.tensor_scalar(slot[:, :, q * NE:(q + 1) * NE], eeq[:, :, :], -1.0 - q * CAP, None, ALU.add)
                link(ins)

                def low(it, first, last):
                    for c in range(first, last):
                        dve.wait_ge(e["hi_ready"], 16 * it + c + 1)
                        V.tensor_tensor(w_lo[:, c % 8 % SPLIT, :], raw[:, raw_at(c), :], w_hi[:, c % 8 % SPLIT, :],
                                        ALU.subtract).then_inc(e["lo_ready"], 1)

                def one_hot(n):
                    for s in range(2):
                        for t in range(TT):
                            ins = V.tensor_scalar(pick[:, t, s * CAP:(s + 1) * CAP], iota[:, :],
                                                  slot[:, t, bass.ds(2 * n + s, 1)], None, ALU.is_equal)
                    ins.then_inc(e["pick_ready"], 1)

                def gated(n):
                    for s in range(2):
                        for t in range(TT):
                            ins = V.tensor_scalar(pw[:, t, s * CAP:(s + 1) * CAP], iota[:, :],
                                                  slot[:, t, bass.ds(2 * n + s, 1)], gate[:, t, bass.ds(2 * n + s, 1)],
                                                  ALU.is_equal, ALU.mult)
                    ins.then_inc(e["pw_ready"], 1)

                def tokens_low(n):
                    for b in range(2):
                        dve.wait_ge(e["xhi_ready"], 2 * n - 1 + b)
                        ins = V.tensor_tensor(xs[:, :, 4 * b:4 * b + 4, CAP:PAIR].rearrange("p s k c -> p k s c"),
                                              bank[4 + b][:, :].rearrange("p (k s c) -> p k s c", k=4, s=2),
                                              xs[:, :, 4 * b:4 * b + 4, 0:CAP].rearrange("p s k c -> p k s c"), ALU.subtract)
                    ins.then_inc(e["xs_ready"], 1)

                def hidden(n, s):
                    dve.wait_ge(e["silu_done"], n)
                    dve.wait_ge(e["sum_done"], 2 * n)
                    V.tensor_tensor(hid[:, s, :, s * CAP:(s + 1) * CAP], sil[:, :, :],
                                    bank[1][:, 0:KF * CAP].rearrange("p (k c) -> p k c", k=KF),
                                    ALU.mult).then_inc(e["hid_ready"], 1)

                def gated_low(n):
                    dve.wait_ge(e["y_hi_ready"], n)
                    for b in range(2):
                        ins = V.scalar_tensor_tensor(out=y_lo[:, b * HALF:(b + 1) * HALF], in0=bank[2 + b][:, :], scalar=gate_c[:, :],
                                                     in1=y_hi[:, b * HALF:(b + 1) * HALF], op0=ALU.mult, op1=ALU.subtract)
                    ins.then_inc(e["y_ready"], 1)

                def add_scattered(j, it, added):
                    t, hf = j // 2, j % 2
                    dve.wait_ge(e["s_done"], 4 * it + 1 + j)
                    V.tensor_tensor(h[:, t, hf * HALF:(hf + 1) * HALF], bank[6 + j % 2][:, :],
                                    h[:, t, hf * HALF:(hf + 1) * HALF], ALU.add).then_inc(added, 1)

                one_hot(0)
                dve.wait_ge(count_done, l + 1)
                link(V.tensor_reduce(cmx[:, 0:1], bank[6][:, 0:NE], AX_X, ALU.max))
                for q in range(1, PASSES):
                    link(V.tensor_scalar(cmx[:, q:q + 1], cmx[:, 0:1], q * CAP + 0.5, float(PAIRS), ALU.is_ge, ALU.mult))
                link(V.tensor_reduce(cmx[:, 0:1], cmx[:, 1:PASSES], AX_X, ALU.add))
                V.tensor_scalar(npairs_i[:, :], cmx[:, 0:1], float(PAIRS), None, ALU.add).then_inc(npairs_ready, 1)
                low(0, 0, SPLIT)
                tokens_low(1)
                dve.wait_ge(gexp_ready, l + 1)
                link(V.tensor_reduce(gsm[:, :], gex[:, :, :], AX_X, ALU.add))
                link(V.reciprocal(gw[:, :], gsm[:, :]))
                dve.wait_ge(eexp_ready, l + 1)
                link(V.tensor_scalar(w1[:, :], w2[:, :], 1.0, None, ALU.add))
                link(V.reciprocal(w1[:, :], w1[:, :]))
                link(V.tensor_tensor(w1[:, :], w1[:, :], gw[:, :], ALU.mult))
                link(V.tensor_tensor(w2[:, :], w1[:, :], w2[:, :], ALU.mult))
                link(V.tensor_tensor(oh1[:, :, :], oh1[:, :, :], over(w1[:, :], NE), ALU.mult))
                link(V.tensor_tensor(oh2[:, :, :], oh2[:, :, :], over(w2[:, :], NE), ALU.mult))
                link(V.tensor_tensor(oh1[:, :, :], oh1[:, :, :], oh2[:, :, :], ALU.add))
                for q in range(PASSES):
                    ins = V.tensor_copy(gate[:, :, q * NE:(q + 1) * NE], oh1[:, :, :])
                link(ins)
                for s in range(2):
                    V.memset(hid[:, s, :, (1 - s) * CAP:(2 - s) * CAP], 0.0)
                dve.wait_ge(npairs_ready, l + 1)
                n_pairs = dve.value_load(npairs_i[0:1, 0:1], min_val=PAIRS, max_val=PAIRS * PASSES)

                def pair(it):
                    gated(it)
                    low(it, SPLIT, 8)
                    gated_low(it + 1)
                    add_scattered(0, it, e["s_added"])
                    add_scattered(1, it, e["s_added"])
                    low(it, 8, 9)
                    hidden(2 * it + 1, 0)
                    add_scattered(2, it, e["s_added"])
                    add_scattered(3, it, e["s_added"])
                    low(it, 9, 13)
                    dve.wait_ge(e["back_done"], it + 1)
                    one_hot(it + 1)
                    low(it, 13, 16)
                    hidden(2 * it + 2, 1)
                    tokens_low(it + 2)

                pair(0)
                with dve.Fori(1, n_pairs) as it:
                    low(it, 0, SPLIT)
                    pair(it)
                gated_low(n_pairs + 1)
                for j in range(4):
                    add_scattered(j, n_pairs, h_ready[2 + 2 * l])

            experts(0)

            across(2, "b_norm_g")
            inverse_rms(2)
            dve.wait_ge(trig, 2)
            link(V.tensor_tensor(cos[:, :, :], cos[:, :, :], cos[:, :, :], ALU.mult))
            link(V.tensor_scalar(cos[:, :, :], cos[:, :, :], -2.0, 1.0, ALU.mult, ALU.add))
            dve.wait_ge(crms_ready, 1)
            link(V.reciprocal(rr[:, 2:4], rms[:, 2:4]))
            for t in range(TT):
                V.tensor_scalar(cq_n[:, t, :], bank[6 + t][:, 0:RQ], rn[:, t:t + 1], rr[:, 2 + t:3 + t], ALU.mult,
                                ALU.mult).then_inc(cn_ready, 1)

            def latents(dst, b, g, w, n):
                dve.wait_ge(ctr_done, n)
                V.tensor_tensor(dst, bank[b][:, 0:w * S].rearrange("p (k q) -> p k q", k=w), over(g, S), ALU.mult).then_inc(cT_ready, 1)

            latents(cqT[:, 0:2, :], 1, col("q_latent_g", 0, 2), 2, 1)
            latents(cqT[:, 2:3, :], 2, col("q_latent_g", 2, 1), 1, 2)
            dve.wait_ge(crms_ready, 2)
            link(V.reciprocal(rr[:, 0:2], rms[:, 0:2]))
            for t in range(TT):
                V.tensor_scalar(kr_raw[:, t, :], bank[4 + t][:, RKV:RKV + ROPE], rn[:, t:t + 1], None, ALU.mult)
                V.tensor_scalar(ckv_n[:, t, :], bank[4 + t][:, 0:RKV], rn[:, t:t + 1], rr[:, t:t + 1], ALU.mult,
                                ALU.mult).then_inc(cn_ready, 1)
            V.tensor_scalar(ss_kr[:, :], ss_kr[:, :], 1.0 / QK, EPS, ALU.mult, ALU.add).then_inc(kr_ready, 1)

            def rotate(dst, src, shape, tmp):
                def like(x):
                    return x if len(shape) == 3 else x.unsqueeze(2).to_broadcast([P, TT, H, HR])
                lo, hi = (slice(0, HR), slice(HR, ROPE))
                pick_ = (lambda x, s: x[:, :, s]) if len(shape) == 3 else (lambda x, s: x[:, :, :, s])
                c, s_ = like(cos[:, :, :]), like(sin[:, :, :])
                x1, x2 = pick_(src, lo), pick_(src, hi)
                V.tensor_tensor(tmp[0], x1, c, ALU.mult)
                V.tensor_tensor(tmp[1], x2, s_, ALU.mult)
                V.tensor_tensor(tmp[2], x1, s_, ALU.mult)
                link(V.tensor_tensor(tmp[3], x2, c, ALU.mult))
                V.tensor_tensor(pick_(dst, lo), tmp[0], tmp[1], ALU.subtract)
                link(V.tensor_tensor(pick_(dst, hi), tmp[2], tmp[3], ALU.add))

            def q_out(i):
                t, ch = i // 3, i % 3
                dve.wait_ge(qmm_done, i + 1)
                V.tensor_copy(q_tok[:, t, ch * HALF:(ch + 1) * HALF], bank[i % 4][:, :]).then_inc(q_evac, 1)

            q_out(0)
            q_out(1)
            dve.wait_ge(cn_ready, 4)
            link(V.tensor_tensor(kr_raw, kr_raw, qk_gr[:, 0, :].unsqueeze(1).to_broadcast([P, TT, ROPE]), ALU.mult))
            rotate(kr_rot, kr_raw, (P, TT, HR), [t[:, :, 0, :] for t in rot_tmp])
            q_out(2)
            latents(ckvT, 6, col("kv_latent_g", 0, 2), 2, 3)
            for i in range(3, 6):
                q_out(i)
            dve.wait_ge(qrms_ready, 1)
            link(V.reciprocal(r_h[:, 1, :], r_h[:, 1, :]))
            q_all = q_tok.rearrange("p t (h c) -> p (t h) c", h=H)
            link(V.tensor_tensor(q_all, q_all, over(r_h[:, 1, :], QK), ALU.mult))
            q_r = q_h[:, :, :, NOPE:QK]
            link(V.tensor_tensor(q_r, q_r, qk_gr[:, 1, :].unsqueeze(1).unsqueeze(1).to_broadcast([P, TT, H, ROPE]), ALU.mult))
            rotate(qrr, q_r, (P, TT, H, HR), rot_tmq)
            V.memset(cmx[:, 0:1], 0.0).then_inc(q_ready, 1)
            for t in range(TT):
                dve.wait_ge(krms_ready, t + 1)
                dve.wait_ge(kv_evac, 4 * t + 4)
                rk = r_h[:, 0, t * H:(t + 1) * H]
                link(V.reciprocal(rk, rk))
                V.tensor_tensor(k_tok[:, t, :, :], k_tok[:, t, :, :], over(rk, NOPE), ALU.mult)
                ins = V.tensor_tensor(krh[:, t, :, :], kr_rot[:, t, :].unsqueeze(1).to_broadcast([P, H, ROPE]), over(rk, ROPE), ALU.mult)
            ins.then_inc(k_ready, 1)
            for n in range(0, 16, 2):
                dve.wait_ge(hd_tr, n + 1)
                dst, rot, g = head_block(n)
                if rot:
                    V.tensor_copy(dst, bank[n % 8][0:ROPE, :].rearrange("p (h q) -> p h q", h=4)).then_inc(hd_dve, 1)
                else:
                    V.tensor_scalar(dst, bank[n % 8][:, :].rearrange("p (h q) -> p h q", h=4), g, None, ALU.mult).then_inc(hd_dve, 1)
            scale = float(QK) ** -0.5

            def masked(n):
                dve.wait_ge(sc_done, n + 1)
                if n < 2:
                    dst, w, mk = sc0[:, 4 * n:4 * n + 4, :], 4, mask[:, S - P:S]
                else:
                    dst, w, mk = sc1[:, 2 * (n - 2):2 * (n - 2) + 2, :], 2, mask[:, 0:S]
                return V.scalar_tensor_tensor(out=dst, in0=bank[n][:, :].rearrange("p (h k) -> p h k", h=w), scalar=scale,
                                              in1=mk.unsqueeze(1).to_broadcast([P, w, HALF // w]), op0=ALU.mult, op1=ALU.add)

            def minus_max(t):
                link(V.tensor_reduce(smax[:, t, :], sc0 if t == 0 else sc1, AX_X, ALU.max))
                V.tensor_scalar(smax[:, t, :], smax[:, t, :], -1.0, None, ALU.mult).then_inc(smax_ready, 1)

            def probs(t):
                dve.wait_ge(exp_done, (t + 1) * H)
                link(V.reciprocal(sinv[:, t, :], ssum[:, t, :]))
                sc = sc0 if t == 0 else sc1
                V.tensor_tensor(sc, sc, over(sinv[:, t, :], (t + 1) * P), ALU.mult).then_inc(p_ready, 1)

            def probs_across(n):
                dve.wait_ge(ptr_done, n + 1)
                V.tensor_copy(prob_block(n), bank[prob_bank(n)][:, :].rearrange("p (a q) -> p a q", a=4)).then_inc(pT_dve, 1)

            def heads_out(t):
                dve.wait_ge(o_done, 2 * t + 1)
                V.tensor_copy(oT[:, 0:4, t * P:(t + 1) * P], bank[0][:, :].rearrange("p (h q) -> p h q", h=4)).then_inc(o_dve, 1)

            def add_attention(t):
                for hf in range(2):
                    dve.wait_ge(wo_done, 2 * t + hf + 1)
                    V.tensor_tensor(h[:, t, hf * HALF:(hf + 1) * HALF], bank[wo_bank(2 * t + hf)][:, :],
                                    h[:, t, hf * HALF:(hf + 1) * HALF], ALU.add).then_inc(h_ready[3], 1)

            masked(0)
            link(masked(1))
            minus_max(0)
            for n in range(2, 5):
                masked(n)
            link(masked(5))
            probs(0)
            minus_max(1)
            probs_across(0)
            heads_out(0)
            probs(1)
            add_attention(0)
            probs_across(2)
            probs_across(4)
            heads_out(1)
            add_attention(1)

            experts(1)


_INS = ["x", "positions", "a_norm_g", "a_pw1_w", "a_pw1_b", "a_dw_w", "a_dw_b", "a_ln_g", "a_ln_b", "a_pw2_w", "a_pw2_b",
        "kv_norm_g", "w_dkv", "kv_latent_g", "w_kr", "w_ukv", "k_norm_g", "b_norm_g", "w_dq", "q_latent_g", "w_uq",
        "q_norm_g", "w_o", "ffn_norm_g", "w_group", "b_group", "w_router", "b_router", "w_gate_up", "w_down"]


def kernel(**inputs):
    import numpy as _np
    import concourse.bacc as _bacc
    from concourse import mybir as _mybir
    from concourse.bass_utils import run_bass_kernel_spmd as _run

    nc = _bacc.Bacc("TRN2", target_bir_lowering=False, num_devices=1)
    arrays, args = {}, {}

    def declare(name, a):
        arrays[f"in_{name}_dram"] = a
        args[name] = nc.dram_tensor(f"in_{name}_dram", a.shape, _mybir.dt.from_np(a.dtype), kind="ExternalInput").ap()

    for name in _INS:
        declare(name, _np.ascontiguousarray(inputs[name]))
    rope = args["w_kr"].shape[1]
    inv = _np.float32(ROPE_THETA) ** (-_np.arange(0, rope, 2, dtype=_np.float32) / _np.float32(rope))
    declare("inv_freq", inv.astype(_np.float32).reshape(1, rope // 2))
    shape = inputs["x"].shape
    out = nc.dram_tensor("out_0_dram", shape, F32, kind="ExternalOutput").ap()
    trunk_kernel(nc, args, out)
    r = _run(nc, [arrays], core_ids=[0])
    return r.results[0]["out_0_dram"]
```
